# Optimizing a Trainium2 kernel written in Bass

```python
import jax, jax.numpy as jnp
from jax import lax
import numpy as np

D_MODEL = 1024
BATCH = 1
SEQ = 512
DEPTH = 2

POOL_GROUPS = 4
POOL_GROUP_DIM = 64
POOL_WINDOWS = (2, 4, 8, 16)
D_POOL = POOL_GROUPS * POOL_GROUP_DIM
D_CONV = 256
CONV_WIDTH = 31
N_HEADS = 8
N_KV_HEADS = 2
HEAD_DIM = 64
D_ATTN = N_HEADS * HEAD_DIM
D_KV = N_KV_HEADS * HEAD_DIM
IDX_HEADS = 8
IDX_DIM = 64
TOPK_MAX = 256
Q_BLOCK = 128
ROPE_THETA = 10000.0
N_BRANCH = 3
IN_SIZES = (D_POOL, 2 * D_CONV, D_ATTN, D_KV, D_KV, IDX_HEADS * IDX_DIM, IDX_DIM, IDX_HEADS, N_BRANCH * D_MODEL)
D_IN = sum(IN_SIZES)
D_FF = 2816
FFN_CONV_WIDTH = 3
LN_EPS = 1e-5
DEEPNORM_ALPHA = (2 * DEPTH) ** 0.25
DEEPNORM_BETA = (8 * DEPTH) ** -0.25


def layer_norm(x, g, b):
    xf = x.astype(jnp.float32)
    mu = jnp.mean(xf, axis=-1, keepdims=True)
    var = jnp.mean(jnp.square(xf - mu), axis=-1, keepdims=True)
    y = (xf - mu) * lax.rsqrt(var + LN_EPS) * g.astype(jnp.float32) + b.astype(jnp.float32)
    return y.astype(x.dtype)

def rope(x, positions):
    half = x.shape[-1] // 2
    inv_freq = ROPE_THETA ** (-jnp.arange(half, dtype=jnp.float32) / half)
    ang = positions.astype(jnp.float32)[..., None] * inv_freq
    cos = jnp.cos(ang)[:, :, None, :]
    sin = jnp.sin(ang)[:, :, None, :]
    xf = x.astype(jnp.float32)
    x1, x2 = xf[..., :half], xf[..., half:]
    return jnp.concatenate([x1 * cos - x2 * sin, x2 * cos + x1 * sin], axis=-1).astype(x.dtype)

def causal_dwconv(x, w, b):
    k, c = w.shape
    y = lax.conv_general_dilated(
        x, w[:, None, :].astype(x.dtype), window_strides=(1,), padding=[(k - 1, 0)],
        dimension_numbers=('NWC', 'WIO', 'NWC'), feature_group_count=c)
    return y + b

def split_cols(z, sizes):
    out, off = [], 0
    for s in sizes:
        out.append(z[..., off:off + s])
        off += s
    return out

def pool_mixer(u, pool_w, pool_scale):
    B, L, _ = u.shape
    uf = u.astype(jnp.float32).reshape(B, L, POOL_GROUPS, POOL_GROUP_DIM)
    cs0 = jnp.pad(jnp.cumsum(uf, axis=1), ((0, 0), (1, 0), (0, 0), (0, 0)))
    t = jnp.arange(L)
    pooled = []
    for g, win in enumerate(POOL_WINDOWS):
        start = jnp.maximum(t + 1 - win, 0)
        s = cs0[:, 1:, g] - cs0[:, start, g]
        cnt = (t + 1 - start).astype(jnp.float32)[None, :, None]
        pooled.append(s / cnt)
    mixed = jnp.stack(pooled, axis=2) - uf
    y = jnp.einsum('blgc,gcd->blgd', mixed, pool_w.astype(jnp.float32))
    return (y.reshape(B, L, D_POOL) * pool_scale.astype(jnp.float32)).astype(u.dtype)

def conformer_conv(u, dw_w, dw_b, ln_g, ln_b, w_pw):
    a, gate = jnp.split(u, 2, axis=-1)
    h = a * jax.nn.sigmoid(gate)
    h = causal_dwconv(h, dw_w, dw_b)
    h = jax.nn.silu(layer_norm(h, ln_g, ln_b))
    return h @ w_pw

def dsa_attention(q, k, v, q_idx, k_idx, w_idx):
    B, L = q.shape[0], q.shape[1]
    topk = min(TOPK_MAX, L // 4)
    n_blk = L // Q_BLOCK
    group = N_HEADS // N_KV_HEADS
    key_pos = jnp.arange(L)
    k_idx_f = k_idx.astype(jnp.float32)

    def block(i):
        q0 = i * Q_BLOCK
        qpos = q0 + jnp.arange(Q_BLOCK)
        qb = lax.dynamic_slice_in_dim(q, q0, Q_BLOCK, axis=1)
        qib = lax.dynamic_slice_in_dim(q_idx, q0, Q_BLOCK, axis=1).astype(jnp.float32)
        wib = lax.dynamic_slice_in_dim(w_idx, q0, Q_BLOCK, axis=1).astype(jnp.float32)
        logits = jnp.einsum('bqhd,bsd->bqsh', qib, k_idx_f)
        score = jnp.einsum('bqsh,bqh->bqs', jax.nn.relu(logits), wib)
        causal = key_pos[None, :] <= qpos[:, None]
        score = jnp.where(causal[None], score, -jnp.inf)
        _, idx = lax.top_k(score, topk)
        valid = idx <= qpos[None, :, None]
        k_sel = jax.vmap(lambda kk, ii: kk[ii])(k, idx)
        v_sel = jax.vmap(lambda vv, ii: vv[ii])(v, idx)
        qg = qb.reshape(B, Q_BLOCK, N_KV_HEADS, group, HEAD_DIM).astype(jnp.float32)
        s = jnp.einsum('bqngd,bqknd->bngqk', qg, k_sel.astype(jnp.float32)) * (HEAD_DIM ** -0.5)
        s = jnp.where(valid[:, None, None], s, -jnp.inf)
        p = jax.nn.softmax(s, axis=-1)
        o = jnp.einsum('bngqk,bqknd->bqngd', p, v_sel.astype(jnp.float32))
        return o.reshape(B, Q_BLOCK, D_ATTN).astype(q.dtype)

    out = lax.map(block, jnp.arange(n_blk))
    return out.transpose(1, 0, 2, 3).reshape(B, L, D_ATTN)

def token_mix(h, positions, w_in, b_in, pool_w, pool_scale, w_pool_out, conv_dw_w, conv_dw_b,
              conv_ln_g, conv_ln_b, w_conv_out, w_attn_out, w_o):
    B, L, _ = h.shape
    z = h @ w_in + b_in
    u_pool, u_conv, q, k, v, qi, ki, wi, gates = split_cols(z, IN_SIZES)
    q = rope(q.reshape(B, L, N_HEADS, HEAD_DIM), positions)
    k = rope(k.reshape(B, L, N_KV_HEADS, HEAD_DIM), positions)
    v = v.reshape(B, L, N_KV_HEADS, HEAD_DIM)
    qi = rope(qi.reshape(B, L, IDX_HEADS, IDX_DIM), positions) * (IDX_DIM ** -0.5)
    ki = rope(ki[:, :, None, :], positions)[:, :, 0, :]
    wi = wi * (IDX_HEADS ** -0.5)
    y_pool = pool_mixer(u_pool, pool_w, pool_scale) @ w_pool_out
    y_conv = conformer_conv(u_conv, conv_dw_w, conv_dw_b, conv_ln_g, conv_ln_b, w_conv_out)
    y_attn = dsa_attention(q, k, v, qi, ki, wi) @ w_attn_out
    g = jax.nn.sigmoid(gates.astype(jnp.float32)).reshape(B, L, N_BRANCH, D_MODEL).astype(h.dtype)
    merged = g[:, :, 0] * y_pool + g[:, :, 1] * y_conv + g[:, :, 2] * y_attn
    return merged @ w_o

def conv_ffn(h, w_up, ffn_dw_w, ffn_dw_b, w_down):
    u = causal_dwconv(h @ w_up, ffn_dw_w, ffn_dw_b)
    gate, val = jnp.split(u, 2, axis=-1)
    return (jax.nn.silu(gate) * val) @ w_down

def first_inputs(seed: int = 0) -> dict:
    key = jax.random.key(seed)
    ks = jax.random.split(key, 24)
    f32 = jnp.float32

    def nrm(k, shape, scale):
        return jax.random.normal(k, shape, f32) * scale

    return {
        "x": nrm(ks[0], (BATCH, SEQ, D_MODEL), 1.0),
        "positions": jnp.broadcast_to(jnp.arange(SEQ, dtype=jnp.int32), (BATCH, SEQ)),
        "ln_in_g": 1.0 + nrm(ks[1], (D_MODEL,), 0.02),
        "ln_in_b": nrm(ks[2], (D_MODEL,), 0.02),
        "w_in": nrm(ks[3], (DEPTH, D_MODEL, D_IN), D_MODEL ** -0.5),
        "b_in": nrm(ks[4], (DEPTH, D_IN), 0.02),
        "pool_w": nrm(ks[5], (DEPTH, POOL_GROUPS, POOL_GROUP_DIM, POOL_GROUP_DIM), POOL_GROUP_DIM ** -0.5),
        "pool_scale": 1.0 + nrm(ks[6], (DEPTH, D_POOL), 0.1),
        "w_pool_out": nrm(ks[7], (DEPTH, D_POOL, D_MODEL), D_POOL ** -0.5),
        "conv_dw_w": nrm(ks[8], (DEPTH, CONV_WIDTH, D_CONV), CONV_WIDTH ** -0.5),
        "conv_dw_b": nrm(ks[9], (DEPTH, D_CONV), 0.02),
        "conv_ln_g": 1.0 + nrm(ks[10], (DEPTH, D_CONV), 0.02),
        "conv_ln_b": nrm(ks[11], (DEPTH, D_CONV), 0.02),
        "w_conv_out": nrm(ks[12], (DEPTH, D_CONV, D_MODEL), D_CONV ** -0.5),
        "w_attn_out": nrm(ks[13], (DEPTH, D_ATTN, D_MODEL), D_ATTN ** -0.5),
        "w_o": nrm(ks[14], (DEPTH, D_MODEL, D_MODEL), DEEPNORM_BETA * D_MODEL ** -0.5),
        "ln1_g": 1.0 + nrm(ks[15], (DEPTH, D_MODEL), 0.02),
        "ln1_b": nrm(ks[16], (DEPTH, D_MODEL), 0.02),
        "w_up": nrm(ks[17], (DEPTH, D_MODEL, 2 * D_FF), D_MODEL ** -0.5),
        "ffn_dw_w": nrm(ks[18], (DEPTH, FFN_CONV_WIDTH, 2 * D_FF), FFN_CONV_WIDTH ** -0.5),
        "ffn_dw_b": nrm(ks[19], (DEPTH, 2 * D_FF), 0.02),
        "w_down": nrm(ks[20], (DEPTH, D_FF, D_MODEL), DEEPNORM_BETA * D_FF ** -0.5),
        "ln2_g": 1.0 + nrm(ks[21], (DEPTH, D_MODEL), 0.02),
        "ln2_b": nrm(ks[22], (DEPTH, D_MODEL), 0.02),
    }

def first_block(x, positions, ln_in_g, ln_in_b, w_in, b_in, pool_w, pool_scale, w_pool_out,
              conv_dw_w, conv_dw_b, conv_ln_g, conv_ln_b, w_conv_out, w_attn_out, w_o,
              ln1_g, ln1_b, w_up, ffn_dw_w, ffn_dw_b, w_down, ln2_g, ln2_b):
    h = layer_norm(x, ln_in_g, ln_in_b)
    for l in range(DEPTH):
        mix = token_mix(h, positions, w_in[l], b_in[l], pool_w[l], pool_scale[l], w_pool_out[l],
                        conv_dw_w[l], conv_dw_b[l], conv_ln_g[l], conv_ln_b[l], w_conv_out[l],
                        w_attn_out[l], w_o[l])
        h = layer_norm(DEEPNORM_ALPHA * h + mix, ln1_g[l], ln1_b[l])
        ffn = conv_ffn(h, w_up[l], ffn_dw_w[l], ffn_dw_b[l], w_down[l])
        h = layer_norm(DEEPNORM_ALPHA * h + ffn, ln2_g[l], ln2_b[l])
    return h


GRID_W = 64
CTX_LEN = 256
N_EVEN = (DEPTH + 1) // 2
N_ODD = DEPTH // 2
EPS = 1e-6

RWKV_HEAD = 64
RWKV_HEADS = (3 * D_MODEL // 4) // RWKV_HEAD
RWKV_W = RWKV_HEADS * RWKV_HEAD
LORA_W = 64
LORA_A = 64
FOUR_GROUPS = 4
FOUR_W = D_MODEL - RWKV_W
FOUR_GROUP_W = FOUR_W // FOUR_GROUPS
MIX_W = RWKV_W + FOUR_W
N_SHIFT = 3 * RWKV_W + 2 * LORA_W + 2 * LORA_A
EVEN_IN = N_SHIFT + RWKV_W + 2 * FOUR_W
RWKV_GN_EPS = 64e-5

RET_HEADS = 8
RET_HEAD = D_MODEL // RET_HEADS
RET_W = RET_HEADS * RET_HEAD
ODD_IN = 4 * RET_W
RET_CHUNK = 128
ROPE_BASE = 10000.0


def rmsnorm(x, g):
    xf = x.astype(jnp.float32)
    y = xf * lax.rsqrt(jnp.mean(xf * xf, axis=-1, keepdims=True) + EPS)
    return (y * g.astype(jnp.float32)).astype(x.dtype)

def qshift(u, rows):
    b, l, ch = u.shape
    g = u.reshape(b, rows, GRID_W, ch // 4, 4)
    left = jnp.pad(g[:, :, :-1, :, 0], ((0, 0), (0, 0), (1, 0), (0, 0)))
    right = jnp.pad(g[:, :, 1:, :, 1], ((0, 0), (0, 0), (0, 1), (0, 0)))
    up = jnp.pad(g[:, :-1, :, :, 2], ((0, 0), (1, 0), (0, 0), (0, 0)))
    down = jnp.pad(g[:, 1:, :, :, 3], ((0, 0), (0, 1), (0, 0), (0, 0)))
    return jnp.stack([left, right, up, down], axis=-1).reshape(b, l, ch)

def bishift(u):
    b, l, ch = u.shape
    g = u.reshape(b, l, ch // 2, 2)
    prev = jnp.pad(g[:, :-1, :, 0], ((0, 0), (1, 0), (0, 0)))
    nxt = jnp.pad(g[:, 1:, :, 1], ((0, 0), (0, 1), (0, 0)))
    return jnp.stack([prev, nxt], axis=-1).reshape(b, l, ch)

def rwkv_dir_terms(r, k0, v, wl, al, w0, w2, a0, a2, k_k, k_a, r_k):
    b, l, _ = r.shape
    hs = lambda t: t.reshape(b, l, RWKV_HEADS, RWKV_HEAD)
    w_log = -jax.nn.softplus(-(w0 + jnp.tanh(wl) @ w2)) - 0.5
    decay = jnp.exp(-jnp.exp(w_log))
    a = jax.nn.sigmoid(a0 + al @ a2)
    kk = hs(k0 * k_k)
    kk = kk / jnp.maximum(jnp.sqrt(jnp.sum(kk * kk, axis=-1, keepdims=True)), 1e-12)
    k = hs(k0 * (1.0 + (a - 1.0) * k_a))
    rh, vh = hs(r), hs(v)
    bonus = jnp.sum(rh * k * r_k, axis=-1, keepdims=True) * vh
    return rh, hs(decay), k, vh, kk, kk * hs(a), bonus

def rwkv7_scan(r, w, k, v, kk, bb, s0, reverse):
    def step(s, inp):
        r_t, w_t, k_t, v_t, kk_t, b_t = inp
        sa = jnp.einsum('bhij,bhj->bhi', s, kk_t)
        s = s * w_t[:, :, None, :] - sa[..., None] * b_t[:, :, None, :] + v_t[..., None] * k_t[:, :, None, :]
        return s, jnp.einsum('bhij,bhj->bhi', s, r_t)
    xs = tuple(jnp.moveaxis(t, 1, 0) for t in (r, w, k, v, kk, bb))
    s, ys = lax.scan(step, s0, xs, reverse=reverse)
    return s, jnp.moveaxis(ys, 0, 1)

def fourier_mix(u):
    b, l, _ = u.shape
    g = u.astype(jnp.float32).reshape(b, l, FOUR_GROUPS, FOUR_GROUP_W)
    f = jnp.fft.fft2(g, axes=(1, 3), norm='ortho').real
    return f.reshape(b, l, FOUR_W).astype(u.dtype)

def even_mixer(hc, hl, rows, w_in, mu, w0, w2, a0, a2, k_k, k_a, r_k, lnx_g, lnx_b, w_out, need_ctx):
    cuts = np.cumsum([RWKV_W, RWKV_W, RWKV_W, LORA_W, LORA_W, LORA_A]).tolist()

    def proj(h, shift_fn):
        u = h @ w_in
        s, gate_r, four, gate_f = jnp.split(u, [N_SHIFT, N_SHIFT + RWKV_W, N_SHIFT + RWKV_W + FOUR_W], axis=-1)
        s = (s + (shift_fn(s) - s) * mu).astype(jnp.float32)
        r, k0, v, wl_f, wl_b, al_f, al_b = jnp.split(s, cuts, axis=-1)
        return r, k0, v, (wl_f, wl_b), (al_f, al_b), gate_r, four, gate_f

    pc = proj(hc, bishift)
    pl = proj(hl, lambda t: qshift(t, rows))
    bsz = hl.shape[0]
    zeros = jnp.zeros((bsz, RWKV_HEADS, RWKV_HEAD, RWKV_HEAD), jnp.float32)
    oc, ol = 0.0, 0.0
    for d in range(2):
        tc = rwkv_dir_terms(pc[0], pc[1], pc[2], pc[3][d], pc[4][d], w0[d], w2[d], a0[d], a2[d], k_k, k_a, r_k)
        tl = rwkv_dir_terms(pl[0], pl[1], pl[2], pl[3][d], pl[4][d], w0[d], w2[d], a0[d], a2[d], k_k, k_a, r_k)
        s_ctx, yc = rwkv7_scan(*tc[:6], zeros, d == 1)
        _, yl = rwkv7_scan(*tl[:6], s_ctx, d == 1)
        oc = oc + yc + tc[6]
        ol = ol + yl + tl[6]

    def finish(o, gate_r, four, gate_f):
        b, l = o.shape[:2]
        mean = jnp.mean(o, axis=-1, keepdims=True)
        var = jnp.mean(jnp.square(o - mean), axis=-1, keepdims=True)
        o = ((o - mean) * lax.rsqrt(var + RWKV_GN_EPS)).reshape(b, l, RWKV_W) * lnx_g + lnx_b
        yr = o.astype(gate_r.dtype) * jax.nn.silu(gate_r)
        yf = fourier_mix(four) * jax.nn.silu(gate_f)
        return jnp.concatenate([yr, yf], axis=-1) @ w_out

    out_l = finish(ol, pl[5], pl[6], pl[7])
    out_c = finish(oc, pc[5], pc[6], pc[7]) if need_ctx else None
    return out_c, out_l

def axial_rope(t):
    l = t.shape[1]
    pos = jnp.arange(l)
    rc = jnp.stack([pos // GRID_W, pos % GRID_W], axis=-1).astype(jnp.float32)
    half = RET_HEAD // 2
    inv = ROPE_BASE ** (-jnp.arange(0, half, 2, dtype=jnp.float32) / half)
    ang = (rc[:, :, None] * inv).reshape(l, half)[:, None, :]
    cos, sin = jnp.cos(ang), jnp.sin(ang)
    t1, t2 = t[..., :half], t[..., half:]
    return jnp.concatenate([t1 * cos - t2 * sin, t1 * sin + t2 * cos], axis=-1)

def retention_scan(q, k, v, log_gamma, r0, strict):
    bsz, l, h, dk = q.shape
    dv = v.shape[-1]
    n_chunks = l // RET_CHUNK
    pos = jnp.arange(RET_CHUNK, dtype=jnp.float32)
    diff = pos[:, None] - pos[None, :]
    mask = diff > 0 if strict else diff >= 0
    dmat = jnp.where(mask[None], jnp.exp(jnp.where(mask, diff, 0.0)[None] * log_gamma[:, None, None]), 0.0)
    xi = jnp.exp((pos[:, None] + 1.0) * log_gamma[None, :])
    zeta = jnp.exp((RET_CHUNK - 1.0 - pos[:, None]) * log_gamma[None, :])
    g_chunk = jnp.exp(RET_CHUNK * log_gamma)

    def chunk(r, inp):
        qc, kc, vc = inp
        sc = jnp.einsum('bihd,bjhd->bhij', qc, kc) * dmat
        inner = jnp.einsum('bhij,bjhe->bihe', sc, vc)
        cross = jnp.einsum('bihd,bhde->bihe', qc, r) * xi[None, :, :, None]
        r = r * g_chunk[None, :, None, None] + jnp.einsum('bjhd,bjhe->bhde', kc * zeta[None, :, :, None], vc)
        return r, inner + cross

    to_chunks = lambda t: jnp.moveaxis(t.reshape(bsz, n_chunks, RET_CHUNK, h, t.shape[-1]), 1, 0)
    r, o = lax.scan(chunk, r0, (to_chunks(q), to_chunks(k), to_chunks(v)))
    return r, jnp.moveaxis(o, 0, 1).reshape(bsz, l, h, dv)

def odd_mixer(hc, hl, w_in, decay_logit, w_out, need_ctx):
    bsz = hl.shape[0]

    def proj(h, rope):
        u = h @ w_in
        q, k, v, g = jnp.split(u, 4, axis=-1)
        l = h.shape[1]
        hs = lambda t: t.astype(jnp.float32).reshape(bsz, l, RET_HEADS, RET_HEAD)
        q, k, v = hs(q), hs(k) * (RET_HEAD ** -0.5), hs(v)
        if rope:
            q, k = axial_rope(q), axial_rope(k)
        return q, k, v, g

    qc, kc, vc, gc = proj(hc, False)
    ql, kl, vl, gl = proj(hl, True)
    lg = jax.nn.log_sigmoid(decay_logit.astype(jnp.float32))
    zeros = jnp.zeros((bsz, RET_HEADS, RET_HEAD, RET_HEAD), jnp.float32)
    flip = lambda t: jnp.flip(t, axis=1)
    rc_f, oc_f = retention_scan(qc, kc, vc, lg[0], zeros, False)
    _, ol_f = retention_scan(ql, kl, vl, lg[0], rc_f, False)
    rc_b, oc_b = retention_scan(flip(qc), flip(kc), flip(vc), lg[1], zeros, True)
    _, ol_b = retention_scan(flip(ql), flip(kl), flip(vl), lg[1], rc_b, True)

    def finish(of, ob, g):
        o = of + flip(ob)
        o = o * lax.rsqrt(jnp.mean(o * o, axis=-1, keepdims=True) + EPS)
        o = o.reshape(o.shape[0], o.shape[1], RET_W).astype(g.dtype)
        return (o * jax.nn.silu(g)) @ w_out

    out_l = finish(ol_f, ol_b, gl)
    out_c = finish(oc_f, oc_b, gc) if need_ctx else None
    return out_c, out_l

def second_inputs(seed: int = 0) -> dict:
    key = jax.random.key(seed)
    ks = jax.random.split(key, 24)
    f32 = jnp.float32
    nrm = lambda k, shape, s: jax.random.normal(k, shape, f32) * s
    D = D_MODEL
    gam = 1.0 - 2.0 ** (-5.0 - jnp.arange(RET_HEADS, dtype=f32))
    return {
        'x': nrm(ks[0], (BATCH, SEQ, D), 1.0),
        'c': nrm(ks[1], (BATCH, D), 1.0),
        'ctx': nrm(ks[2], (BATCH, CTX_LEN, D), 1.0),
        'c_ctx': nrm(ks[3], (D,), 1.0),
        'ada_w': nrm(ks[4], (DEPTH, D, 3 * D), D ** -0.5),
        'ada_b': nrm(ks[5], (DEPTH, 3 * D), 0.02),
        'norm_pre': 1.0 + nrm(ks[6], (DEPTH, D), 0.05),
        'norm_post': 1.0 + nrm(ks[7], (DEPTH, D), 0.05),
        'ev_w_in': nrm(ks[8], (N_EVEN, D, EVEN_IN), D ** -0.5),
        'ev_mu': jax.random.uniform(ks[9], (N_EVEN, N_SHIFT), f32),
        'ev_w0': jax.random.uniform(ks[10], (N_EVEN, 2, RWKV_W), f32, -4.0, 0.5),
        'ev_w2': nrm(ks[11], (N_EVEN, 2, LORA_W, RWKV_W), 0.1 * LORA_W ** -0.5),
        'ev_a0': nrm(ks[12], (N_EVEN, 2, RWKV_W), 0.5),
        'ev_a2': nrm(ks[13], (N_EVEN, 2, LORA_A, RWKV_W), 0.1 * LORA_A ** -0.5),
        'ev_k_k': 0.85 + nrm(ks[14], (N_EVEN, RWKV_W), 0.05),
        'ev_k_a': 1.0 + nrm(ks[15], (N_EVEN, RWKV_W), 0.05),
        'ev_r_k': nrm(ks[16], (N_EVEN, RWKV_HEADS, RWKV_HEAD), 0.1),
        'ev_lnx_g': 1.0 + nrm(ks[17], (N_EVEN, RWKV_W), 0.05),
        'ev_lnx_b': nrm(ks[18], (N_EVEN, RWKV_W), 0.02),
        'ev_w_out': nrm(ks[19], (N_EVEN, MIX_W, D), MIX_W ** -0.5),
        'od_w_in': nrm(ks[20], (N_ODD, D, ODD_IN), D ** -0.5),
        'od_decay_logit': (jnp.log(gam) - jnp.log1p(-gam)) + nrm(ks[21], (N_ODD, 2, RET_HEADS), 0.1),
        'od_w_out': nrm(ks[22], (N_ODD, RET_W, D), RET_W ** -0.5),
    }

def second_block(x, c, ctx, c_ctx, ada_w, ada_b, norm_pre, norm_post, ev_w_in, ev_mu, ev_w0, ev_w2, ev_a0, ev_a2,
              ev_k_k, ev_k_a, ev_r_k, ev_lnx_g, ev_lnx_b, ev_w_out, od_w_in, od_decay_logit, od_w_out):
    rows = x.shape[1] // GRID_W
    xl, xc = x, ctx
    sc, scc = jax.nn.silu(c), jax.nn.silu(c_ctx)
    for layer in range(DEPTH):
        need_ctx = layer < DEPTH - 1
        shift_l, scale_l, gate_l = jnp.split(sc @ ada_w[layer] + ada_b[layer], 3, axis=-1)
        shift_c, scale_c, gate_c = jnp.split(scc @ ada_w[layer] + ada_b[layer], 3, axis=-1)
        hl = rmsnorm(xl, norm_pre[layer]) * (1.0 + scale_l[:, None, :]) + shift_l[:, None, :]
        hc = rmsnorm(xc, norm_pre[layer]) * (1.0 + scale_c) + shift_c
        if layer % 2 == 0:
            i = layer // 2
            oc, ol = even_mixer(hc, hl, rows, ev_w_in[i], ev_mu[i], ev_w0[i], ev_w2[i], ev_a0[i], ev_a2[i],
                                ev_k_k[i], ev_k_a[i], ev_r_k[i], ev_lnx_g[i], ev_lnx_b[i], ev_w_out[i], need_ctx)
        else:
            i = layer // 2
            oc, ol = odd_mixer(hc, hl, od_w_in[i], od_decay_logit[i], od_w_out[i], need_ctx)
        xl = xl + gate_l[:, None, :] * rmsnorm(ol, norm_post[layer])
        if need_ctx:
            xc = xc + gate_c * rmsnorm(oc, norm_post[layer])
    return xl


def setup_inputs(seed=0):
    out = dict(first_inputs(seed))
    for name, value in second_inputs(seed + 1).items():
        if name != "x":
            out[name + "_2"] = value
    return out


def reference(
    x, positions, ln_in_g, ln_in_b, w_in, b_in, pool_w, pool_scale, w_pool_out, conv_dw_w,
    conv_dw_b, conv_ln_g, conv_ln_b, w_conv_out, w_attn_out, w_o, ln1_g, ln1_b, w_up, ffn_dw_w,
    ffn_dw_b, w_down, ln2_g, ln2_b, c_2, ctx_2, c_ctx_2, ada_w_2, ada_b_2, norm_pre_2,
    norm_post_2, ev_w_in_2, ev_mu_2, ev_w0_2, ev_w2_2, ev_a0_2, ev_a2_2, ev_k_k_2, ev_k_a_2,
    ev_r_k_2, ev_lnx_g_2, ev_lnx_b_2, ev_w_out_2, od_w_in_2, od_decay_logit_2, od_w_out_2,
):
    x = first_block(
        x, positions, ln_in_g, ln_in_b, w_in, b_in, pool_w, pool_scale, w_pool_out, conv_dw_w,
        conv_dw_b, conv_ln_g, conv_ln_b, w_conv_out, w_attn_out, w_o, ln1_g, ln1_b, w_up,
        ffn_dw_w, ffn_dw_b, w_down, ln2_g, ln2_b,
    )
    return second_block(
        x, c_2, ctx_2, c_ctx_2, ada_w_2, ada_b_2, norm_pre_2, norm_post_2, ev_w_in_2, ev_mu_2,
        ev_w0_2, ev_w2_2, ev_a0_2, ev_a2_2, ev_k_k_2, ev_k_a_2, ev_r_k_2, ev_lnx_g_2,
        ev_lnx_b_2, ev_w_out_2, od_w_in_2, od_decay_logit_2, od_w_out_2,
    )


_drawn_inputs = setup_inputs


def setup_inputs(seed=0):
    import zlib

    import numpy as np

    out = dict(_drawn_inputs(seed))
    spreads = {}
    factors = {'b_in': 4.073,
     'conv_dw_b': 5.036,
     'conv_ln_g': 8.0,
     'conv_ln_b': 8.0,
     'ffn_dw_b': 4.527,
     'ev_w2_2': 5.599,
     'ev_lnx_b_2': 4.477}
    for name, (base, spread) in spreads.items():
        noise = np.random.default_rng([zlib.crc32(name.encode()), seed]).standard_normal(out[name].shape)
        drawn = base * np.exp(spread * noise) if base else spread * noise
        out[name] = __import__('jax').numpy.asarray(drawn.astype(out[name].dtype))
    for name, factor in factors.items():
        out[name] = (out[name] * factor).astype(out[name].dtype)
    return out
```

```python
import math
from contextlib import ExitStack, contextmanager

import numpy as np

import concourse.bass as bass
from concourse import mybir

F32 = mybir.dt.float32
I32 = mybir.dt.int32
ALU = mybir.AluOpType
ACT = mybir.ActivationFunctionType
AX_X = mybir.AxisListType.X

P = 128
D = 1024
KD = D // P
L = 512
DEPTH = 2
POOL_WINDOWS = (2, 4, 8, 16)
POOL_TAIL = max(POOL_WINDOWS)
D_CONV = 256
TAPS = 31
HEADS, HEAD_DIM = 8, 64
TOPK = min(256, L // 4)
QB = L // P
D_FF = 2816
KF = D_FF // P
UF = 2 * KF
ALPHA = (2 * DEPTH) ** 0.25
CTX = 256
T2 = CTX + L
GRID_W = 64
RW_HEADS = 12
RW_PAIRS = RW_HEADS // 2
RWKV_W = RW_HEADS * 64
N_SHIFT = 3 * RWKV_W + 256
CH = 64
NCH = T2 // CH
RET_HEADS = 8
DECAY = math.exp(-0.5)

C_POOL, C_CONV, C_Q, C_K, C_V, C_QI, C_KI, C_WI, C_GATE = 0, 256, 768, 1280, 1408, 1536, 2048, 2112, 2120

PICKED = -3.0e38
FUTURE = -2.0e38
MASKED = -1.0e30
ROUND = 12582912.0
TWO_PI_1 = 6.28125
TWO_PI_2 = float(np.float32(np.round((2 * math.pi - TWO_PI_1) * 2**22) / 2**22))
TWO_PI_3 = 2 * math.pi - TWO_PI_1 - TWO_PI_2
PI_IN = 3.1415925


def const_table():
    eye = np.eye(P)
    p = np.arange(P)
    t = {}
    t["ident"] = eye
    t["mean_d"] = np.full((P, P), 1.0 / D)
    t["mean_conv"] = np.full((P, P), 1.0 / D_CONV)
    rot64 = np.zeros((P, P))
    for m in range(P):
        if m % 64 < 32:
            rot64[m + 32, m] = -1
        else:
            rot64[m - 32, m] = 1
    t["rot64"] = rot64
    rot128 = np.zeros((P, P))
    for m in range(P):
        if m < 64:
            rot128[m + 64, m] = -1
        else:
            rot128[m - 64, m] = 1
    t["rot128"] = rot128
    same = (p[:, None] // 64 == p[None, :] // 64).astype(float)
    t["head_sum"] = same
    t["head_mean"] = same / 64
    t["mean_head128"] = np.full((P, P), 1.0 / P)
    t["future"] = np.where(p[None, :] <= p[:, None], 0.0, FUTURE)
    t["masked"] = np.where(p[None, :] <= p[:, None], 0.0, MASKED)
    cut = np.zeros((P, 2, POOL_TAIL))
    for ch in range(2):
        for half in range(2):
            win = POOL_WINDOWS[2 * ch + half]
            cut[64 * half:64 * half + 64, ch, :] = 1.0 / np.minimum(np.arange(POOL_TAIL) + 1, win)
    t["pool_cut"] = cut.reshape(P, -1)
    t["inv_freq"] = (np.float32(10000.0) ** (-(p % 32).astype(np.float32) / np.float32(32)))[:, None]
    cls = np.zeros((P, 6))
    for j in range(4):
        cls[:, j] = p % 4 == j
    cls[:, 4], cls[:, 5] = p % 2 == 0, p % 2 == 1
    t["lane"] = cls
    s, q = p[:, None] % 64, p[None, :] % 64
    t["upper"] = same * (s < q)
    t["lower"] = same * (s > q)
    t["upper_eq"] = (s <= q).astype(float)[:, :64]
    t["lower_eq"] = (s >= q).astype(float)[:, :64]
    for b in (1, 2, 4, 8, 16, 32):
        off = same * (s // (2 * b) == q // (2 * b)) * (s // b != q // b)
        t[f"up{b}"] = off * (s < q)
        t[f"lo{b}"] = off * (s > q)
    k64 = np.arange(64)
    ang = 2 * np.pi * np.outer(k64, k64) / 64
    bd = lambda m: np.kron(np.eye(2), m)
    t["dft_ch"] = np.concatenate([bd(np.cos(ang)), bd(np.sin(ang))], 1) / 8.0
    rc = np.stack([np.arange(L) // GRID_W, np.arange(L) % GRID_W], -1).astype(np.float32)
    inv = (np.float32(10000.0) ** (-np.arange(0, 64, 2, dtype=np.float32) / np.float32(64)))
    axial = (rc[:, :, None] * inv).reshape(L, 64)
    axial = np.concatenate([axial, axial], 1).T
    t["axial_cos"], t["axial_sin"] = np.cos(axial), np.sin(axial)
    widths, at = {}, 0
    for name, a in t.items():
        widths[name] = (at, a.shape[1])
        at += a.shape[1]
    return np.concatenate([a for a in t.values()], 1).astype(np.float32), widths


def dft_tables():
    out = []
    for n in (CTX, L):
        a = 2 * np.pi * (np.outer(np.arange(n), np.arange(n)) % n) / n
        out.append(np.stack([np.cos(a), -np.sin(a)]).astype(np.float32) / np.float32(math.sqrt(n)))
    return out


def retention_tables():
    p = np.arange(P)[:, None]
    d = np.arange(7 * P)[None, :] - 3 * P - p
    fwd, bwd = np.maximum(d, 0), np.maximum(-d, 0)
    x = np.arange(5 * P)[None, :]
    cf = x + P - p
    cb = 2 * L + 0 * x - x + p - L + P
    return np.concatenate([fwd, bwd, cf, cb], 1).astype(np.float32)


CONSTS, CONST_AT = const_table()


@contextmanager
def stage(nc, names):
    with ExitStack() as ctx:
        sems = [ctx.enter_context(nc.semaphore(n)) for n in names.split()]
        with nc.Block() as block:
            yield block, sems
        with nc.Block() as cleared:
            @cleared.gpsimd
            def _(pool):
                for s in sems:
                    pool.sem_clear(s)


class Chain:

    def __init__(self, engine, sem):
        self.engine, self.sem, self.count = engine, sem, 0

    def then(self, instruction):
        self.count += 1
        instruction.then_inc(self.sem, 1)
        self.engine.wait_ge(self.sem, self.count)


def cols(ap, at, n=1):
    return ap[:, at:at + n]


def layer(ap, l):
    letters = " ".join("abcd"[:len(ap.shape) - 1])
    return ap[bass.ds(l, 1)].rearrange(f"o {letters} -> (o a) {letters[2:]}" if len(ap.shape) > 2
                                       else "o a -> (o a)")


def load_columns(nc, rows, columns, psum, ident, vectors):
    n_tiles = rows.shape[1]
    pieces = []
    for view, row, at in vectors:
        done = 0
        while done < view.shape[0]:
            r = (row + done) % P
            k = min(view.shape[0] - done, P - r)
            pieces.append((view[done:done + k, :], (row + done) // P, r, at))
            done += k
    transfers = len(pieces)
    with stage(nc, "rows_zeroed rows_landed transposed") as (block, sems):
        rows_zeroed, rows_landed, transposed = sems

        @block.vector
        def _(dve):
            nc.vector.memset(rows[:, :, :], 0.0).then_inc(rows_zeroed, 1)
            for i in range(n_tiles):
                dve.wait_ge(transposed, i + 1)
                nc.vector.tensor_copy(columns[:, i * P:(i + 1) * P], psum[:, i * 512:i * 512 + P])

        @block.sync
        def _(sp):
            sp.wait_ge(rows_zeroed, 1)
            for view, tile, r, at in pieces:
                k, width = view.shape
                sp.dma_start(rows[r:r + k, tile, at:at + width], view).then_inc(rows_landed, 16)

        @block.tensor
        def _(pe):
            pe.wait_ge(rows_landed, 16 * transfers)
            for i in range(n_tiles):
                nc.tensor.transpose(psum[:, i * 512:i * 512 + P], rows[:, i, :], ident)\
                    .then_inc(transposed, 1)


def layer_norm(nc, x, sq, stats, psum, mean_w, gain, bias, eps, silu=False):
    K, T = x.shape[1], x.shape[2]
    mean, var = psum[:, 0:T], psum[:, 512:512 + T]
    with stage(nc, "mean_ready centered squared var_ready var_safe std_ready rstd_ready scaled") as (block, sems):
        mean_ready, centered, squared, var_ready, var_safe, std_ready, rstd_ready, scaled = sems

        @block.tensor
        def _(pe):
            for c in range(K):
                last = nc.tensor.matmul(mean, mean_w, x[:, c, :], start=c == 0, stop=c == K - 1)
            last.then_inc(mean_ready, 1)
            for c in range(K):
                pe.wait_ge(squared, c + 1)
                last = nc.tensor.matmul(var, mean_w, sq[:, c, :], start=c == 0, stop=c == K - 1)
            last.then_inc(var_ready, 1)

        @block.vector
        def _(dve):
            dve.wait_ge(mean_ready, 1)
            for c in range(K):
                nc.vector.tensor_tensor(x[:, c, :], x[:, c, :], mean, ALU.subtract)\
                    .then_inc(centered, 1)
            dve.wait_ge(var_ready, 1)
            nc.vector.tensor_scalar(stats, var, eps, None, ALU.add).then_inc(var_safe, 1)
            dve.wait_ge(std_ready, 1)
            nc.vector.reciprocal(stats, stats).then_inc(rstd_ready, 1)
            dve.wait_ge(rstd_ready, 1)
            for c in range(K):
                nc.vector.tensor_tensor(x[:, c, :], x[:, c, :], stats, ALU.mult).then_inc(scaled, 1)

        @block.scalar
        def _(act):
            for c in range(K):
                act.wait_ge(centered, c + 1)
                nc.scalar.activation(sq[:, c, :], x[:, c, :], ACT.Square).then_inc(squared, 1)
            act.wait_ge(var_safe, 1)
            nc.scalar.activation(stats, stats, ACT.Sqrt).then_inc(std_ready, 1)
            for c in range(K):
                act.wait_ge(scaled, c + 1)
                nc.scalar.activation(x[:, c, :], x[:, c, :], ACT.Silu if silu else ACT.Identity,
                                     bias=bias[:, c:c + 1], scale=gain[:, c:c + 1])


class Products:

    def __init__(self, nc, sems, ring, loads, groups, psum, regions):
        self.nc, self.ring, self.loads, self.groups = nc, ring, loads, groups
        self.landed = sems[:ring.shape[1]]
        self.ready, self.by_act, self.by_dve = sems[ring.shape[1]:]
        self.psum, self.regions = psum, regions
        self.slots = ring.shape[1]
        self.count, self.lands = [0] * self.slots, []
        for i, parts in enumerate(loads):
            self.count[i % self.slots] += 16 * len(parts)
            self.lands.append(self.count[i % self.slots])
        self.last_of = {g[0]: n for n, g in enumerate(groups)}

    @staticmethod
    def names(slots):
        return " ".join(f"weights_landed{i}" for i in range(slots)) + " products_ready evacuated_act evacuated_dve"

    def region(self, g):
        at, width = self.regions[g % len(self.regions)]
        return self.psum[:, at:at + width]

    def evacuated(self, g, who):
        return sum(x[2] == who for x in self.groups[:g + 1])

    def load(self, sp):
        for i, parts in enumerate(self.loads):
            if i >= self.slots:
                sp.wait_ge(self.ready, self.last_of[i - self.slots] + 1)
            for at, shape, view in parts:
                k, n = shape
                dst = self.ring[:, i % self.slots, at:at + k * n].rearrange("p (k n) -> p k n", k=k)
                sp.dma_start(dst, view).then_inc(self.landed[i % self.slots], 16)

    def multiply(self, pe, g):
        tile, products, who = self.groups[g]
        if g == 0 or self.groups[g - 1][0] != tile:
            pe.wait_ge(self.landed[tile % self.slots], self.lands[tile])
        prior = g - len(self.regions)
        if prior >= 0:
            before = self.groups[prior][2]
            pe.wait_ge(self.by_act if before == "act" else self.by_dve, self.evacuated(prior, before))
        slot = self.ring[:, tile % self.slots, :]
        region = self.region(g)
        for make in products:
            last = make(slot, region)
        last.then_inc(self.ready, 1)


def stream(nc, ring, loads, groups, psum, regions, consume, more=""):
    names = Products.names(ring.shape[1]) + " " + more
    with stage(nc, names) as (block, sems):
        n_own = ring.shape[1] + 3
        s = Products(nc, sems[:n_own], ring, loads, groups, psum, regions)
        s.more = sems[n_own:]

        @block.sync
        def _(sp):
            s.load(sp)

        @block.tensor
        def _(pe):
            for g in range(len(groups)):
                s.multiply(pe, g)

        @block.vector
        def _(dve):
            consume(dve, s)


def ffn_up(nc, ring, loads, groups, psum, u, cv, hidden, col):
    names = Products.names(ring.shape[1]) + " step convolved activated multiplied"
    with stage(nc, names) as (block, sems):
        n_own = ring.shape[1] + 3
        s = Products(nc, sems[:n_own], ring, loads, groups, psum, [(512 * b, 512) for b in range(8)])
        step, convolved, activated, multiplied = sems[n_own:]

        @block.sync
        def _(sp):
            s.load(sp)

        @block.tensor
        def _(pe):
            for g in range(len(groups)):
                s.multiply(pe, g)

        @block.scalar
        def _(act):
            def silu(i):
                act.wait_ge(convolved, 2 * i + 1)
                nc.scalar.activation(cv[:, 2 * i % 4, :], cv[:, 2 * i % 4, :], ACT.Silu).then_inc(activated, 1)

            for g in range(len(groups)):
                act.wait_ge(s.ready, g + 1)
                if g >= 4:
                    act.wait_ge(convolved, g - 3)
                nc.scalar.activation(u[:, g % 4, 2:], s.region(g), ACT.Identity).then_inc(s.by_act, 1)
                if g % 2 == 1 and g >= 3:
                    silu(g // 2 - 1)
            silu(len(groups) // 2 - 1)

        @block.vector
        def _(dve):
            chain = Chain(dve, step)

            def product(i):
                dve.wait_ge(activated, i + 1)
                nc.vector.tensor_tensor(hidden[:, i, :], cv[:, 2 * i % 4, :], cv[:, (2 * i + 1) % 4, :], ALU.mult)\
                    .then_inc(multiplied, 1)

            for g in range(len(groups)):
                chunk = g // 2 + KF * (g % 2)
                x, y = u[:, g % 4, :], cv[:, g % 4, :]
                dve.wait_ge(s.by_act, g + 1)
                if g >= 4:
                    dve.wait_ge(multiplied, (g - 4) // 2 + 1)
                chain.then(nc.vector.tensor_scalar(y, x[:, 2:], col("ffn_w", 2 * UF + chunk), col("ffn_dw_b", chunk), ALU.mult, ALU.add))
                chain.then(nc.vector.scalar_tensor_tensor(y, x[:, 1:L + 1], col("ffn_w", UF + chunk), y, ALU.mult, ALU.add))
                nc.vector.scalar_tensor_tensor(y, x[:, 0:L], col("ffn_w", chunk), y, ALU.mult, ALU.add).then_inc(convolved, 1)
                if g % 2 == 1 and g >= 3:
                    dve.wait_ge(convolved, g - 1)
                    product(g // 2 - 1)
            dve.wait_ge(convolved, len(groups))
            product(len(groups) // 2 - 1)


def attention(nc, q, kd, qi, ki, v, wi, o, psum, common):
    ident = common["ident"]
    with ExitStack() as ctx:
        sb = lambda name, shape: ctx.enter_context(nc.sbuf_tensor(name, shape, F32))
        relu = sb("relu", [P, 2, L])
        score = sb("score", [P, L])
        top8 = sb("top8", [P, 8])
        left_out = sb("left_out", [P, L])
        prob = sb("prob", [P, HEADS, L])
        prob_t = sb("prob_t", [P, 2, QB, 4, P])
        stat = sb("stat", [P, 3, HEADS])
        names = ("logits_ready logits_taken weighted step scores_ready scores_taken max_ready "
                 "exp_ready normed turned turned_taken pv_ready o_taken")
        with stage(nc, names) as (block, sems):
            (logits_ready, logits_taken, weighted, step, scores_ready, scores_taken, max_ready,
             exp_ready, normed, turned, turned_taken, pv_ready, o_taken) = sems
            bank = lambda b, n=512: psum[:, b * 512:b * 512 + n]

            @block.tensor
            def _(pe):
                def logits(b, h, idx):
                    ps = slice(64 * (h % 2), 64 * (h % 2) + 64)
                    if idx >= 2:
                        pe.wait_ge(logits_taken, idx - 1)
                    nc.tensor.matmul(bank(idx % 2, (b + 1) * P), qi[ps, h // 2, b * P:(b + 1) * P],
                                     ki[ps, 0:(b + 1) * P], start=True, stop=True).then_inc(logits_ready, 1)

                def scores(b, h):
                    n = b * HEADS + h
                    ps = slice(64 * (h % 2), 64 * (h % 2) + 64)
                    if n >= 2:
                        pe.wait_ge(scores_taken, n - 1)
                    nc.tensor.matmul(bank(2 + n % 2, (b + 1) * P), q[ps, h // 2, b * P:(b + 1) * P],
                                     kd[ps, h // 4, 0:(b + 1) * P], start=True, stop=True).then_inc(scores_ready, 1)

                def turn(b, h):
                    n = b * HEADS + h
                    pe.wait_ge(normed, n + 1)
                    if n >= 2:
                        pe.wait_ge(turned_taken, n - 1)
                    for s in range(b + 1):
                        last = nc.tensor.transpose(psum[:, (4 + n % 2) * 512 + s * P:(4 + n % 2) * 512 + (s + 1) * P],
                                                   prob[:, h, s * P:(s + 1) * P], ident)
                    last.then_inc(turned, 1)

                def values(b, n):
                    done = 2 * b + n
                    pe.wait_ge(turned_taken, b * HEADS + 4 * n + 4)
                    if done >= 2:
                        pe.wait_ge(o_taken, done - 1)
                    for e in range(2):
                        for s in range(b + 1):
                            last = nc.tensor.matmul(psum[64 * e:64 * e + 64, (6 + done % 2) * 512:(6 + done % 2) * 512 + 2 * P],
                                                    v[:, s, 64 * n:64 * n + 64], prob_t[:, n, s, e::2, :],
                                                    start=s == 0, stop=s == b)
                    last.then_inc(pv_ready, 1)

                idx = 0
                for b in range(QB):
                    if b:
                        for h in range(HEADS):
                            logits(b, h, idx)
                            idx += 1
                    for h in range(HEADS + 3):
                        if h < HEADS:
                            scores(b, h)
                        if h >= 3:
                            turn(b, h - 3)
                            if (h - 3) % 4 == 3:
                                values(b, (h - 3) // 4)

            @block.scalar
            def _(act):
                idx = 0
                for b in range(QB):
                    if b:
                        for h in range(HEADS):
                            act.wait_ge(logits_ready, idx + 1)
                            if idx >= 2:
                                act.wait_ge(weighted, idx - 1)
                            nc.scalar.activation(relu[:, idx % 2, 0:(b + 1) * P], bank(idx % 2, (b + 1) * P), ACT.Relu,
                                                 scale=(HEAD_DIM * HEADS) ** -0.5).then_inc(logits_taken, 1)
                            idx += 1

                    def exp(h):
                        act.wait_ge(max_ready, b * HEADS + h + 1)
                        x = prob[:, h, 0:(b + 1) * P]
                        nc.scalar.activation(x, x, ACT.Exp, bias=stat[:, 0, h:h + 1], accum_out=stat[:, 1, h:h + 1])\
                            .then_inc(exp_ready, 1)

                    def take(h):
                        n = b * HEADS + h
                        act.wait_ge(turned, n + 1)
                        if b and h % 4 == 0:
                            act.wait_ge(pv_ready, 2 * (b - 1) + h // 4 + 1)
                        nc.scalar.activation(prob_t[:, h // 4, 0:b + 1, h % 4, :],
                                             bank(4 + n % 2, (b + 1) * P).rearrange("p (s n) -> p s n", n=P), ACT.Identity)\
                            .then_inc(turned_taken, 1)

                    for h in range(HEADS + 3):
                        if h < HEADS:
                            exp(h)
                        if h >= 3:
                            take(h - 3)

            @block.vector
            def _(dve):
                chain = Chain(dve, step)
                idx = 0
                for b in range(QB):
                    S = (b + 1) * P
                    if b:
                        for h in range(HEADS):
                            dve.wait_ge(logits_taken, idx + 1)
                            if h == 0:
                                made = nc.vector.tensor_scalar(score[:, 0:S], relu[:, idx % 2, 0:S], wi[:, b, 0:1], None, ALU.mult)
                            else:
                                made = nc.vector.scalar_tensor_tensor(score[:, 0:S], relu[:, idx % 2, 0:S], wi[:, b, h:h + 1],
                                                                      score[:, 0:S], ALU.mult, ALU.add)
                            made.then_inc(weighted, 1)
                            idx += 1
                            dve.wait_ge(weighted, idx)
                        diag = score[:, b * P:S]
                        chain.then(nc.vector.tensor_tensor(diag, diag, common["future"], ALU.add))
                        for _ in range(TOPK // 8):
                            chain.then(nc.vector.max(top8[:, :], score[:, 0:S]))
                            chain.then(nc.vector.match_replace(score[:, 0:S], top8[:, :], score[:, 0:S], PICKED))
                        chain.then(nc.vector.tensor_scalar(left_out[:, 0:S], score[:, 0:S], -2.5e38, MASKED, ALU.is_gt, ALU.mult))
                    else:
                        chain.then(nc.vector.tensor_copy(left_out[:, 0:P], common["masked"]))

                    def peak(h):
                        n = b * HEADS + h
                        dve.wait_ge(scores_ready, n + 1)
                        if b:
                            dve.wait_ge(turned, n - HEADS + 1)
                        nc.vector.scalar_tensor_tensor(prob[:, h, 0:S], bank(2 + n % 2, S), HEAD_DIM ** -0.5, left_out[:, 0:S],
                                                       ALU.mult, ALU.add).then_inc(scores_taken, 1)
                        dve.wait_ge(scores_taken, n + 1)
                        nc.vector.tensor_reduce(stat[:, 0, h:h + 1], prob[:, h, 0:S], AX_X, ALU.max, negate=True)\
                            .then_inc(max_ready, 1)

                    def norm(h):
                        dve.wait_ge(exp_ready, b * HEADS + h + 1)
                        chain.then(nc.vector.reciprocal(stat[:, 2, h:h + 1], stat[:, 1, h:h + 1]))
                        nc.vector.tensor_scalar(prob[:, h, 0:S], prob[:, h, 0:S], stat[:, 2, h:h + 1], None, ALU.mult)\
                            .then_inc(normed, 1)

                    for h in range(HEADS + 2):
                        if h < HEADS:
                            peak(h)
                        if h >= 2:
                            norm(h - 2)
                    for n in range(2):
                        done = 2 * b + n
                        dve.wait_ge(pv_ready, done + 1)
                        nc.vector.tensor_copy(o[:, 2 * n:2 * n + 2, b * P:S],
                                              bank(6 + done % 2, 2 * P).rearrange("p (c n) -> p c n", c=2)).then_inc(o_taken, 1)


def product_stage(nc, ring, loads, groups, psum, regions, evacuate, also_pe=None, also_dve=None,
                  more=""):
    names = Products.names(ring.shape[1]) + " " + more
    with stage(nc, names) as (block, sems):
        n_own = ring.shape[1] + 3
        s = Products(nc, sems[:n_own], ring, loads, groups, psum, regions)
        s.more = sems[n_own:]

        @block.sync
        def _(sp):
            s.load(sp)

        @block.tensor
        def _(pe):
            for g in range(len(groups)):
                s.multiply(pe, g)
                if also_pe:
                    also_pe(pe, g, s)

        @block.scalar
        def _(act):
            for g, group in enumerate(groups):
                if group[2] == "act":
                    act.wait_ge(s.ready, g + 1)
                    evacuate("act", g, s.region(g)).then_inc(s.by_act, 1)

        @block.vector
        def _(dve):
            if also_dve:
                also_dve(dve, s)
            for g, group in enumerate(groups):
                if group[2] == "dve":
                    dve.wait_ge(s.ready, g + 1)
                    evacuate("dve", g, s.region(g)).then_inc(s.by_dve, 1)


def dense(nc, offset, n_k, moving, start=True, stop=True, width=P, step=512, out=None):
    made = []
    for k in range(n_k):
        def make(slot, region, k=k):
            to = region
            if out:
                p0, np_, c0, nc_ = out
                to = region[p0:p0 + np_, c0:c0 + nc_]
            at = offset + k * step
            return nc.tensor.matmul(to, slot[:, at:at + width], moving(k),
                                    start=start and k == 0, stop=stop and k == n_k - 1)
        made.append(make)
    return made


def transpose_in(nc, x_tokens, h, psum, ident, x_dram):
    with stage(nc, "x_landed turned taken") as (block, sems):
        x_landed, turned, taken = sems

        @block.sync
        def _(sp):
            sp.dma_start(x_tokens[:, :, :], x_dram.rearrange("(b p) d -> p b d", p=P))\
                .then_inc(x_landed, 16)

        @block.tensor
        def _(pe):
            pe.wait_ge(x_landed, 16)
            for c in range(KD):
                if c >= 4:
                    pe.wait_ge(taken, c - 3)
                for b in range(x_tokens.shape[1]):
                    last = nc.tensor.transpose(psum[:, (c % 4) * 512 + b * P:(c % 4) * 512 + (b + 1) * P],
                                               x_tokens[:, b, c * P:(c + 1) * P], ident)
                last.then_inc(turned, 1)

        @block.vector
        def _(dve):
            width = x_tokens.shape[1] * P
            for c in range(KD):
                dve.wait_ge(turned, c + 1)
                nc.vector.tensor_copy(h[:, c, :], psum[:, (c % 4) * 512:(c % 4) * 512 + width])\
                    .then_inc(taken, 1)


def rope_tables(nc, pos_i, cos, sin, tmp, positions, inv_freq):
    with stage(nc, "positions_landed step reduced cos_arg") as (block, sems):
        positions_landed, step, reduced, cos_arg = sems
        a, q = tmp[:, 0, :], tmp[:, 1, :]

        @block.sync
        def _(sp):
            sp.dma_start(pos_i[:, :], positions.partition_broadcast(P)).then_inc(positions_landed, 16)

        @block.vector
        def _(dve):
            c = Chain(dve, step)
            dve.wait_ge(positions_landed, 16)
            c.then(nc.vector.tensor_copy(a, pos_i[:, :]))
            c.then(nc.vector.tensor_scalar(a, a, inv_freq, None, ALU.mult))
            c.then(nc.vector.tensor_scalar(q, a, float(np.float32(1 / (2 * math.pi))), ROUND, ALU.mult, ALU.add))
            c.then(nc.vector.tensor_scalar(q, q, ROUND, None, ALU.subtract))
            for part in (TWO_PI_1, TWO_PI_2, TWO_PI_3):
                c.then(nc.vector.scalar_tensor_tensor(a, q, -part, a, ALU.mult, ALU.add))
            nc.vector.tensor_scalar(a, a, PI_IN, -PI_IN, ALU.min, ALU.max).then_inc(reduced, 1)
            dve.wait_ge(reduced, 1)
            c.then(nc.vector.scalar_tensor_tensor(q, a, -1.0, a, ALU.mult, ALU.max))
            nc.vector.tensor_scalar(q, q, -1.0, math.pi / 2, ALU.mult, ALU.add).then_inc(cos_arg, 1)

        @block.scalar
        def _(act):
            act.wait_ge(reduced, 1)
            nc.scalar.activation(sin, a, ACT.Sin)
            act.wait_ge(cos_arg, 1)
            nc.scalar.activation(cos, q, ACT.Sin)


def first_block_layer(nc, l, w, h, common, psum, cos, sin, columns, rows):
    ident, mean_d, rot64 = common["ident"], common["mean_d"], common["rot64"]
    w_in = layer(w["w_in"], l).rearrange("(k p) n -> p k n", p=P)
    b_in = layer(w["b_in"], l)

    vectors, at = [], {}
    row = 0

    def put(name, view):
        nonlocal row
        at[name] = row
        vectors.append((view, row, 0))
        row += view.shape[0]

    def seg(a, n):
        return b_in[a:a + n].rearrange("(c p) -> c p", p=P)

    put("b_q", seg(C_Q, 512))
    for name, start in (("b_k0", C_K), ("b_k1", C_K + 64), ("b_ki", C_KI)):
        at[name] = row
        for half in range(2):
            vectors.append((b_in[start:start + 64].rearrange("(c p) -> c p", p=64), row, 64 * half))
        row += 1
    put("b_qi", seg(C_QI, 512))
    put("b_pool", seg(C_POOL, 256))
    put("b_conv", seg(C_CONV, 512))
    put("b_gate", seg(C_GATE, 3 * D))
    vec = lambda name: layer(w[name], l).rearrange("(c p) -> c p", p=P)
    mat = lambda name: layer(w[name], l).rearrange("k (c p) -> (k c) p", p=P)
    put("pool_scale", vec("pool_scale"))
    put("conv_w", mat("conv_dw_w"))
    for name in ("conv_dw_b", "conv_ln_g", "conv_ln_b", "ln1_g", "ln1_b", "ln2_g", "ln2_b", "ffn_dw_b"):
        put(name, vec(name))
    put("ffn_w", mat("ffn_dw_w"))
    assert row <= rows.shape[1] * P
    load_columns(nc, rows, columns, psum, ident, vectors)
    col = lambda name, i=0: cols(columns, at[name] + i)

    with ExitStack() as ctx:
        sb = lambda name, shape: ctx.enter_context(nc.sbuf_tensor(name, shape, F32))
        gates = sb("gates", [P, 3 * KD, L])
        queries = sb("queries", [P, 8, L])
        q, qi = queries[:, 0:4, :], queries[:, 4:8, :]
        kd = sb("k_twice", [P, 2, L])
        ki = sb("k_idx_twice", [P, L])
        v = sb("v", [P, QB, P])
        wi = sb("w_idx", [P, QB, 8])
        pool_in = sb("pool_in", [P, 2, L])
        conv = sb("conv", [P, 2, L])
        vrow = sb("bias_rows", [1, P + 8])
        ones = sb("ones", [1, P])

        with ExitStack() as inner:
            sbi = lambda name, shape: inner.enter_context(nc.sbuf_tensor(name, shape, F32))
            ring = sbi("ring", [P, 3, KD * 512])
            conv_a = sbi("conv_a", [P, 2, L])
            conv_g = sbi("conv_g", [P, 2, L])
            padded = sbi("conv_padded", [P, 2, L + TAPS - 1])
            rope_t = sbi("rope_t", [P, 2, L])
            sums = sbi("sums", [P, 2, L])

            with stage(nc, "bias_landed") as (block, sems):
                @block.sync
                def _(sp):
                    sp.dma_start(vrow[:, 0:P], b_in[C_V:C_V + P].rearrange("(o p) -> o p", o=1)).then_inc(sems[0], 16)
                    sp.dma_start(vrow[:, P:P + 8], b_in[C_WI:C_WI + 8].rearrange("(o p) -> o p", o=1)).then_inc(sems[0], 16)
                    sp.wait_ge(sems[0], 32)

                @block.vector
                def _(dve):
                    nc.vector.memset(ones[:, :], 1.0)
                    nc.vector.memset(padded[:, :, 0:TAPS - 1], 0.0)

            def tile(*segments):
                out, done = [], 0
                for start, n in segments:
                    out.append((done, n, w_in[:, :, start:start + n]))
                    done += n
                return out

            tiles = [tile((C_Q, 512)),
                     tile((C_K, 64), (C_K, 64), (C_K + 64, 64), (C_K + 64, 64), (C_KI, 64), (C_KI, 64), (C_V, 128)),
                     tile((C_QI, 512)),
                     tile((C_CONV, 512)),
                     tile((C_POOL, 256), (C_WI, 8))]
            tiles += [tile((C_GATE + 512 * i, 512)) for i in range(6)]
            loads = [[(KD * at_, (KD, n), view) for at_, n, view in t] for t in tiles]
            hk = lambda k: h[:, k, :]
            groups, what = [], []

            def feature(tile_i, seg_at, seg_n, c, kind, i, who="act"):
                groups.append((tile_i, dense(nc, KD * seg_at + c, KD, hk, step=seg_n), who))
                what.append((kind, i))

            def halves(tile_i, seg_at, kind):
                made = []
                for half in range(2):
                    made += dense(nc, KD * (seg_at + 64 * half), KD, hk, width=64, step=64,
                                  out=(64 * half, 64, 0, L))
                groups.append((tile_i, made, "act"))
                what.append((kind, 0))

            def by_token(tile_i, seg_at, n, bias_at, kind, who):
                made = []
                for b in range(QB):
                    for k in range(KD + 1):
                        def make(slot, region, k=k, b=b):
                            out = region[:, b * n:(b + 1) * n]
                            if k == KD:
                                return nc.tensor.matmul(out, ones[:, :], vrow[:, bias_at:bias_at + n], start=False, stop=True)
                            at_ = KD * seg_at + k * n
                            return nc.tensor.matmul(out, h[:, k, b * P:(b + 1) * P], slot[:, at_:at_ + n],
                                                    start=k == 0, stop=False)
                        made.append(make)
                groups.append((tile_i, made, who))
                what.append((kind, 0))

            for i in range(4):
                feature(0, 0, 512, i * P, "q", i)
            halves(1, 0, "k0")
            halves(1, 128, "k1")
            halves(1, 256, "ki")
            by_token(1, 384, 128, 0, "v", "act")
            for i in range(4):
                feature(2, 0, 512, i * P, "qi", i)
            for i in range(4):
                feature(3, 0, 512, i * P, "conv_a" if i < 2 else "conv_g", i % 2)
            for i in range(2):
                feature(4, 0, 256, i * P, "pool", i)
            by_token(4, 256, 8, P, "wi", "act")
            for i in range(24):
                feature(5 + i // 4, 0, 512, (i % 4) * P, "gate", i)
            home = {"q": lambda i: q[:, i, :], "k0": lambda i: kd[:, 0, :], "k1": lambda i: kd[:, 1, :],
                    "ki": lambda i: ki[:, :], "qi": lambda i: qi[:, i, :]}
            bias_of = {"q": "b_q", "k0": "b_k0", "k1": "b_k1", "ki": "b_ki", "qi": "b_qi"}
            roped = [(g, home[kind](i)) for g, (kind, i) in enumerate(what) if kind in home]
            rope_at = {g: n for n, (g, _) in enumerate(roped)}
            done_at = {w_: g for g, w_ in enumerate(what)}

            def evacuate(_, g, region):
                kind, i = what[g]
                if kind in home:
                    return nc.scalar.activation(home[kind](i), region, ACT.Identity, bias=col(bias_of[kind], i))
                if kind == "v":
                    return nc.scalar.activation(v[:, :, :], region.rearrange("p (b n) -> p b n", b=QB), ACT.Identity)
                if kind == "wi":
                    return nc.scalar.activation(wi[:, :, :], region[:, 0:QB * 8].rearrange("p (b n) -> p b n", b=QB), ACT.Identity)
                if kind == "conv_a":
                    return nc.scalar.activation(conv_a[:, i, :], region, ACT.Identity, bias=col("b_conv", i))
                if kind == "conv_g":
                    return nc.scalar.activation(conv_g[:, i, :], region, ACT.Sigmoid, bias=col("b_conv", 2 + i))
                if kind == "pool":
                    return nc.scalar.activation(pool_in[:, i, :], region, ACT.Identity, bias=col("b_pool", i))
                return nc.scalar.activation(gates[:, i, :], region, ACT.Sigmoid, bias=col("b_gate", i))

            rotated = [psum[:, 6 * 512:7 * 512], psum[:, 7 * 512:8 * 512]]

            def also_pe(pe, g, s):
                turned, roped_out, _ = s.more
                if g - 1 in rope_at:
                    n = rope_at[g - 1]
                    pe.wait_ge(s.by_act, s.evacuated(g - 1, "act"))
                    if n >= 2:
                        pe.wait_ge(roped_out, n - 1)
                    nc.tensor.matmul(rotated[n % 2], rot64, roped[n][1], start=True, stop=True).then_inc(turned, 1)

            def also_dve(dve, s):
                turned, roped_out, step = s.more
                chain = Chain(dve, step)
                for n, (g, x) in enumerate(roped):
                    dve.wait_ge(turned, n + 1)
                    chain.then(nc.vector.tensor_tensor(rope_t[:, n % 2, :], rotated[n % 2], sin, ALU.mult))
                    chain.then(nc.vector.tensor_tensor(x, x, cos, ALU.mult))
                    nc.vector.tensor_tensor(x, x, rope_t[:, n % 2, :], ALU.add).then_inc(roped_out, 1)
                for i in range(2):
                    dve.wait_ge(s.by_act, s.evacuated(done_at[("conv_g", i)], "act"))
                    chain.then(nc.vector.tensor_tensor(padded[:, i, TAPS - 1:], conv_a[:, i, :], conv_g[:, i, :], ALU.mult))
                    chain.then(nc.vector.tensor_scalar(conv[:, i, :], padded[:, i, TAPS - 1:], col("conv_w", 2 * (TAPS - 1) + i),
                                                       col("conv_dw_b", i), ALU.mult, ALU.add))
                    for k in range(TAPS - 1):
                        chain.then(nc.vector.scalar_tensor_tensor(conv[:, i, :], padded[:, i, k:k + L], col("conv_w", 2 * k + i),
                                                                  conv[:, i, :], ALU.mult, ALU.add))
                for i in range(2):
                    dve.wait_ge(s.by_act, s.evacuated(done_at[("pool", i)], "act"))
                    a, b = sums[:, 0, :], sums[:, 1, :]
                    for half in range(2):
                        ps = slice(64 * half, 64 * half + 64)
                        src, shift, which = pool_in[ps, i, :], 1, 0
                        win = POOL_WINDOWS[2 * i + half]
                        while shift < win:
                            dst = sums[ps, which, :]
                            chain.then(nc.vector.tensor_tensor(dst[:, shift:], src[:, shift:], src[:, 0:L - shift], ALU.add))
                            chain.then(nc.vector.tensor_copy(dst[:, 0:shift], src[:, 0:shift]))
                            src, which, shift = dst, 1 - which, 2 * shift
                        cut = common["pool_cut"][ps, i * POOL_TAIL:(i + 1) * POOL_TAIL]
                        x = pool_in[ps, i, :]
                        other = sums[ps, which, 0:POOL_TAIL]
                        chain.then(nc.vector.tensor_tensor(other, src[:, 0:POOL_TAIL], cut, ALU.mult))
                        chain.then(nc.vector.scalar_tensor_tensor(x[:, POOL_TAIL:], src[:, POOL_TAIL:], 1.0 / win,
                                                                  x[:, POOL_TAIL:], ALU.mult, ALU.subtract))
                        chain.then(nc.vector.tensor_tensor(x[:, 0:POOL_TAIL], other, x[:, 0:POOL_TAIL], ALU.subtract))

            product_stage(nc, ring, loads, groups, psum, [(512 * b, 512) for b in range(6)], evacuate,
                          also_pe, also_dve, "turned roped step")


        o = sb("o", [P, 4, L])
        attention(nc, q, kd, qi, ki, v, wi, o, psum, common)

        with ExitStack() as inner:
            sbi = lambda name, shape: inner.enter_context(nc.sbuf_tensor(name, shape, F32))
            ring = sbi("ring2", [P, 3, KD * 512])
            pool_y = sbi("pool_y", [P, 2, L])
            sq = queries[:, :, :]
            stats = sbi("stats", [P, L])
            merged = sbi("merged", [P, KD, L])
            y3 = sbi("y3", [P, 3, L])
            pool_w = sbi("pool_w", [P, 2, 64])

            pw = layer(w["pool_w"], l)
            with stage(nc, "pool_w_landed mixed") as (block, sems):
                landed, mixed = sems

                @block.sync
                def _(sp):
                    for half in range(2):
                        sp.dma_start(pool_w[64 * half:64 * half + 64, :, :],
                                     pw.rearrange("(c h) i j -> h i c j", c=2)[half]).then_inc(landed, 16)

                @block.tensor
                def _(pe):
                    pe.wait_ge(landed, 32)
                    for c in range(2):
                        for half in range(2):
                            ps = slice(64 * half, 64 * half + 64)
                            last = nc.tensor.matmul(psum[ps, c * 512:(c + 1) * 512], pool_w[ps, c, :], pool_in[ps, c, :],
                                                    start=True, stop=True)
                    last.then_inc(mixed, 1)

                @block.vector
                def _(dve):
                    dve.wait_ge(mixed, 1)
                    for c in range(2):
                        nc.vector.tensor_scalar(pool_y[:, c, :], psum[:, c * 512:(c + 1) * 512], col("pool_scale", c), None, ALU.mult)

            layer_norm(nc, conv[:, :, :], sq[:, 0:2, :], stats[:, :], psum, common["mean_conv"],
                       columns[:, at["conv_ln_g"]:at["conv_ln_g"] + 2], columns[:, at["conv_ln_b"]:at["conv_ln_b"] + 2],
                       1e-5, silu=True)

            outs = [layer(w[n], l).rearrange("(k p) n -> p k n", p=P) for n in ("w_pool_out", "w_conv_out", "w_attn_out")]
            loads = [[(0, (2, 512), outs[0][:, :, 512 * i:512 * i + 512]),
                      (1024, (2, 512), outs[1][:, :, 512 * i:512 * i + 512]),
                      (2048, (4, 512), outs[2][:, :, 512 * i:512 * i + 512])] for i in range(2)]
            groups = []
            for m in range(KD):
                at_ = (m % 4) * P
                groups.append((m // 4, dense(nc, at_, 2, lambda k: pool_y[:, k, :]), "dve"))
                groups.append((m // 4, dense(nc, 1024 + at_, 2, lambda k: conv[:, k, :]), "dve"))
                groups.append((m // 4, dense(nc, 2048 + at_, 4, lambda k: o[:, k, :]), "dve"))

            def merge(dve, s):
                (step,) = s.more
                chain = Chain(dve, step)
                for m in range(KD):
                    for j in range(3):
                        g = 3 * m + j
                        dve.wait_ge(s.ready, g + 1)
                        nc.vector.tensor_tensor(y3[:, j, :], s.region(g), gates[:, j * KD + m, :], ALU.mult).then_inc(s.by_dve, 1)
                    dve.wait_ge(s.by_dve, 3 * m + 3)
                    chain.then(nc.vector.tensor_tensor(y3[:, 0, :], y3[:, 0, :], y3[:, 1, :], ALU.add))
                    chain.then(nc.vector.tensor_tensor(merged[:, m, :], y3[:, 0, :], y3[:, 2, :], ALU.add))

            stream(nc, ring, loads, groups, psum, [(512 * b, 512) for b in range(8)], merge, "step")

            wo = layer(w["w_o"], l).rearrange("(k p) n -> p k n", p=P)
            loads = [[(0, (KD, 512), wo[:, :, 512 * i:512 * i + 512])] for i in range(2)]
            groups = [(m // 4, dense(nc, (m % 4) * P, KD, lambda k: merged[:, k, :]), "dve") for m in range(KD)]
            product_stage(nc, ring, loads, groups, psum, [(512 * b, 512) for b in range(8)],
                          lambda _, g, region: nc.vector.scalar_tensor_tensor(h[:, g, :], h[:, g, :], ALPHA, region, ALU.mult, ALU.add))
            layer_norm(nc, h, sq, stats[:, :], psum, mean_d, columns[:, at["ln1_g"]:at["ln1_g"] + KD],
                       columns[:, at["ln1_b"]:at["ln1_b"] + KD], 1e-5)

    with ExitStack() as inner:
        sbi = lambda name, shape: inner.enter_context(nc.sbuf_tensor(name, shape, F32))
        ring = sbi("ring3", [P, 3, KD * 512])
        act_ = sbi("hidden", [P, KF, L])
        u = sbi("u", [P, 4, L + 2])
        cv = sbi("cv", [P, 4, L])
        sq = sbi("sq2", [P, KD, L])
        stats = sbi("stats2", [P, L])
        with stage(nc, "unused") as (block, sems):
            @block.vector
            def _(dve):
                nc.vector.memset(u[:, :, 0:2], 0.0)
        wu = layer(w["w_up"], l).rearrange("(k p) n -> p k n", p=P)
        loads = [[(0, (KD, 256), wu[:, :, 256 * i:256 * i + 256]),
                  (KD * 256, (KD, 256), wu[:, :, D_FF + 256 * i:D_FF + 256 * i + 256])] for i in range(KF // 2)]
        hk = lambda k: h[:, k, :]
        groups = []
        for i in range(KF):
            for part in range(2):
                groups.append((i // 2, dense(nc, part * KD * 256 + (i % 2) * P, KD, hk, step=256), "act"))

        ffn_up(nc, ring, loads, groups, psum, u, cv, act_, col)
        wd = layer(w["w_down"], l).rearrange("(k p) n -> p k n", p=P)
        loads = [[(0, (KF, P), wd[:, :, P * m:P * m + P])] for m in range(KD)]
        groups = [(m, dense(nc, 0, KF, lambda k: act_[:, k, :], step=P), "dve") for m in range(KD)]
        product_stage(nc, ring, loads, groups, psum, [(512 * b, 512) for b in range(8)],
                      lambda _, g, region: nc.vector.scalar_tensor_tensor(h[:, g, :], h[:, g, :], ALPHA, region, ALU.mult, ALU.add))
        layer_norm(nc, h, sq, stats[:, :], psum, mean_d, columns[:, at["ln2_g"]:at["ln2_g"] + KD],
                   columns[:, at["ln2_b"]:at["ln2_b"] + KD], 1e-5)


EPS2 = 1e-6
SPLIT = ((0, CTX), (CTX, T2))
LEVELS = (2, 4, 8, 16, 32)


def wide(psum, i):
    return psum[:, i * 1024 + 1024 - T2:(i + 1) * 1024]


def modulation(nc, ring, psum, columns, at, mod, silu_c, w):
    loads, groups = [], []
    for l in range(DEPTH):
        aw = w["ada_w_2"][l].rearrange("(k p) n -> p k n", p=P)
        for i in range(6):
            loads.append([(0, (KD, 512), aw[:, :, 512 * i:512 * i + 512])])
        for m in range(24):
            groups.append((6 * l + m // 4, dense(nc, (m % 4) * P, KD, lambda k: silu_c[:, k, :], out=(0, P, 0, 2)), "dve"))
    product_stage(nc, ring, loads, groups, psum, [(512 * b, 512) for b in range(8)],
                  lambda _, g, region: nc.vector.tensor_scalar(mod[:, g // 24, g % 24, :], region[:, 0:2],
                                                               cols(columns, at["ada_b"] + g), None, ALU.add))


def rms_norm(nc, pieces, sq, stats, psum, mean_d):
    with stage(nc, "squared sum_ready safe root scaled rstd_ready") as (block, sems):
        squared, sum_ready, safe, root, scaled, rstd_ready = sems
        n = len(pieces)
        spans, done = [], 1024 - sum(x[0].shape[2] for x in pieces)
        for piece in pieces:
            spans.append((done, done + piece[0].shape[2]))
            done += piece[0].shape[2]
        lo, hi = spans[0][0], 1024

        @block.scalar
        def _(act):
            for (x, y, gain, bias, add_to), (a, b) in zip(pieces, spans):
                for c in range(KD):
                    nc.scalar.activation(sq[:, c, a - lo:b - lo], x[:, c, :], ACT.Square).then_inc(squared, 1)
            act.wait_ge(safe, 1)
            nc.scalar.activation(stats[:, 0:hi - lo], stats[:, 0:hi - lo], ACT.Sqrt).then_inc(root, 1)
            i = 0
            for (x, y, gain, bias, add_to), (a, b) in zip(pieces, spans):
                for c in range(KD):
                    i += 1
                    if add_to is None:
                        act.wait_ge(scaled, i)
                        nc.scalar.activation(y[:, c, :], y[:, c, :], ACT.Identity, bias=bias[:, c:c + 1],
                                             scale=gain[:, c:c + 1])

        @block.tensor
        def _(pe):
            for i, (a, b) in enumerate(spans):
                for c in range(KD):
                    pe.wait_ge(squared, i * KD + c + 1)
                    last = nc.tensor.matmul(psum[:, a:b], mean_d, sq[:, c, a - lo:b - lo], start=c == 0, stop=c == KD - 1)
            last.then_inc(sum_ready, 1)

        @block.vector
        def _(dve):
            dve.wait_ge(sum_ready, 1)
            nc.vector.tensor_scalar(stats[:, 0:hi - lo], psum[:, lo:hi], EPS2, None, ALU.add).then_inc(safe, 1)
            dve.wait_ge(root, 1)
            nc.vector.reciprocal(stats[:, 0:hi - lo], stats[:, 0:hi - lo]).then_inc(rstd_ready, 1)
            dve.wait_ge(rstd_ready, 1)
            i = 0
            for (x, y, gain, bias, add_to), (a, b) in zip(pieces, spans):
                for c in range(KD):
                    i += 1
                    nc.vector.tensor_tensor(y[:, c, :], x[:, c, :], stats[:, a - lo:b - lo], ALU.mult).then_inc(scaled, 1)
                    if add_to is not None:
                        dve.wait_ge(scaled, i)
                        nc.vector.scalar_tensor_tensor(add_to[:, c, :], y[:, c, :], gain[:, c:c + 1], add_to[:, c, :],
                                                       ALU.mult, ALU.add)


def serial(nc, steps):
    with stage(nc, "step_done") as (block, sems):
        (step_done,) = sems

        def run(engine, name):
            for i, (who, issue) in enumerate(steps):
                if who == name:
                    if i:
                        engine.wait_ge(step_done, i)
                    issue().then_inc(step_done, 1)

        @block.vector
        def _(dve):
            run(dve, "dve")

        @block.scalar
        def _(act):
            run(act, "act")

        @block.tensor
        def _(pe):
            run(pe, "pe")


def even_layer(nc, w, h, xc, common, psum, columns, at, mod, coef):
    ident = common["ident"]
    col = lambda name, i=0: cols(columns, at[name] + i)
    gates_dram = nc.dram_tensor("gates_spill", [P, 8, T2], F32, kind="Internal").ap()
    with ExitStack() as ctx:
        sb = lambda name, shape: ctx.enter_context(nc.sbuf_tensor("second_" + name, shape, F32))
        u = sb("mixed_in", [P, 20, T2])
        with ExitStack() as inner:
            sbi = lambda name, shape: inner.enter_context(nc.sbuf_tensor("second_" + name, shape, F32))
            gated = sbi("gated", [P, 10, T2])
            hn = sbi("hn", [P, KD, T2])
            stats = sbi("stats", [P, T2])
            norm_in(nc, h, xc, hn, gated[:, 0:KD, :], stats, psum, common, coef, 0)
            with ExitStack() as inner2:
                ring = inner2.enter_context(nc.sbuf_tensor("ring4", [P, 2, KD * 512], F32))
                raw = inner2.enter_context(nc.sbuf_tensor("raw", [P, 2, T2], F32))
                mus = inner2.enter_context(nc.sbuf_tensor("mus", [P, 7, 20], F32))
                mu = columns[:, at["mu"]:at["mu"] + 20]
                serial(nc, [("dve", lambda j=j: nc.vector.tensor_scalar(mus[:, j, :], mu, cols(common["lane"], j), None, ALU.mult))
                            for j in range(6)]
                       + [("dve", lambda: nc.vector.tensor_scalar(mus[:, 6, :], mu, -1.0, 1.0, ALU.mult, ALU.add))])
                ew = w["ev_w_in_2"][0].rearrange("(k p) n -> p k n", p=P)
                loads = [[(0, (KD, min(512, 3840 - 512 * i)), ew[:, :, 512 * i:min(512 * i + 512, 3840)])] for i in range(8)]
                groups = []
                for m in range(30):
                    step = 512 if m < 28 else 256
                    made = []
                    for a, b in SPLIT:
                        made += dense(nc, (m % 4) * P, KD, lambda k, a=a, b=b: hn[:, k, a:b], step=step, out=(0, P, a, b - a))
                    groups.append((m // 4, made, "act"))

                def evacuate(_, g, region):
                    if g < 20:
                        return nc.scalar.activation(raw[:, g % 2, :], region, ACT.Identity)
                    func = ACT.Identity if 26 <= g < 28 else ACT.Silu
                    return nc.scalar.activation(gated[:, g - 20, :], region, func)

                names = Products.names(2) + " step shifted"
                with stage(nc, names) as (block, sems):
                    s = Products(nc, sems[:5], ring, loads, groups, psum, [(1024 * r + 1024 - T2, T2) for r in range(4)])
                    step_, shifted = sems[5:]

                    @block.sync
                    def _(sp):
                        s.load(sp)

                    @block.tensor
                    def _(pe):
                        for g in range(len(groups)):
                            s.multiply(pe, g)

                    @block.scalar
                    def _(act):
                        for g in range(len(groups)):
                            act.wait_ge(s.ready, g + 1)
                            if 2 <= g < 20:
                                act.wait_ge(shifted, g - 1)
                            evacuate("act", g, s.region(g)).then_inc(s.by_act, 1)

                    @block.vector
                    def _(dve):
                        chain = Chain(dve, step_)
                        for g in range(20):
                            dve.wait_ge(s.by_act, g + 1)
                            x, y = raw[:, g % 2, :], u[:, g, :]
                            xg = x[:, CTX:].rearrange("p (r c) -> p r c", c=GRID_W)
                            yg = y[:, CTX:].rearrange("p (r c) -> p r c", c=GRID_W)
                            chain.then(nc.vector.tensor_scalar(y, x, mus[:, 6, g:g + 1], None, ALU.mult))
                            pairs = [(y[:, 1:CTX], x[:, 0:CTX - 1], 4), (y[:, 0:CTX - 1], x[:, 1:CTX], 5),
                                     (yg[:, :, 1:], xg[:, :, :-1], 0), (yg[:, :, :-1], xg[:, :, 1:], 1),
                                     (yg[:, 1:, :], xg[:, :-1, :], 2), (yg[:, :-1, :], xg[:, 1:, :], 3)]
                            for i, (dst, src, j) in enumerate(pairs):
                                made = nc.vector.scalar_tensor_tensor(dst, src, mus[:, j, g:g + 1], dst, ALU.mult, ALU.add)
                                if i < 5:
                                    chain.then(made)
                                else:
                                    made.then_inc(shifted, 1)
            fourier(nc, gated, psum, w, hn)
            with stage(nc, "spilled") as (block, sems):
                @block.sync
                def _(sp):
                    sp.dma_start(gates_dram, gated[:, 0:8, :]).then_inc(sems[0], 16)
                    sp.wait_ge(sems[0], 16)
        rwkv(nc, w, u, common, psum, col, at, columns)
        even_finish(nc, w, u, h, xc, gates_dram, psum, common, col, columns, at, coef)


def norm_in(nc, h, xc, hn, sq, stats, psum, common, coef, l):
    rms_norm(nc, [(xc, hn[:, :, 0:CTX], coef[:, l, 0, 1, :], coef[:, l, 1, 1, :], None),
                  (h, hn[:, :, CTX:T2], coef[:, l, 0, 0, :], coef[:, l, 1, 0, :], None)],
             sq, stats, psum, common["mean_d"])


def fourier(nc, gated, psum, w, hn):
    with ExitStack() as ctx:
        sb = lambda name, shape: ctx.enter_context(nc.sbuf_tensor("second_" + name, shape, F32))
        ch = sb("dft_channels", [P, 2 * P])
        seq = sb("dft_seq", [P, 2, 4, L])
        cx = sb("dft_ctx", [P, 2, 2, CTX])
        z = sb("z", [P, 2, 6, 2 * P])
        with stage(nc, "tables_landed by_channel taken by_token") as (block, sems):
            tables_landed, by_channel, taken, by_token = sems

            @block.sync
            def _(sp):
                a, n = CONST_AT["dft_ch"]
                sp.dma_start(ch[:, :], w["consts"][:, a:a + n]).then_inc(tables_landed, 16)
                sp.dma_start(seq[:, :, :, :], w["dft_seq"].rearrange("s (c p) f -> p s c f", p=P)).then_inc(tables_landed, 16)
                sp.dma_start(cx[:, :, :, :], w["dft_ctx"].rearrange("s (c p) f -> p s c f", p=P)).then_inc(tables_landed, 16)

            @block.tensor
            def _(pe):
                pe.wait_ge(tables_landed, 48)
                for j in range(2):
                    for t in range(6):
                        i = 6 * j + t
                        if i >= 2:
                            pe.wait_ge(taken, i - 1)
                        nc.tensor.matmul(psum[:, (i % 2) * 512:(i % 2) * 512 + 2 * P], gated[:, 6 + j, t * P:(t + 1) * P], ch[:, :],
                                         start=True, stop=True).then_inc(by_channel, 1)
                pe.wait_ge(taken, 12)
                for j in range(2):
                    out = wide(psum, 1 + j)
                    for table, t0, nt, a, b in ((cx, 0, 2, 0, CTX), (seq, 2, 4, CTX, T2)):
                        for part in range(2):
                            for t in range(nt):
                                last = nc.tensor.matmul(out[:, a:b], z[:, j, t0 + t, part * P:(part + 1) * P], table[:, part, t, :],
                                                        start=part == 0 and t == 0, stop=part == 1 and t == nt - 1)
                    last.then_inc(by_token, 1)

            @block.scalar
            def _(act):
                for i in range(12):
                    act.wait_ge(by_channel, i + 1)
                    nc.scalar.activation(z[:, i // 6, i % 6, :], psum[:, (i % 2) * 512:(i % 2) * 512 + 2 * P], ACT.Identity).then_inc(taken, 1)

            @block.vector
            def _(dve):
                for j in range(2):
                    dve.wait_ge(by_token, j + 1)
                    nc.vector.tensor_tensor(gated[:, 6 + j, :], wide(psum, 1 + j), gated[:, 8 + j, :], ALU.mult)


def rwkv(nc, w, u, common, psum, col, at, columns):
    with ExitStack() as ctx:
        sb = lambda name, shape: ctx.enter_context(nc.sbuf_tensor("second_" + name, shape, F32))
        m0 = CONST_AT["upper"][0]
        m1 = CONST_AT["dft_ch"][0]
        masks = sb("masks", [P, m1 - m0])
        mask = lambda name: masks[:, CONST_AT[name][0] - m0:sum(CONST_AT[name]) - m0]
        w2 = sb("w2", [P, 2, RWKV_W])
        T = lambda name: sb(name, [P, T2])
        BD = lambda name: sb(name, [P, NCH, P])
        reset, sg, cum, a, kk, k, o, e1, e2, e3 = (T(n) for n in "reset sg cum a kk k o e1 e2 e3".split())
        rt = e2
        a_bd, b_bd, k_bd, v_tok, b_tok, k_tok = (BD(n) for n in "a_bd b_bd k_bd v_tok b_tok k_tok".split())
        mt, nt, wf, wt, y = (BD(n) for n in "mt nt wf wt y_bd".split())
        v_bd = y
        mm = sb("mm", [P, 4, P])
        rb, rk = (x[:, :].rearrange("p (n t) -> p n t", t=CH) for x in (e3, cum))
        st, sts, xs, us = (sb(n, [P, P]) for n in ("st", "sts", "xs", "us"))
        omka = sb("omka", [P, RW_PAIRS])
        ident = common["ident"]
        V, S, PE = nc.vector, nc.scalar, nc.tensor
        w0_ = lambda i: wide(psum, i)
        by_chunk = lambda x: x.rearrange("p (n t) -> p n t", t=CH)

        with stage(nc, "landed") as (block, sems):
            @block.sync
            def _(sp):
                sp.dma_start(masks[:, :], w["consts"][:, m0:m1]).then_inc(sems[0], 16)
                sp.dma_start(w2[:, 0, :], w["ev_w2_2"][0].rearrange("d k n -> (d k) n")).then_inc(sems[0], 16)
                sp.dma_start(w2[:, 1, :], w["ev_a2_2"][0].rearrange("d k n -> (d k) n")).then_inc(sems[0], 16)
                sp.wait_ge(sems[0], 48)

            @block.vector
            def _(dve):
                for x in (a_bd, b_bd, k_bd):
                    V.memset(x[:, :, :], 0.0)
                V.memset(reset[:, :], 1.0).then_inc(sems[0], 0) if False else V.memset(reset[:, :], 1.0)
                V.tensor_scalar(omka[:, :], columns[:, at["k_a"]:at["k_a"] + 6], -1.0, 1.0, ALU.mult, ALU.add)

            @block.scalar
            def _(act):
                S.activation(u[:, 18, :], u[:, 18, :], ACT.Tanh)
        serial(nc, [("dve", lambda: V.memset(by_chunk(reset[:, :])[:, :, 0:1], 0.0))])

        def halves(dst, x, issue):
            for hf in range(2):
                ps = slice(64 * hf, 64 * hf + 64)
                yield ("dve", lambda ps=ps, hf=hf: issue(dst[ps, :, 64 * hf:64 * hf + 64], ps))

        def project(region, lhsT, rhs):
            for lo_, hi_ in SPLIT:
                last = PE.matmul(region[:, lo_:hi_], lhsT, rhs[:, lo_:hi_], start=True, stop=True)
            return last

        for p in range(RW_PAIRS):
            r, k0, v = u[:, p, :], u[:, 6 + p, :], u[:, 12 + p, :]
            for d in range(2):
                ds_ = slice(64 * d, 64 * d + 64)
                steps = []
                add = steps.append
                add(("pe", lambda: project(w0_(0), w2[ds_, 0, p * P:(p + 1) * P], u[ds_, 18, :])))
                add(("pe", lambda: project(w0_(1), w2[ds_, 1, p * P:(p + 1) * P], u[ds_, 19, :])))
                add(("act", lambda: S.activation(sg[:, :], w0_(0), ACT.Sigmoid, bias=col("w0", 6 * d + p))))
                add(("act", lambda: S.activation(a[:, :], w0_(1), ACT.Sigmoid, bias=col("a0", 6 * d + p))))
                add(("dve", lambda: V.tensor_tensor_scan(cum[:, :], reset[:, :], sg[:, :], 0.0, ALU.mult, ALU.add)))
                if d == 0:
                    add(("dve", lambda: V.tensor_copy(e1[:, :], cum[:, :])))
                    add(("dve", lambda: V.tensor_tensor(e2[:, :], cum[:, :], sg[:, :], ALU.subtract)))
                else:
                    total = by_chunk(cum[:, :])[:, :, CH - 1:CH].to_broadcast([P, NCH, CH])
                    add(("dve", lambda: V.tensor_tensor(by_chunk(e2[:, :]), total, by_chunk(cum[:, :]), ALU.subtract)))
                    add(("dve", lambda: V.tensor_tensor(e1[:, :], e2[:, :], sg[:, :], ALU.add)))
                add(("act", lambda: S.activation(e3[:, :], e1[:, :], ACT.Exp, scale=DECAY)))
                add(("act", lambda: S.activation(e1[:, :], e1[:, :], ACT.Exp, scale=-DECAY)))
                add(("act", lambda: S.activation(e2[:, :], e2[:, :], ACT.Exp, scale=-DECAY)))
                if d == 0:
                    add(("dve", lambda: V.tensor_scalar(kk[:, :], k0, col("k_k", p), None, ALU.mult)))
                    add(("act", lambda: S.activation(cum[:, :], kk[:, :], ACT.Square)))
                    add(("pe", lambda: project(w0_(0), common["head_sum"], cum[:, :])))
                    add(("dve", lambda: V.tensor_scalar(cum[:, :], w0_(0), 1e-24, None, ALU.max)))
                    add(("act", lambda: S.activation(cum[:, :], cum[:, :], ACT.Sqrt)))
                    add(("dve", lambda: V.reciprocal(cum[:, :], cum[:, :])))
                    add(("dve", lambda: V.tensor_tensor(kk[:, :], kk[:, :], cum[:, :], ALU.mult)))
                add(("dve", lambda: V.tensor_scalar(k[:, :], a[:, :], col("k_a", p), omka[:, p:p + 1], ALU.mult, ALU.add)))
                add(("dve", lambda: V.tensor_tensor(k[:, :], k[:, :], k0, ALU.mult)))
                add(("dve", lambda: V.scalar_tensor_tensor(cum[:, :], r, col("r_k", p), k[:, :], ALU.mult, ALU.mult)))
                add(("pe", lambda: project(w0_(0), common["head_sum"], cum[:, :])))
                if d == 0:
                    add(("dve", lambda: V.tensor_tensor(o[:, :], w0_(0), v, ALU.mult)))
                else:
                    add(("dve", lambda: V.tensor_tensor(cum[:, :], w0_(0), v, ALU.mult)))
                    add(("dve", lambda: V.tensor_tensor(o[:, :], o[:, :], cum[:, :], ALU.add)))
                steps += halves(a_bd, None, lambda dst, ps: V.scalar_tensor_tensor(dst, by_chunk(kk[ps, :]), -1.0, by_chunk(e2[ps, :]), ALU.mult, ALU.mult))
                add(("dve", lambda: V.tensor_tensor(cum[:, :], kk[:, :], a[:, :], ALU.mult)))
                steps += halves(b_bd, None, lambda dst, ps: V.tensor_tensor(dst, by_chunk(cum[ps, :]), by_chunk(e3[ps, :]), ALU.mult))
                steps += halves(k_bd, None, lambda dst, ps: V.tensor_tensor(dst, by_chunk(k[ps, :]), by_chunk(e3[ps, :]), ALU.mult))
                add(("dve", lambda: V.tensor_tensor(rt[:, :], r, e1[:, :], ALU.mult)))
                if d == 0:
                    add(("dve", lambda: V.memset(v_bd[:, :, :], 0.0)))
                    steps += halves(v_bd, None, lambda dst, ps: V.tensor_copy(dst, by_chunk(v[ps, :])))
                serial(nc, steps)

                up, lo_, up_eq = ("upper", "lower", "upper_eq") if d == 0 else ("lower", "upper", "lower_eq")
                pre_t, pre_f = ("up", "lo") if d == 0 else ("lo", "up")
                over = lambda name, n=P: mask(name).unsqueeze(1).to_broadcast([P, 4, n])
                turn = [(b_bd, b_tok), (k_bd, k_tok)] + ([(v_bd, v_tok)] if d == 0 else [])
                with stage(nc, "grams_ready grams_taken turned turned_taken step") as (block, sems):
                    grams_ready, grams_taken, turned, turned_taken, step = sems

                    @block.tensor
                    def _(pe):
                        j = 0
                        for g in range(3):
                            if g:
                                pe.wait_ge(grams_taken, g)
                            for i in range(4):
                                n = 4 * g + i
                                PE.matmul(psum[:, i * P:(i + 1) * P], b_bd[:, n, :], a_bd[:, n, :], start=True, stop=True)
                                PE.matmul(psum[:, 512 + i * P:512 + (i + 1) * P], a_bd[:, n, :], b_bd[:, n, :], start=True, stop=True)
                                PE.matmul(psum[:, 1024 + i * P:1024 + (i + 1) * P], k_bd[:, n, :], a_bd[:, n, :], start=True, stop=True)
                                PE.matmul(psum[:, 1536 + i * CH:1536 + (i + 1) * CH], b_bd[:, n, :], rt[:, n * CH:(n + 1) * CH], start=True, stop=True)
                                last = PE.matmul(psum[:, 2048 + i * CH:2048 + (i + 1) * CH], k_bd[:, n, :], rt[:, n * CH:(n + 1) * CH], start=True, stop=True)
                            last.then_inc(grams_ready, 1)
                            for src, dst in turn:
                                if j >= 2:
                                    pe.wait_ge(turned_taken, j - 1)
                                for i in range(4):
                                    bank = (6 + j % 2) * 512
                                    last = PE.transpose(psum[:, bank + i * P:bank + (i + 1) * P], src[:, 4 * g + i, :], ident)
                                last.then_inc(turned, 1)
                                j += 1

                    @block.scalar
                    def _(act):
                        j = 0
                        for g in range(3):
                            for src, dst in turn:
                                act.wait_ge(turned, j + 1)
                                bank = (6 + j % 2) * 512
                                S.activation(dst[:, 4 * g:4 * g + 4, :], psum[:, bank:bank + 512].rearrange("p (i n) -> p i n", n=P), ACT.Identity)\
                                    .then_inc(turned_taken, 1)
                                j += 1

                    @block.vector
                    def _(dve):
                        chain = Chain(dve, step)
                        four = lambda b, n=P: psum[:, b * 512:b * 512 + 4 * n].rearrange("p (i n) -> p i n", n=n)
                        for g in range(3):
                            gs = slice(4 * g, 4 * g + 4)
                            dve.wait_ge(grams_ready, g + 1)
                            eye4 = ident.unsqueeze(1).to_broadcast([P, 4, P])
                            V.tensor_tensor(rb[:, gs, :], four(3, CH), over(up_eq, CH), ALU.mult)
                            V.tensor_tensor(rk[:, gs, :], four(4, CH), over(up_eq, CH), ALU.mult)
                            V.tensor_tensor(nt[:, gs, :], four(2), over(up), ALU.mult)
                            V.tensor_tensor(mt[:, gs, :], four(0), over(up), ALU.mult)
                            chain.then(V.tensor_tensor(wf[:, gs, :], four(1), over(pre_f + "1"), ALU.mult))
                            V.tensor_tensor(wf[:, gs, :], wf[:, gs, :], eye4, ALU.add).then_inc(grams_taken, 1)
                            chain.then(V.tensor_tensor(wt[:, gs, :], mt[:, gs, :], over(pre_t + "1"), ALU.mult))
                            chain.then(V.tensor_tensor(wt[:, gs, :], wt[:, gs, :], eye4, ALU.add))

                with stage(nc, "masked y_ready y_taken ww_ready wt_ready w_added wt_added") as (block, sems):
                    masked, y_ready, y_taken, ww_ready, wt_ready, w_added, wt_added = sems
                    rounds = [(lv, g) for lv in range(len(LEVELS)) for g in range(3)]
                    bank_y = lambda g: 2 * g
                    four_ = lambda b: psum[:, b * 512:(b + 1) * 512].rearrange("p (i n) -> p i n", n=P)

                    @block.gpsimd
                    def _(pool):
                        for i, (lv, g) in enumerate(rounds):
                            if i:
                                pool.wait_ge(y_ready, i)
                            nc.gpsimd.tensor_tensor(mm[:, :, :], mt[:, 4 * g:4 * g + 4, :], over(f"{pre_t}{LEVELS[lv]}"), ALU.mult)\
                                .then_inc(masked, 1)

                    @block.tensor
                    def _(pe):
                        def first(i):
                            lv, g = rounds[i]
                            pe.wait_ge(masked, i + 1)
                            if i >= 3:
                                pe.wait_ge(w_added, i - 2)
                                pe.wait_ge(wt_added, i - 2)
                            for n in range(4):
                                last = PE.matmul(four_(bank_y(g))[:, n, :], mm[:, n, :], wf[:, 4 * g + n, :], start=True, stop=True)
                            last.then_inc(y_ready, 1)

                        def second(i):
                            lv, g = rounds[i]
                            pe.wait_ge(y_taken, i + 1)
                            for n in range(4):
                                last = PE.matmul(four_(bank_y(g) + 1)[:, n, :], wt[:, 4 * g + n, :], y[:, 4 * g + n, :], start=True, stop=True)
                            last.then_inc(ww_ready, 1)
                            for n in range(4):
                                last = PE.matmul(four_(bank_y(g))[:, n, :], y[:, 4 * g + n, :], wt[:, 4 * g + n, :], start=True, stop=True)
                            last.then_inc(wt_ready, 1)

                        for i in range(len(rounds) + 1):
                            if i < len(rounds):
                                first(i)
                            if i >= 1:
                                second(i - 1)

                    @block.scalar
                    def _(act):
                        for i, (lv, g) in enumerate(rounds):
                            act.wait_ge(y_ready, i + 1)
                            S.activation(y[:, 4 * g:4 * g + 4, :], four_(bank_y(g)), ACT.Identity).then_inc(y_taken, 1)

                    @block.vector
                    def _(dve):
                        for i, (lv, g) in enumerate(rounds):
                            gs = slice(4 * g, 4 * g + 4)
                            dve.wait_ge(wt_ready, i + 1)
                            V.tensor_tensor(wf[:, gs, :], wf[:, gs, :], four_(bank_y(g) + 1), ALU.add).then_inc(w_added, 1)
                            V.tensor_tensor(wt[:, gs, :], wt[:, gs, :], four_(bank_y(g)), ALU.add).then_inc(wt_added, 1)

                order = list(range(NCH)) if d == 0 else [3, 2, 1, 0] + list(range(NCH - 1, 3, -1))
                with stage(nc, "x_ready x_taken u_ready u_taken o_ready o_added s_ready decayed state_ready") as (block, sems):
                    x_ready, x_taken, u_ready, u_taken, o_ready, o_added, s_ready, decayed, state_ready = sems
                    bank = lambda b, n=P: psum[:, b * 512:b * 512 + n]

                    @block.tensor
                    def _(pe):
                        for i, n in enumerate(order):
                            tok = slice(n * CH, (n + 1) * CH)
                            PE.matmul(bank(0), nt[:, n, :], v_tok[:, n, :], start=True, stop=False)
                            pe.wait_ge(state_ready, i + 1)
                            PE.matmul(bank(0), a_bd[:, n, :], st[:, :], start=False, stop=True).then_inc(x_ready, 1)
                            if i:
                                pe.wait_ge(o_added, i)
                            PE.matmul(bank(2, CH), st[:, :], rt[:, tok], start=True, stop=False)
                            PE.matmul(bank(2, CH), v_tok[:, n, :], rk[:, n, :], start=False, stop=False)
                            PE.matmul(bank(3), k_tok[:, n, :], v_tok[:, n, :], start=True, stop=False)
                            pe.wait_ge(x_taken, i + 1)
                            PE.matmul(bank(1), wt[:, n, :], xs[:, :], start=True, stop=True).then_inc(u_ready, 1)
                            pe.wait_ge(u_taken, i + 1)
                            PE.matmul(bank(3), b_tok[:, n, :], us[:, :], start=False, stop=True).then_inc(s_ready, 1)
                            PE.matmul(bank(2, CH), us[:, :], rb[:, n, :], start=False, stop=True).then_inc(o_ready, 1)

                    @block.scalar
                    def _(act):
                        for i, n in enumerate(order):
                            last_tok = n * CH + (CH - 1 if d == 0 else 0)
                            act.wait_ge(x_ready, i + 1)
                            S.activation(xs[:, :], bank(0), ACT.Identity).then_inc(x_taken, 1)
                            if i:
                                act.wait_ge(state_ready, i + 1)
                            S.activation(sts[:, :], st[:, :], ACT.Identity, scale=e1[:, last_tok:last_tok + 1]).then_inc(decayed, 1)

                    @block.vector
                    def _(dve):
                        V.memset(st[:, :], 0.0).then_inc(state_ready, 1)
                        for i, n in enumerate(order):
                            last_tok = n * CH + (CH - 1 if d == 0 else 0)
                            dve.wait_ge(u_ready, i + 1)
                            V.tensor_copy(us[:, :], bank(1)).then_inc(u_taken, 1)
                            dve.wait_ge(s_ready, i + 1)
                            dve.wait_ge(decayed, i + 1)
                            dve.wait_ge(o_ready, i + 1)
                            V.scalar_tensor_tensor(st[:, :], bank(3), e1[:, last_tok:last_tok + 1], sts[:, :], ALU.mult, ALU.add)\
                                .then_inc(state_ready, 1)
                            V.tensor_tensor(o[:, n * CH:(n + 1) * CH], o[:, n * CH:(n + 1) * CH], bank(2, CH), ALU.add).then_inc(o_added, 1)
            serial(nc, [("dve", lambda: V.tensor_copy(u[:, p, :], o[:, :]))])


def even_finish(nc, w, u, h, xc, gates_dram, psum, common, col, columns, at, coef):
    with ExitStack() as ctx:
        sb = lambda name, shape: ctx.enter_context(nc.sbuf_tensor("second_" + name, shape, F32))
        gated = sb("gated2", [P, 8, T2])
        sq = sb("sq3", [P, 8, T2])
        stats = sb("stats3", [P, T2])
        out = sb("out_e", [P, KD, T2])
        ring = sb("ring5", [P, 2, KD * 512])
        with stage(nc, "gates_landed mean_ready centered squared var_ready safe root step") as (block, sems):
            gates_landed, mean_ready, centered, squared, var_ready, safe, root, step = sems

            @block.sync
            def _(sp):
                sp.dma_start(gated[:, :, :], gates_dram).then_inc(gates_landed, 16)

            @block.tensor
            def _(pe):
                for c in range(6):
                    if c >= 2:
                        pe.wait_ge(centered, c - 1)
                    for a, b in SPLIT:
                        last = nc.tensor.matmul(wide(psum, c % 2)[:, a:b], common["head_mean"], u[:, c, a:b], start=True, stop=True)
                    last.then_inc(mean_ready, 1)
                for c in range(6):
                    pe.wait_ge(squared, c + 1)
                    if c >= 2:
                        pe.wait_ge(safe, c - 1)
                    for a, b in SPLIT:
                        last = nc.tensor.matmul(wide(psum, 2 + c % 2)[:, a:b], common["head_mean"], sq[:, c, a:b], start=True, stop=True)
                    last.then_inc(var_ready, 1)

            @block.scalar
            def _(act):
                for c in range(6):
                    act.wait_ge(centered, c + 1)
                    nc.scalar.activation(sq[:, c, :], u[:, c, :], ACT.Square).then_inc(squared, 1)
                for c in range(6):
                    act.wait_ge(safe, c + 1)
                    nc.scalar.activation(out[:, c, :], out[:, c, :], ACT.Sqrt).then_inc(root, 1)

            @block.vector
            def _(dve):
                chain = Chain(dve, step)
                for c in range(6):
                    dve.wait_ge(mean_ready, c + 1)
                    nc.vector.tensor_tensor(u[:, c, :], u[:, c, :], wide(psum, c % 2), ALU.subtract).then_inc(centered, 1)
                for c in range(6):
                    dve.wait_ge(var_ready, c + 1)
                    nc.vector.tensor_scalar(out[:, c, :], wide(psum, 2 + c % 2), 64e-5, None, ALU.add).then_inc(safe, 1)
                dve.wait_ge(gates_landed, 16)
                for c in range(6):
                    dve.wait_ge(root, c + 1)
                    chain.then(nc.vector.reciprocal(out[:, c, :], out[:, c, :]))
                    chain.then(nc.vector.tensor_tensor(u[:, c, :], u[:, c, :], out[:, c, :], ALU.mult))
                    chain.then(nc.vector.tensor_scalar(u[:, c, :], u[:, c, :], col("lnx_g", c), col("lnx_b", c), ALU.mult, ALU.add))
                    chain.then(nc.vector.tensor_tensor(gated[:, c, :], u[:, c, :], gated[:, c, :], ALU.mult))
        wo = w["ev_w_out_2"][0].rearrange("(k p) n -> p k n", p=P)
        out_product(nc, wo, gated, out, ring, psum, SPLIT)
        rms_norm(nc, [(out[:, :, 0:CTX], out[:, :, 0:CTX], coef[:, 0, 2, 1, :], None, xc),
                      (out[:, :, CTX:T2], out[:, :, CTX:T2], coef[:, 0, 2, 0, :], None, h)],
                 sq[:, :, :], stats[:, :], psum, common["mean_d"])


def out_product(nc, wo, y, out, ring, psum, split):
    loads = [[(0, (KD, 512), wo[:, :, 512 * i:512 * i + 512])] for i in range(2)]
    n = split[-1][1]
    groups = []
    for m in range(KD):
        made = []
        for a, b in split:
            made += dense(nc, (m % 4) * P, KD, lambda k, a=a, b=b: y[:, k, a:b], out=(0, P, a, b - a))
        groups.append((m // 4, made, "act"))
    product_stage(nc, ring, loads, groups, psum, [(1024 * r + 1024 - n, n) for r in range(4)],
                  lambda _, g, region: nc.scalar.activation(out[:, g, :], region, ACT.Identity))


def odd_layer(nc, w, h, xc, common, psum, coef, lg):
    with ExitStack() as ctx:
        sb = lambda name, shape: ctx.enter_context(nc.sbuf_tensor("second_" + name, shape, F32))
        q = sb("q2", [P, RET_HEADS, L])
        k = sb("k2", [P, RET_HEADS, T2])
        v = sb("v2", [P, 6, D])
        g_ = sb("g2", [P, RET_HEADS, L])
        with ExitStack() as inner:
            sbi = lambda name, shape: inner.enter_context(nc.sbuf_tensor("second_" + name, shape, F32))
            hn = sbi("hn1", [P, KD, T2])
            axial = sbi("axial", [P, 2, L])
            ring = sbi("ring6", [P, 2, KD * 512])
            rope_t = sbi("rope_t2", [P, 2, L])
            with ExitStack() as inner2:
                stats = inner2.enter_context(nc.sbuf_tensor("stats4", [P, T2], F32))
                norm_in(nc, h, xc, hn[:, :, :], k[:, :, :], stats[:, :], psum, common, coef, 1)
            with stage(nc, "axial_landed") as (block, sems):
                @block.sync
                def _(sp):
                    a = CONST_AT["axial_cos"][0]
                    sp.dma_start(axial[:, :, :], w["consts"][:, a:a + 2 * L].rearrange("p (s t) -> p s t", s=2)).then_inc(sems[0], 16)
                    sp.wait_ge(sems[0], 16)
            ow = w["od_w_in_2"][0].rearrange("(k p) n -> p k n", p=P)
            loads = [[(0, (KD, 512), ow[:, :, 512 * i:512 * i + 512])] for i in range(8)]
            groups, what = [], []
            for i in range(8):
                if i in (4, 5):
                    for t in range(6):
                        made = []
                        for kc in range(KD):
                            def make(slot, region, kc=kc, t=t):
                                return nc.tensor.matmul(region[:, 256:768], hn[:, kc, t * P:(t + 1) * P], slot[:, kc * 512:kc * 512 + 512],
                                                        start=kc == 0, stop=kc == KD - 1)
                            made.append(make)
                        groups.append((i, made, "act"))
                        what.append(("v", t, i - 4))
                    continue
                for m in range(4):
                    made = []
                    for a, b in (SPLIT if i in (2, 3) else SPLIT[1:]):
                        made += dense(nc, m * P, KD, lambda kc, a=a, b=b: hn[:, kc, a:b], out=(0, P, a, b - a))
                    groups.append((i, made, "act"))
                    what.append((("q", "k", "v", "g")[i // 2], 4 * (i % 2) + m, 0))

            def evacuate(_, g, region):
                kind, i, j = what[g]
                if kind == "v":
                    return nc.scalar.activation(v[:, i, 512 * j:512 * j + 512], region[:, 256:768], ACT.Identity)
                if kind == "q":
                    return nc.scalar.activation(q[:, i, :], region[:, CTX:], ACT.Identity)
                if kind == "k":
                    return nc.scalar.activation(k[:, i, :], region, ACT.Identity, scale=float(P) ** -0.5)
                return nc.scalar.activation(g_[:, i, :], region[:, CTX:], ACT.Silu)

            roped = [(g, q[:, i, :] if kind == "q" else k[:, i, CTX:]) for g, (kind, i, _) in enumerate(what) if kind in "qk"]
            rope_at = {g: n for n, (g, _) in enumerate(roped)}
            rotated = [psum[:, 6 * 512:7 * 512], psum[:, 7 * 512:8 * 512]]

            def also_pe(pe, g, s):
                turned, roped_out, _ = s.more
                if g - 1 in rope_at:
                    n = rope_at[g - 1]
                    pe.wait_ge(s.by_act, s.evacuated(g - 1, "act"))
                    if n >= 2:
                        pe.wait_ge(roped_out, n - 1)
                    nc.tensor.matmul(rotated[n % 2], common["rot128"], roped[n][1], start=True, stop=True).then_inc(turned, 1)

            def also_dve(dve, s):
                turned, roped_out, step = s.more
                chain = Chain(dve, step)
                for n, (g, x) in enumerate(roped):
                    dve.wait_ge(turned, n + 1)
                    chain.then(nc.vector.tensor_tensor(rope_t[:, n % 2, :], rotated[n % 2], axial[:, 1, :], ALU.mult))
                    chain.then(nc.vector.tensor_tensor(x, x, axial[:, 0, :], ALU.mult))
                    nc.vector.tensor_tensor(x, x, rope_t[:, n % 2, :], ALU.add).then_inc(roped_out, 1)

            product_stage(nc, ring, loads, groups, psum, [(1024 * r + 1024 - T2, T2) for r in range(3)], evacuate,
                          also_pe, also_dve, "turned roped step")

        with ExitStack() as inner:
            sbi = lambda name, shape: inner.enter_context(nc.sbuf_tensor("second_" + name, shape, F32))
            dist = sbi("dist", [P, 24 * P])
            near = sbi("near", [P, 2, 7 * P])
            far = sbi("far", [P, 2, 5 * P])
            far_b = sbi("far_b", [P, 5 * P])
            weighed = sbi("weighed", [P, 6, L])
            y = sbi("y2", [P, RET_HEADS, L])
            sq = sbi("sq4", [P, RET_HEADS, L])
            stats = sbi("stats5", [P, 2, L])
            names = ("dist_landed exponent near_ready far_ready far_b_ready decay_ready scores_ready weighted_ready "
                     "o_ready squared mean_ready safe root step y_ready")
            with stage(nc, names) as (block, sems):
                (dist_landed, exponent, near_ready, far_ready, far_b_ready, decay_ready, scores_ready, weighted_ready,
                 o_ready, squared, mean_ready, safe, root, step, y_ready) = sems
                fwd, bwd = dist[:, 0:7 * P], dist[:, 7 * P:14 * P]
                cf, cb = dist[:, 14 * P:19 * P], dist[:, 19 * P:24 * P]
                order = [0, 1, 2, 3, 4, 5]

                @block.sync
                def _(sp):
                    sp.dma_start(dist[:, :], w["retention"]).then_inc(dist_landed, 16)

                @block.tensor
                def _(pe):
                    for hd in range(RET_HEADS):
                        for c in range(6):
                            n = hd * 6 + c
                            if n >= 2:
                                pe.wait_ge(weighted_ready, n - 1)
                            nc.tensor.matmul(psum[:, (n % 2) * 512:(n % 2) * 512 + L], k[:, hd, c * P:(c + 1) * P], q[:, hd, :],
                                             start=True, stop=True).then_inc(scores_ready, 1)
                        if hd >= 2:
                            pe.wait_ge(y_ready, hd - 1)
                        for c in range(6):
                            pe.wait_ge(weighted_ready, hd * 6 + c + 1)
                            last = nc.tensor.matmul(psum[:, (2 + hd % 2) * 512:(3 + hd % 2) * 512], v[:, c, hd * P:(hd + 1) * P], weighed[:, c, :],
                                                    start=c == 0, stop=c == 5)
                        last.then_inc(o_ready, 1)
                        pe.wait_ge(squared, hd + 1)
                        if hd >= 2:
                            pe.wait_ge(safe, hd - 1)
                        nc.tensor.matmul(psum[:, (4 + hd % 2) * 512:(5 + hd % 2) * 512], common["mean_head128"], sq[:, hd, :],
                                         start=True, stop=True).then_inc(mean_ready, 1)

                @block.scalar
                def _(act):
                    act.wait_ge(dist_landed, 16)
                    def decays(hd):
                        act.wait_ge(exponent, hd + 1)
                        if hd >= 2:
                            act.wait_ge(weighted_ready, 6 * (hd - 1))
                        nc.scalar.activation(near[:, hd % 2, :], near[:, hd % 2, :], ACT.Exp).then_inc(near_ready, 1)
                        if hd >= 1:
                            act.wait_ge(decay_ready, hd)
                        nc.scalar.activation(far[:, hd % 2, :], cf, ACT.Exp, scale=lg[:, hd:hd + 1]).then_inc(far_ready, 1)
                        nc.scalar.activation(far_b[:, :], cb, ACT.Exp, scale=lg[:, 8 + hd:9 + hd]).then_inc(far_b_ready, 1)
                    decays(0)
                    for hd in range(RET_HEADS):
                        if hd + 1 < RET_HEADS:
                            decays(hd + 1)
                        act.wait_ge(o_ready, hd + 1)
                        nc.scalar.activation(sq[:, hd, :], psum[:, (2 + hd % 2) * 512:(3 + hd % 2) * 512], ACT.Square).then_inc(squared, 1)
                        act.wait_ge(safe, hd + 1)
                        nc.scalar.activation(stats[:, hd % 2, :], stats[:, hd % 2, :], ACT.Sqrt).then_inc(root, 1)

                @block.vector
                def _(dve):
                    chain = Chain(dve, step)
                    dve.wait_ge(dist_landed, 16)

                    def exponents(hd):
                        if hd >= 2:
                            dve.wait_ge(weighted_ready, 6 * (hd - 1))
                        chain.then(nc.vector.tensor_scalar(near[:, hd % 2, :], fwd, lg[:, hd:hd + 1], None, ALU.mult))
                        nc.vector.scalar_tensor_tensor(near[:, hd % 2, :], bwd, lg[:, 8 + hd:9 + hd], near[:, hd % 2, :], ALU.mult, ALU.add)\
                            .then_inc(exponent, 1)

                    def far_sum(hd):
                        dve.wait_ge(far_b_ready, hd + 1)
                        nc.vector.tensor_tensor(far[:, hd % 2, :], far[:, hd % 2, :], far_b[:, :], ALU.add).then_inc(decay_ready, 1)

                    exponents(0)
                    far_sum(0)
                    for hd in range(RET_HEADS):
                        if hd + 1 < RET_HEADS:
                            exponents(hd + 1)
                        dve.wait_ge(decay_ready, hd + 1)
                        for c in range(6):
                            n = hd * 6 + c
                            dve.wait_ge(scores_ready, n + 1)
                            if hd:
                                dve.wait_ge(o_ready, hd)
                            if c < 2:
                                factor = far[:, hd % 2, P * (1 - c):P * (1 - c) + L]
                            else:
                                factor = near[:, hd % 2, P * (5 - c):P * (5 - c) + L]
                            nc.vector.tensor_tensor(weighed[:, c, :], psum[:, (n % 2) * 512:(n % 2) * 512 + L], factor, ALU.mult)\
                                .then_inc(weighted_ready, 1)
                        if hd + 1 < RET_HEADS:
                            far_sum(hd + 1)
                        dve.wait_ge(mean_ready, hd + 1)
                        nc.vector.tensor_scalar(stats[:, hd % 2, :], psum[:, (4 + hd % 2) * 512:(5 + hd % 2) * 512], EPS2, None, ALU.add)\
                            .then_inc(safe, 1)
                        dve.wait_ge(root, hd + 1)
                        chain.then(nc.vector.reciprocal(stats[:, hd % 2, :], stats[:, hd % 2, :]))
                        chain.then(nc.vector.tensor_tensor(stats[:, hd % 2, :], stats[:, hd % 2, :], g_[:, hd, :], ALU.mult))
                        nc.vector.tensor_tensor(y[:, hd, :], psum[:, (2 + hd % 2) * 512:(3 + hd % 2) * 512], stats[:, hd % 2, :], ALU.mult)\
                            .then_inc(y_ready, 1)
            with ExitStack() as last:
                ring = last.enter_context(nc.sbuf_tensor("ring7", [P, 1, KD * 512], F32))
                wo = w["od_w_out_2"][0].rearrange("(k p) n -> p k n", p=P)
                out_product(nc, wo, y, sq, ring, psum, ((0, L),))
            rms_norm(nc, [(sq[:, :, :], sq[:, :, :], coef[:, 1, 2, 0, :], None, h)], q[:, :, :], stats[:, 0, :], psum, common["mean_d"])


def second_block(nc, w, out, h, common, psum, columns, rows):
    with ExitStack() as ctx:
        sb = lambda name, shape: ctx.enter_context(nc.sbuf_tensor("second_" + name, shape, F32))
        xc = sb("xc", [P, KD, CTX])[:, :, :]
        coef = sb("coef", [P, DEPTH, 3, 2, KD])
        mod = sb("mod", [P, DEPTH, 24, 2])
        silu_c = sb("silu_c", [P, KD, 2])
        lg = sb("log_gamma", [P, 16])
        lt = sb("log_tmp", [P, 2, 16])
        vectors, at = [], {}
        row = 0
        for name, src in (("c", w["c_2"][0]), ("c_ctx", w["c_ctx_2"]), ("mu", w["ev_mu_2"][0]), ("k_k", w["ev_k_k_2"][0]),
                          ("k_a", w["ev_k_a_2"][0]), ("r_k", w["ev_r_k_2"][0].rearrange("h d -> (h d)")),
                          ("lnx_g", w["ev_lnx_g_2"][0]), ("lnx_b", w["ev_lnx_b_2"][0]),
                          ("w0", w["ev_w0_2"][0].rearrange("a d -> (a d)")), ("a0", w["ev_a0_2"][0].rearrange("a d -> (a d)")),
                          ("ada_b", w["ada_b_2"].rearrange("l d -> (l d)")), ("pre", w["norm_pre_2"].rearrange("l d -> (l d)")),
                          ("post", w["norm_post_2"].rearrange("l d -> (l d)"))):
            view = src.rearrange("(c p) -> c p", p=P)
            at[name] = row
            vectors.append((view, row, 0))
            row += view.shape[0]
        load_columns(nc, rows[:, 0:2, :], columns, psum, common["ident"], vectors)
        with ExitStack() as inner:
            x_tokens = inner.enter_context(nc.sbuf_tensor("ctx_tokens", [P, 2, D], F32))
            transpose_in(nc, x_tokens, xc, psum, common["ident"], w["ctx_2"].rearrange("o t d -> (o t) d"))
        serial(nc, [("act", lambda i=i, n=n: nc.scalar.activation(silu_c[:, :, i], columns[:, at[n]:at[n] + KD], ACT.Silu))
                    for i, n in enumerate(("c", "c_ctx"))])
        with stage(nc, "logits_landed") as (block, sems):
            @block.sync
            def _(sp):
                sp.dma_start(lg[:, :], w["od_decay_logit_2"].rearrange("o a h -> o (a h)").partition_broadcast(P)).then_inc(sems[0], 16)
                sp.wait_ge(sems[0], 16)
        V, S = nc.vector, nc.scalar
        serial(nc, [("dve", lambda: V.scalar_tensor_tensor(lt[:, 0, :], lg[:, :], -1.0, lg[:, :], ALU.mult, ALU.min)),
                    ("act", lambda: S.activation(lt[:, 0, :], lt[:, 0, :], ACT.Exp)),
                    ("dve", lambda: V.tensor_scalar(lt[:, 0, :], lt[:, 0, :], 1.0, None, ALU.add)),
                    ("act", lambda: S.activation(lt[:, 0, :], lt[:, 0, :], ACT.Ln)),
                    ("dve", lambda: V.tensor_scalar(lt[:, 1, :], lg[:, :], 0.0, None, ALU.min)),
                    ("dve", lambda: V.tensor_tensor(lg[:, :], lt[:, 1, :], lt[:, 0, :], ALU.subtract))])
        with ExitStack() as inner:
            ring = inner.enter_context(nc.sbuf_tensor("ring_mod", [P, 4, KD * 512], F32))
            modulation(nc, ring, psum, columns, at, mod, silu_c, w)
        steps = []
        for l in range(DEPTH):
            pre = columns[:, at["pre"] + KD * l:at["pre"] + KD * (l + 1)]
            post = columns[:, at["post"] + KD * l:at["post"] + KD * (l + 1)]
            for who in range(2):
                part = lambda i, l=l, who=who: mod[:, l, KD * i:KD * (i + 1), who]
                steps.append(("dve", lambda l=l, who=who, pre=pre, part=part: V.scalar_tensor_tensor(
                    coef[:, l, 0, who, :], part(1), 1.0, pre, ALU.add, ALU.mult)))
                steps.append(("dve", lambda l=l, who=who, part=part: V.tensor_copy(coef[:, l, 1, who, :], part(0))))
                steps.append(("dve", lambda l=l, who=who, post=post, part=part: V.tensor_tensor(
                    coef[:, l, 2, who, :], part(2), post, ALU.mult)))
        serial(nc, steps)
        even_layer(nc, w, h, xc, common, psum, columns, at, mod, coef)
        odd_layer(nc, w, h, xc, common, psum, coef, lg)
        write_out(nc, h, psum, common["ident"], out)


def write_out(nc, h, psum, ident, out):
    with ExitStack() as ctx:
        y = ctx.enter_context(nc.sbuf_tensor("y_tokens", [P, QB, D], F32))
        with stage(nc, "turned taken stored") as (block, sems):
            turned, taken, stored = sems

            @block.tensor
            def _(pe):
                for b in range(QB):
                    if b >= 4:
                        pe.wait_ge(taken, b - 3)
                    for c in range(KD):
                        last = nc.tensor.transpose(psum[:, b * 1024 + c * P:b * 1024 + (c + 1) * P], h[:, c, b * P:(b + 1) * P], ident)
                    last.then_inc(turned, 1)

            @block.vector
            def _(dve):
                for b in range(QB):
                    dve.wait_ge(turned, b + 1)
                    nc.vector.tensor_copy(y[:, b, :], psum[:, b * 1024:(b + 1) * 1024]).then_inc(taken, 1)

            @block.sync
            def _(sp):
                for b in range(QB):
                    sp.wait_ge(taken, b + 1)
                    sp.dma_start(out[0, b * P:(b + 1) * P, :], y[:, b, :]).then_inc(stored, 16)
                sp.wait_ge(stored, 16 * QB)


COMMON = ("ident", "mean_d", "mean_conv", "rot64", "rot128", "head_sum", "head_mean", "mean_head128",
          "future", "masked", "pool_cut", "inv_freq", "lane")


def program(nc, w, out):
    with ExitStack() as ctx:
        sb = lambda name, shape, dt=F32: ctx.enter_context(nc.sbuf_tensor(name, shape, dt))
        psum = ctx.enter_context(nc.psum_tensor("psum", [P, 8 * 512], F32))
        n_common = CONST_AT["upper"][0]
        table = sb("table", [P, n_common])
        h = sb("h", [P, KD, L])
        columns = sb("columns", [P, 3 * P])
        rows = sb("rows", [P, 3, P])
        common = {n: table[:, CONST_AT[n][0]:sum(CONST_AT[n])] for n in COMMON}
        with stage(nc, "table_landed") as (block, sems):
            @block.sync
            def _(sp):
                sp.dma_start(table[:, :], w["consts"][:, 0:n_common]).then_inc(sems[0], 16)
                sp.wait_ge(sems[0], 16)
        with ExitStack() as inner:
            sbi = lambda name, shape, dt=F32: inner.enter_context(nc.sbuf_tensor(name, shape, dt))
            cos, sin = sbi("cos", [P, L]), sbi("sin", [P, L])
            with ExitStack() as start:
                sbs = lambda name, shape, dt=F32: start.enter_context(nc.sbuf_tensor(name, shape, dt))
                x_tokens = sbs("x_tokens", [P, QB, D])
                transpose_in(nc, x_tokens, h[:, :, :], psum, common["ident"], w["x"].rearrange("o t d -> (o t) d"))
                rope_tables(nc, sbs("pos", [P, L], I32), cos[:, :], sin[:, :], sbs("tmp", [P, 2, L]), w["positions"], common["inv_freq"])
                vec = lambda n: w[n].rearrange("(c p) -> c p", p=P)
                load_columns(nc, rows[:, 0:1, :], columns, psum, common["ident"],
                             [(vec("ln_in_g"), 0, 0), (vec("ln_in_b"), KD, 0)])
                layer_norm(nc, h[:, :, :], sbs("sq0", [P, KD, L])[:, :, :], sbs("stats0", [P, L])[:, :], psum, common["mean_d"],
                           columns[:, 0:KD], columns[:, KD:2 * KD], 1e-5)
            with nc.Fori(0, DEPTH) as l:
                first_block_layer(nc, l, w, h[:, :, :], common, psum, cos[:, :], sin[:, :], columns, rows)
        second_block(nc, w, out, h[:, :, :], common, psum, columns, rows)


def kernel(**inputs):
    import concourse.bacc as bacc
    from concourse.bass_utils import run_bass_kernel_spmd

    nc = bacc.Bacc("TRN2", target_bir_lowering=False, num_devices=1)
    arrays = {name: np.ascontiguousarray(a) for name, a in inputs.items()}
    dft_ctx, dft_seq = dft_tables()
    arrays.update(consts=CONSTS, dft_ctx=dft_ctx, dft_seq=dft_seq, retention=retention_tables())
    w = {name: nc.dram_tensor(f"in_{name}", a.shape, mybir.dt.from_np(a.dtype), kind="ExternalInput").ap()
         for name, a in arrays.items()}
    out = nc.dram_tensor("out", (1, L, D), F32, kind="ExternalOutput").ap()
    program(nc, w, out)
    r = run_bass_kernel_spmd(nc, [{f"in_{name}": a for name, a in arrays.items()}], core_ids=[0])
    return np.asarray(r.results[0]["out"])
```

```python
import math
from contextlib import ExitStack, contextmanager

import numpy as np

import concourse.bass as bass
from concourse import mybir

F32 = mybir.dt.float32
F32R = mybir.dt.float32r
I32 = mybir.dt.int32
ALU = mybir.AluOpType
ACT = mybir.ActivationFunctionType
AX_X = mybir.AxisListType.X

P = 128
D = 1024
KD = D // P
L = 512
DEPTH = 2
POOL_WINDOWS = (2, 4, 8, 16)
POOL_TAIL = max(POOL_WINDOWS)
D_CONV = 256
TAPS = 31
HEADS, HEAD_DIM = 8, 64
TOPK = min(256, L // 4)
QB = L // P
D_FF = 2816
KF = D_FF // P
UF = 2 * KF
ALPHA = (2 * DEPTH) ** 0.25
CTX = 256
T2 = CTX + L
GRID_W = 64
RW_HEADS = 12
RW_PAIRS = RW_HEADS // 2
RWKV_W = RW_HEADS * 64
N_SHIFT = 3 * RWKV_W + 256
CH = 64
NCH = T2 // CH
RET_HEADS = 8
DECAY = math.exp(-0.5)

C_POOL, C_CONV, C_Q, C_K, C_V, C_QI, C_KI, C_WI, C_GATE = 0, 256, 768, 1280, 1408, 1536, 2048, 2112, 2120

PICKED = -3.0e38
FUTURE = -2.0e38
MASKED = -1.0e30
ROUND = 12582912.0
TWO_PI_1 = 6.28125
TWO_PI_2 = float(np.float32(np.round((2 * math.pi - TWO_PI_1) * 2**22) / 2**22))
TWO_PI_3 = 2 * math.pi - TWO_PI_1 - TWO_PI_2
PI_IN = 3.1415925


def const_table():
    eye = np.eye(P)
    p = np.arange(P)
    t = {}
    t["ident"] = eye
    t["mean_d"] = np.full((P, P), 1.0 / D)
    t["mean_conv"] = np.full((P, P), 1.0 / D_CONV)
    rot64 = np.zeros((P, P))
    for m in range(P):
        if m % 64 < 32:
            rot64[m + 32, m] = -1
        else:
            rot64[m - 32, m] = 1
    t["rot64"] = rot64
    rot128 = np.zeros((P, P))
    for m in range(P):
        if m < 64:
            rot128[m + 64, m] = -1
        else:
            rot128[m - 64, m] = 1
    t["rot128"] = rot128
    same = (p[:, None] // 64 == p[None, :] // 64).astype(float)
    t["head_sum"] = same
    t["head_mean"] = same / 64
    t["mean_head128"] = np.full((P, P), 1.0 / P)
    t["future"] = np.where(p[None, :] <= p[:, None], 0.0, FUTURE)
    t["masked"] = np.where(p[None, :] <= p[:, None], 0.0, MASKED)
    cut = np.zeros((P, 2, POOL_TAIL))
    for ch in range(2):
        for half in range(2):
            win = POOL_WINDOWS[2 * ch + half]
            cut[64 * half:64 * half + 64, ch, :] = 1.0 / np.minimum(np.arange(POOL_TAIL) + 1, win)
    t["pool_cut"] = cut.reshape(P, -1)
    t["inv_freq"] = (np.float32(10000.0) ** (-(p % 32).astype(np.float32) / np.float32(32)))[:, None]
    cls = np.zeros((P, 6))
    for j in range(4):
        cls[:, j] = p % 4 == j
    cls[:, 4], cls[:, 5] = p % 2 == 0, p % 2 == 1
    t["lane"] = cls
    t["pick_pair"] = np.zeros((P, 2 * RW_HEADS - 2))
    t["pick_pair"][:64, RW_HEADS - 2] = t["pick_pair"][64:, RW_HEADS - 1] = 1.0 / 64
    t["pick_head"] = np.zeros((P, 2 * RET_HEADS - 1))
    t["pick_head"][:, RET_HEADS - 1] = 1.0 / P
    s, q = p[:, None] % 64, p[None, :] % 64
    t["upper"] = same * (s < q)
    t["lower"] = same * (s > q)
    t["upper_eq"] = same * (s <= q)
    t["lower_eq"] = same * (s >= q)
    for b in (1, 2, 4, 8, 16, 32):
        off = same * (s // (2 * b) == q // (2 * b)) * (s // b != q // b)
        t[f"up{b}"] = off * (s < q)
        t[f"lo{b}"] = off * (s > q)
    k64 = np.arange(64)
    ang = 2 * np.pi * np.outer(k64, k64) / 64
    bd = lambda m: np.kron(np.eye(2), m)
    t["dft_ch"] = np.concatenate([bd(np.cos(ang)), bd(np.sin(ang))], 1) / 8.0
    rc = np.stack([np.arange(L) // GRID_W, np.arange(L) % GRID_W], -1).astype(np.float32)
    inv = (np.float32(10000.0) ** (-np.arange(0, 64, 2, dtype=np.float32) / np.float32(64)))
    axial = (rc[:, :, None] * inv).reshape(L, 64)
    axial = np.concatenate([axial, axial], 1).T
    t["axial_cos"], t["axial_sin"] = np.cos(axial), np.sin(axial)
    widths, at = {}, 0
    for name, a in t.items():
        widths[name] = (at, a.shape[1])
        at += a.shape[1]
    return np.concatenate([a for a in t.values()], 1).astype(np.float32), widths


def dft_tables():
    out = []
    for n in (CTX, L):
        a = 2 * np.pi * (np.outer(np.arange(n), np.arange(n)) % n) / n
        out.append(np.stack([np.cos(a), -np.sin(a)]).astype(np.float32) / np.float32(math.sqrt(n)))
    return out


def retention_tables():
    p = np.arange(P)[:, None]
    d = np.arange(7 * P)[None, :] - 3 * P - p
    fwd, bwd = np.maximum(d, 0), np.maximum(-d, 0)
    x = np.arange(5 * P)[None, :]
    cf = x + P - p
    cb = 2 * L + 0 * x - x + p - L + P
    return np.concatenate([fwd, bwd, cf, cb], 1).astype(np.float32)


def head_rows():
    pairs, heads = np.zeros((RW_HEADS, RW_PAIRS, 2, 64)), np.zeros((RW_HEADS, RET_HEADS, P))
    for h in range(RW_HEADS):
        pairs[h, h // 2, h % 2] = 1
    for h in range(RET_HEADS):
        heads[h, h] = 1
    return np.concatenate([pairs.reshape(RW_HEADS, -1), heads.reshape(RW_HEADS, -1)], 1).astype(np.float32)


CONSTS, CONST_AT = const_table()


class Used:
    sems, held, turn = [], None, 0


def clear(pool, sems):
    for s in sems:
        pool.sem_clear(s)


@contextmanager
def stage(nc, names):
    ctx = ExitStack()
    Used.turn = 1 - Used.turn
    sems = [ctx.enter_context(nc.semaphore(f"{n}_{Used.turn}")) for n in names.split()]
    with nc.Block() as block:
        if Used.sems:
            @block.gpsimd
            def _(pool):
                clear(pool, Used.sems)
        yield block, sems
    if Used.held:
        Used.held.close()
    Used.sems, Used.held = sems, ctx


def clear_last(nc):
    with nc.Block() as block:
        @block.gpsimd
        def _(pool):
            clear(pool, Used.sems)
    Used.held.close()
    Used.sems, Used.held = [], None


class Chain:

    def __init__(self, engine, sem):
        self.engine, self.sem, self.count = engine, sem, 0

    def then(self, instruction):
        self.count += 1
        instruction.then_inc(self.sem, 1)
        self.engine.wait_ge(self.sem, self.count)


def cols(ap, at, n=1):
    return ap[:, at:at + n]


def layer(ap, l):
    letters = " ".join("abcd"[:len(ap.shape) - 1])
    return ap[bass.ds(l, 1)].rearrange(f"o {letters} -> (o a) {letters[2:]}" if len(ap.shape) > 2
                                       else "o a -> (o a)")


def load_columns(nc, rows, columns, psum, ident, vectors):
    n_tiles = rows.shape[1]
    pieces = []
    for view, row, at in vectors:
        done = 0
        while done < view.shape[0]:
            r = (row + done) % P
            k = min(view.shape[0] - done, P - r)
            pieces.append((view[done:done + k, :], (row + done) // P, r, at))
            done += k
    transfers = len(pieces)

    def transfer(engine, start):
        engine.wait_ge(rows_zeroed, 1)
        for view, tile, r, at in pieces[start::2]:
            k, width = view.shape
            engine.dma_start(rows[r:r + k, tile, at:at + width], view).then_inc(rows_landed, 16)

    with stage(nc, "rows_zeroed rows_landed transposed") as (block, sems):
        rows_zeroed, rows_landed, transposed = sems

        @block.vector
        def _(dve):
            nc.vector.memset(rows[:, :, :], 0.0).then_inc(rows_zeroed, 1)
            for i in range(n_tiles):
                dve.wait_ge(transposed, i + 1)
                nc.vector.tensor_copy(columns[:, i * P:(i + 1) * P], psum[:, i * 512:i * 512 + P])

        @block.sync
        def _(sp):
            transfer(sp, 0)

        @block.scalar
        def _(act):
            transfer(act, 1)

        @block.tensor
        def _(pe):
            pe.wait_ge(rows_landed, 16 * transfers)
            for i in range(n_tiles):
                nc.tensor.transpose(psum[:, i * 512:i * 512 + P], rows[:, i, :], ident)\
                    .then_inc(transposed, 1)


def layer_norm(nc, x, sq, stats, psum, mean_w, gain, bias, eps, silu=False, parts=None):
    K, T = x.shape[1], x.shape[2]
    mean, var = psum[:, 0:T], psum[:, 512:512 + T]
    with stage(nc, "mean_ready centered squared var_ready var_safe std_ready rstd_ready scaled result_ready rounded") as (block, sems):
        mean_ready, centered, squared, var_ready, var_safe, std_ready, rstd_ready, scaled, result_ready, rounded = sems

        @block.tensor
        def _(pe):
            for c in range(K):
                last = nc.tensor.matmul(mean, mean_w, x[:, c, :], start=c == 0, stop=c == K - 1)
            last.then_inc(mean_ready, 1)
            for c in range(K):
                pe.wait_ge(squared, c + 1)
                last = nc.tensor.matmul(var, mean_w, sq[:, c, :], start=c == 0, stop=c == K - 1)
            last.then_inc(var_ready, 1)

        @block.vector
        def _(dve):
            dve.wait_ge(mean_ready, 1)
            for c in range(K):
                nc.vector.tensor_tensor(x[:, c, :], x[:, c, :], mean, ALU.subtract)\
                    .then_inc(centered, 1)
            dve.wait_ge(var_ready, 1)
            nc.vector.tensor_scalar(stats, var, eps, None, ALU.add).then_inc(var_safe, 1)
            dve.wait_ge(std_ready, 1)
            nc.vector.reciprocal(stats, stats).then_inc(rstd_ready, 1)
            dve.wait_ge(rstd_ready, 1)
            for c in range(K):
                nc.vector.tensor_tensor(x[:, c, :], x[:, c, :], stats, ALU.mult).then_inc(scaled, 1)
            if parts:
                for c in range(K):
                    dve.wait_ge(rounded, c + 1)
                    nc.vector.tensor_tensor(parts[1][:, c, :], x[:, c, :], parts[0][:, c, :].bitcast(F32), ALU.subtract)

        @block.scalar
        def _(act):
            for c in range(K):
                act.wait_ge(centered, c + 1)
                nc.scalar.activation(sq[:, c, :], x[:, c, :], ACT.Square).then_inc(squared, 1)
            act.wait_ge(var_safe, 1)
            nc.scalar.activation(stats, stats, ACT.Sqrt).then_inc(std_ready, 1)
            for c in range(K):
                act.wait_ge(scaled, c + 1)
                nc.scalar.activation(x[:, c, :], x[:, c, :], ACT.Silu if silu else ACT.Identity,
                                     bias=bias[:, c:c + 1], scale=gain[:, c:c + 1]).then_inc(result_ready, 1)
                if parts and c:
                    act.wait_ge(result_ready, c)
                    nc.scalar.activation(parts[0][:, c - 1, :], x[:, c - 1, :], ACT.Identity).then_inc(rounded, 1)
            if parts:
                act.wait_ge(result_ready, K)
                nc.scalar.activation(parts[0][:, K - 1, :], x[:, K - 1, :], ACT.Identity).then_inc(rounded, 1)


class Ring:

    def __init__(self, nc, ctx, name, landing, width, split=2, lent=()):
        sb = lambda what, n, dt: ctx.enter_context(nc.sbuf_tensor(f"{name}_{what}", [P, n, width], dt))
        self.landing, self.split = landing, split
        self.raw = sb("raw", landing, F32)
        self.hi, self.lo = [[x] for x in lent] or ([], [])
        own = split - len(self.hi)
        if own:
            hi, lo = sb("hi", own, F32R), sb("lo", own, F32R)
            self.hi += [hi[:, i, :] for i in range(own)]
            self.lo += [lo[:, i, :] for i in range(own)]


class Products:

    def __init__(self, nc, sems, ring, loads, groups, psum, regions, raw_tiles=(), both=()):
        self.nc, self.ring, self.loads, self.groups = nc, ring, loads, groups
        n = ring.landing
        self.landed = sems[:n]
        self.hi_done, self.first_lo_done, self.lo_done, self.ready, self.by_act, self.by_dve = sems[n:n + 6]
        self.more = sems[n + 6:]
        self.psum, self.regions = psum, regions
        count, self.lands = [0] * n, []
        for i, parts in enumerate(loads):
            count[i % n] += 16 * len(parts)
            self.lands.append(count[i % n])
        self.width = [sum(math.prod(view.shape[1:]) for _, view in parts) for parts in loads]
        self.last_of = {g[0]: i for i, g in enumerate(groups)}
        self.split_tiles = [t for t in range(len(loads)) if t not in raw_tiles]
        self.split_at = {t: i for i, t in enumerate(self.split_tiles)}
        self.whole = set(raw_tiles) | set(both)
        self.first = min(ring.split, len(self.split_tiles))

    @staticmethod
    def names(ring):
        return " ".join(f"weights_landed{i}" for i in range(ring.landing)) + \
            " hi_done first_lo_done lo_done products_ready evacuated_act evacuated_dve "

    def region(self, g):
        at, width = self.regions[g % len(self.regions)]
        return self.psum[:, at:at + width]

    def evacuated(self, g, who):
        return sum(x[2] == who for x in self.groups[:g + 1])

    def load(self, sp):
        n = self.ring.landing
        for i, parts in enumerate(self.loads):
            if i >= n:
                if i - n in self.split_at:
                    self.wait_lo(sp, self.split_at[i - n])
                if i - n in self.whole:
                    sp.wait_ge(self.ready, self.last_of[i - n] + 1)
            for place, view in parts:
                sp.dma_start(place(self.ring.raw[:, i % n, :]), view).then_inc(self.landed[i % n], 16)

    def split_hi(self, act, i):
        if i >= len(self.split_tiles):
            return
        t, n = self.split_tiles[i], self.ring.split
        act.wait_ge(self.landed[t % self.ring.landing], self.lands[t])
        if i >= n:
            act.wait_ge(self.ready, self.last_of[self.split_tiles[i - n]] + 1)
        width = self.width[t]
        self.nc.scalar.activation(self.ring.hi[i % n][:, 0:width], self.ring.raw[:, t % self.ring.landing, 0:width], ACT.Identity)\
            .then_inc(self.hi_done, 1)

    def split_before(self, act, g):
        tile = self.groups[g][0]
        if g == 0:
            for i in range(self.ring.split):
                self.split_hi(act, i)
        elif self.groups[g - 1][0] != tile and tile in self.split_at and self.split_at[tile]:
            self.split_hi(act, self.split_at[tile] + self.ring.split - 1)

    def wait_lo(self, engine, i):
        if i < self.first:
            engine.wait_ge(self.first_lo_done, i + 1)
        else:
            engine.wait_ge(self.lo_done, i - self.first + 1)

    def make_lo(self, engine, ops, i):
        t = self.split_tiles[i]
        n, width = self.ring.split, self.width[t]
        engine.wait_ge(self.hi_done, i + 1)
        return ops.tensor_tensor(self.ring.lo[i % n][:, 0:width], self.ring.raw[:, t % self.ring.landing, 0:width],
                                 self.ring.hi[i % n][:, 0:width].bitcast(F32), ALU.subtract)

    def split_first(self, dve):
        for i in range(self.first):
            self.make_lo(dve, self.nc.vector, i).then_inc(self.first_lo_done, 1)

    def split_lo(self, pool):
        for i in range(self.first, len(self.split_tiles)):
            self.make_lo(pool, self.nc.gpsimd, i).then_inc(self.lo_done, 1)

    def multiply(self, pe, g):
        tile, products, who = self.groups[g]
        if g == 0 or self.groups[g - 1][0] != tile:
            if tile in self.whole:
                pe.wait_ge(self.landed[tile % self.ring.landing], self.lands[tile])
            if tile in self.split_at:
                self.wait_lo(pe, self.split_at[tile])
        prior = g - len(self.regions)
        if prior >= 0:
            before = self.groups[prior][2]
            pe.wait_ge(self.by_act if before == "act" else self.by_dve, self.evacuated(prior, before))
        raw = self.ring.raw[:, tile % self.ring.landing, :]
        hi = lo = None
        if tile in self.split_at:
            i = self.split_at[tile] % self.ring.split
            hi, lo = self.ring.hi[i], self.ring.lo[i]
        for issue in products:
            last = issue(raw, hi, lo, self.region(g))
        last.then_inc(self.ready, 1)


def block_of(at, k, n, left=0, width=None):
    def place(slot):
        view = slot[:, at:at + k * n].rearrange("p (k n) -> p k n", k=k)
        return view if width is None else view[:, :, left:left + width]
    return place


def ffn_up(nc, ring, loads, groups, psum, u, cv, hidden, col):
    with stage(nc, Products.names(ring) + "step convolved activated multiplied rounded") as (block, sems):
        s = Products(nc, sems, ring, loads, groups, psum, [(512 * b, 512) for b in range(8)])
        step, convolved, activated, multiplied, rounded = s.more
        chunks = len(groups) // 2

        @block.sync
        def _(sp):
            s.load(sp)

        @block.gpsimd
        def _(pool):
            s.split_lo(pool)

        @block.tensor
        def _(pe):
            for g in range(len(groups)):
                s.multiply(pe, g)

        @block.scalar
        def _(act):
            def silu(i):
                act.wait_ge(convolved, 2 * i + 1)
                nc.scalar.activation(cv[:, 2 * i % 4, :], cv[:, 2 * i % 4, :], ACT.Silu).then_inc(activated, 1)

            def round_(i):
                act.wait_ge(multiplied, i + 1)
                nc.scalar.activation(hidden[0][:, i, :], cv[:, 2 * i % 4, :], ACT.Identity).then_inc(rounded, 1)

            for g in range(len(groups)):
                s.split_before(act, g)
                if g % 2 == 0 and g >= 4:
                    round_(g // 2 - 2)
                act.wait_ge(s.ready, g + 1)
                if g >= 2:
                    act.wait_ge(convolved, g - 1)
                nc.scalar.activation(u[:, g % 2, 2:], s.region(g), ACT.Identity).then_inc(s.by_act, 1)
                if g % 2 == 1 and g >= 3:
                    silu(g // 2 - 1)
            round_(chunks - 2)
            silu(chunks - 1)
            round_(chunks - 1)

        @block.vector
        def _(dve):
            s.split_first(dve)
            chain = Chain(dve, step)

            def product(i):
                dve.wait_ge(activated, i + 1)
                nc.vector.tensor_tensor(cv[:, 2 * i % 4, :], cv[:, 2 * i % 4, :], cv[:, (2 * i + 1) % 4, :], ALU.mult)\
                    .then_inc(multiplied, 1)

            def rest(i):
                dve.wait_ge(rounded, i + 1)
                chain.then(nc.vector.tensor_tensor(hidden[1][:, i, :], cv[:, 2 * i % 4, :], hidden[0][:, i, :].bitcast(F32), ALU.subtract))

            for g in range(len(groups)):
                chunk = g // 2 + KF * (g % 2)
                x, y = u[:, g % 2, :], cv[:, g % 4, :]
                if g % 2 == 0 and g >= 4:
                    rest(g // 2 - 2)
                dve.wait_ge(s.by_act, g + 1)
                chain.then(nc.vector.tensor_scalar(y, x[:, 2:], col("ffn_w", 2 * UF + chunk), col("ffn_dw_b", chunk), ALU.mult, ALU.add))
                chain.then(nc.vector.scalar_tensor_tensor(y, x[:, 1:L + 1], col("ffn_w", UF + chunk), y, ALU.mult, ALU.add))
                nc.vector.scalar_tensor_tensor(y, x[:, 0:L], col("ffn_w", chunk), y, ALU.mult, ALU.add).then_inc(convolved, 1)
                if g % 2 == 1 and g >= 3:
                    dve.wait_ge(convolved, g - 1)
                    product(g // 2 - 1)
            rest(chunks - 2)
            dve.wait_ge(convolved, len(groups))
            product(chunks - 1)
            rest(chunks - 1)


GATES_WHILE_PICKING = (0, 3, 4, 4)
GATES_AFTER_HEAD = ((), (5,), (5,), (5,))


def attention(nc, q, kd, qi, ki, v, wi, o, psum, common, ring, loads, groups, evacuate):
    ident = common["ident"]
    with ExitStack() as ctx:
        sb = lambda name, shape: ctx.enter_context(nc.sbuf_tensor(name, shape, F32))
        relu = sb("relu", [P, 2, L])
        score = sb("score", [P, L])
        top8 = sb("top8", [P, 8])
        left_out = sb("left_out", [P, L])
        prob = sb("prob", [P, HEADS, L])
        prob_t = sb("prob_t", [P, 2, QB, 4, P])
        stat = sb("stat", [P, 3, HEADS])
        names = ("logits_ready logits_taken weighted step scores_ready scores_taken max_ready "
                 "exp_ready normed turned turned_taken pv_ready o_taken")
        places, g = {}, 0
        for b in range(QB):
            for place, count in [("pick", GATES_WHILE_PICKING[b])] + [(h, 1) for h in GATES_AFTER_HEAD[b]]:
                places[b, place] = range(g, g + count)
                g += count
        assert g == len(groups)
        with stage(nc, Products.names(ring) + names) as (block, sems):
            s = Products(nc, sems, ring, loads, groups, psum, [(2 * 512, 512), (3 * 512, 512)])
            (logits_ready, logits_taken, weighted, step, scores_ready, scores_taken, max_ready,
             exp_ready, normed, turned, turned_taken, pv_ready, o_taken) = s.more
            bank = lambda b, n=512: psum[:, b * 512:b * 512 + n]

            @block.sync
            def _(sp):
                s.load(sp)

            @block.gpsimd
            def _(pool):
                s.split_lo(pool)

            @block.tensor
            def _(pe):
                def logits(b, h, idx):
                    ps = slice(64 * (h % 2), 64 * (h % 2) + 64)
                    if h < 2:
                        pe.wait_ge(scores_taken, (b - 1) * HEADS + HEADS - 1 + h)
                    else:
                        pe.wait_ge(logits_taken, idx - 1)
                    nc.tensor.matmul(bank(idx % 2, (b + 1) * P), qi[ps, h // 2, b * P:(b + 1) * P],
                                     ki[ps, 0:(b + 1) * P], start=True, stop=True).then_inc(logits_ready, 1)

                def scores(b, h):
                    n = b * HEADS + h
                    ps = slice(64 * (h % 2), 64 * (h % 2) + 64)
                    if h >= 2:
                        pe.wait_ge(scores_taken, n - 1)
                    elif b:
                        pe.wait_ge(logits_taken, (b - 1) * HEADS + HEADS - 1 + h)
                    nc.tensor.matmul(bank(n % 2, (b + 1) * P), q[ps, h // 2, b * P:(b + 1) * P],
                                     kd[ps, h // 4, 0:(b + 1) * P], start=True, stop=True).then_inc(scores_ready, 1)

                def turn(b, h):
                    n = b * HEADS + h
                    pe.wait_ge(normed, n + 1)
                    if n >= 2:
                        pe.wait_ge(turned_taken, n - 1)
                    for s in range(b + 1):
                        last = nc.tensor.transpose(psum[:, (4 + n % 2) * 512 + s * P:(4 + n % 2) * 512 + (s + 1) * P],
                                                   prob[:, h, s * P:(s + 1) * P], ident)
                    last.then_inc(turned, 1)

                def values(b, n):
                    done = 2 * b + n
                    pe.wait_ge(turned_taken, b * HEADS + 4 * n + 4)
                    if done >= 2:
                        pe.wait_ge(o_taken, done - 1)
                    for e in range(2):
                        for s in range(b + 1):
                            last = nc.tensor.matmul(psum[64 * e:64 * e + 64, (6 + done % 2) * 512:(6 + done % 2) * 512 + 2 * P],
                                                    v[:, s, 64 * n:64 * n + 64], prob_t[:, n, s, e::2, :],
                                                    start=s == 0, stop=s == b)
                    last.then_inc(pv_ready, 1)

                idx = 0
                for b in range(QB):
                    if b:
                        for h in range(HEADS):
                            logits(b, h, idx)
                            idx += 1
                    for g in places[b, "pick"]:
                        s.multiply(pe, g)
                    for h in range(HEADS + 3):
                        if h < HEADS:
                            scores(b, h)
                        if h >= 3:
                            turn(b, h - 3)
                            if (h - 3) % 4 == 3:
                                values(b, (h - 3) // 4)
                        for g in places.get((b, h), ()):
                            s.multiply(pe, g)

            @block.scalar
            def _(act):
                idx = 0
                taken = 0

                def take_groups(until):
                    nonlocal taken
                    while taken < until:
                        if taken:
                            s.split_before(act, taken)
                        act.wait_ge(s.ready, taken + 1)
                        evacuate(taken, s.region(taken)).then_inc(s.by_act, 1)
                        taken += 1

                for i in range(ring.split):
                    s.split_hi(act, i)
                for b in range(QB):
                    if b:
                        for h in range(HEADS):
                            act.wait_ge(logits_ready, idx + 1)
                            if idx >= 2:
                                act.wait_ge(weighted, idx - 1)
                            nc.scalar.activation(relu[:, idx % 2, 0:(b + 1) * P], bank(idx % 2, (b + 1) * P), ACT.Relu,
                                                 scale=(HEAD_DIM * HEADS) ** -0.5).then_inc(logits_taken, 1)
                            idx += 1
                    if b:
                        take_groups(places[b, "pick"].stop)

                    def exp(h):
                        act.wait_ge(max_ready, b * HEADS + h + 1)
                        x = prob[:, h, 0:(b + 1) * P]
                        nc.scalar.activation(x, x, ACT.Exp, bias=stat[:, 0, h:h + 1], accum_out=stat[:, 1, h:h + 1])\
                            .then_inc(exp_ready, 1)

                    def take(h):
                        n = b * HEADS + h
                        act.wait_ge(turned, n + 1)
                        if b and h % 4 == 0:
                            act.wait_ge(pv_ready, 2 * (b - 1) + h // 4 + 1)
                        nc.scalar.activation(prob_t[:, h // 4, 0:b + 1, h % 4, :],
                                             bank(4 + n % 2, (b + 1) * P).rearrange("p (s n) -> p s n", n=P), ACT.Identity)\
                            .then_inc(turned_taken, 1)

                    for h in range(HEADS + 3):
                        if h < HEADS:
                            exp(h)
                        if h >= 3:
                            take(h - 3)
                        if places.get((b, h - 1)):
                            take_groups(places[b, h - 1].stop)

            @block.vector
            def _(dve):
                s.split_first(dve)
                chain = Chain(dve, step)
                idx = 0
                for b in range(QB):
                    S = (b + 1) * P
                    if b:
                        for h in range(HEADS):
                            dve.wait_ge(logits_taken, idx + 1)
                            if h == 0:
                                made = nc.vector.tensor_scalar(score[:, 0:S], relu[:, idx % 2, 0:S], wi[:, b, 0:1], None, ALU.mult)
                            else:
                                made = nc.vector.scalar_tensor_tensor(score[:, 0:S], relu[:, idx % 2, 0:S], wi[:, b, h:h + 1],
                                                                      score[:, 0:S], ALU.mult, ALU.add)
                            made.then_inc(weighted, 1)
                            idx += 1
                            dve.wait_ge(weighted, idx)
                        diag = score[:, b * P:S]
                        chain.then(nc.vector.tensor_tensor(diag, diag, common["future"], ALU.add))
                        for _ in range(TOPK // 8):
                            chain.then(nc.vector.max(top8[:, :], score[:, 0:S]))
                            chain.then(nc.vector.match_replace(score[:, 0:S], top8[:, :], score[:, 0:S], PICKED))
                        chain.then(nc.vector.tensor_scalar(left_out[:, 0:S], score[:, 0:S], -2.5e38, MASKED, ALU.is_gt, ALU.mult))
                    else:
                        chain.then(nc.vector.tensor_copy(left_out[:, 0:P], common["masked"]))

                    def peak(h):
                        n = b * HEADS + h
                        dve.wait_ge(scores_ready, n + 1)
                        if b:
                            dve.wait_ge(turned, n - HEADS + 1)
                        nc.vector.scalar_tensor_tensor(prob[:, h, 0:S], bank(n % 2, S), HEAD_DIM ** -0.5, left_out[:, 0:S],
                                                       ALU.mult, ALU.add).then_inc(scores_taken, 1)
                        dve.wait_ge(scores_taken, n + 1)
                        nc.vector.tensor_reduce(stat[:, 0, h:h + 1], prob[:, h, 0:S], AX_X, ALU.max, negate=True)\
                            .then_inc(max_ready, 1)

                    def norm(h):
                        dve.wait_ge(exp_ready, b * HEADS + h + 1)
                        chain.then(nc.vector.reciprocal(stat[:, 2, h:h + 1], stat[:, 1, h:h + 1]))
                        nc.vector.tensor_scalar(prob[:, h, 0:S], prob[:, h, 0:S], stat[:, 2, h:h + 1], None, ALU.mult)\
                            .then_inc(normed, 1)

                    for h in range(HEADS + 2):
                        if h < HEADS:
                            peak(h)
                        if h >= 2:
                            norm(h - 2)
                    for n in range(2):
                        done = 2 * b + n
                        dve.wait_ge(pv_ready, done + 1)
                        nc.vector.tensor_copy(o[:, 2 * n:2 * n + 2, b * P:S],
                                              bank(6 + done % 2, 2 * P).rearrange("p (c n) -> p c n", c=2)).then_inc(o_taken, 1)


def product_stage(nc, ring, loads, groups, psum, regions, evacuate, also_pe=None, also_dve=None,
                  also_act=None, more="", raw_tiles=(), both=()):
    with stage(nc, Products.names(ring) + more) as (block, sems):
        s = Products(nc, sems, ring, loads, groups, psum, regions, raw_tiles, both)

        @block.sync
        def _(sp):
            s.load(sp)

        @block.gpsimd
        def _(pool):
            s.split_lo(pool)

        @block.tensor
        def _(pe):
            for g in range(len(groups)):
                s.multiply(pe, g)
                if also_pe:
                    also_pe(pe, g, s)

        @block.scalar
        def _(act):
            for g, group in enumerate(groups):
                s.split_before(act, g)
                if group[2] == "act":
                    act.wait_ge(s.ready, g + 1)
                    evacuate(g, s.region(g)).then_inc(s.by_act, 1)
                if also_act:
                    also_act(act, g, s)

        @block.vector
        def _(dve):
            s.split_first(dve)
            if also_dve:
                also_dve(dve, s)
            for g, group in enumerate(groups):
                if evacuate and group[2] == "dve":
                    dve.wait_ge(s.ready, g + 1)
                    evacuate(g, s.region(g)).then_inc(s.by_dve, 1)


def dense(nc, offset, n_k, moving, step=256, columns=None, start=True, stop=True):
    def product(k, i, which, part):
        def issue(raw, hi, lo, region):
            at = offset + k * step
            to = region[:, columns[0]:columns[1]] if columns else region
            return nc.tensor.matmul(to, (hi, lo)[which][:, at:at + P], moving(k)[part],
                                    start=start and k == 0 and i == 0, stop=stop and k == n_k - 1 and i == 2)
        return issue
    return [product(k, i, which, part) for k in range(n_k) for i, (which, part) in enumerate(((0, 0), (0, 1), (1, 0)))]


def moving_of(parts):
    return lambda k: (parts[0][:, k, :], parts[1][:, k, :])


def split_chunks(nc, chunks, parts):
    with stage(nc, "rounded") as (block, sems):
        (rounded,) = sems

        @block.scalar
        def _(act):
            for c, x in enumerate(chunks):
                nc.scalar.activation(parts[0][:, c, :], x, ACT.Identity).then_inc(rounded, 1)

        @block.vector
        def _(dve):
            for c, x in enumerate(chunks):
                dve.wait_ge(rounded, c + 1)
                nc.vector.tensor_tensor(parts[1][:, c, :], x, parts[0][:, c, :].bitcast(F32), ALU.subtract)


def transpose_in(nc, x_tokens, h, psum, ident, x_dram):
    with stage(nc, "x_landed turned taken") as (block, sems):
        x_landed, turned, taken = sems

        @block.sync
        def _(sp):
            sp.dma_start(x_tokens[:, :, :], x_dram.rearrange("(b p) d -> p b d", p=P))\
                .then_inc(x_landed, 16)

        @block.tensor
        def _(pe):
            pe.wait_ge(x_landed, 16)
            for c in range(KD):
                if c >= 4:
                    pe.wait_ge(taken, c - 3)
                for b in range(x_tokens.shape[1]):
                    last = nc.tensor.transpose(psum[:, (c % 4) * 512 + b * P:(c % 4) * 512 + (b + 1) * P],
                                               x_tokens[:, b, c * P:(c + 1) * P], ident)
                last.then_inc(turned, 1)

        @block.vector
        def _(dve):
            width = x_tokens.shape[1] * P
            for c in range(KD):
                dve.wait_ge(turned, c + 1)
                nc.vector.tensor_copy(h[:, c, :], psum[:, (c % 4) * 512:(c % 4) * 512 + width])\
                    .then_inc(taken, 1)


def rope_tables(nc, pos_i, cos, sin, tmp, positions, inv_freq):
    with stage(nc, "positions_landed step reduced cos_arg") as (block, sems):
        positions_landed, step, reduced, cos_arg = sems
        a, q = tmp[:, 0, :], tmp[:, 1, :]

        @block.sync
        def _(sp):
            sp.dma_start(pos_i[:, :], positions.partition_broadcast(P)).then_inc(positions_landed, 16)

        @block.vector
        def _(dve):
            c = Chain(dve, step)
            dve.wait_ge(positions_landed, 16)
            c.then(nc.vector.tensor_copy(a, pos_i[:, :]))
            c.then(nc.vector.tensor_scalar(a, a, inv_freq, None, ALU.mult))
            c.then(nc.vector.tensor_scalar(q, a, float(np.float32(1 / (2 * math.pi))), ROUND, ALU.mult, ALU.add))
            c.then(nc.vector.tensor_scalar(q, q, ROUND, None, ALU.subtract))
            for part in (TWO_PI_1, TWO_PI_2, TWO_PI_3):
                c.then(nc.vector.scalar_tensor_tensor(a, q, -part, a, ALU.mult, ALU.add))
            nc.vector.tensor_scalar(a, a, PI_IN, -PI_IN, ALU.min, ALU.max).then_inc(reduced, 1)
            dve.wait_ge(reduced, 1)
            c.then(nc.vector.scalar_tensor_tensor(q, a, -1.0, a, ALU.mult, ALU.max))
            nc.vector.tensor_scalar(q, q, -1.0, math.pi / 2, ALU.mult, ALU.add).then_inc(cos_arg, 1)

        @block.scalar
        def _(act):
            act.wait_ge(reduced, 1)
            nc.scalar.activation(sin, a, ACT.Sin)
            act.wait_ge(cos_arg, 1)
            nc.scalar.activation(cos, q, ACT.Sin)


def first_block_layer(nc, l, w, h, parts, common, psum, cos, sin, columns):
    ident, mean_d, rot64 = common["ident"], common["mean_d"], common["rot64"]
    w_in = layer(w["w_in"], l).rearrange("(k p) n -> p k n", p=P)
    b_in = layer(w["b_in"], l)

    vectors, at = [], {}
    row = 0

    def put(name, view):
        nonlocal row
        at[name] = row
        vectors.append((view, row, 0))
        row += view.shape[0]

    def seg(a, n):
        return b_in[a:a + n].rearrange("(c p) -> c p", p=P)

    put("b_q", seg(C_Q, 512))
    for name, start in (("b_k0", C_K), ("b_k1", C_K + 64), ("b_ki", C_KI)):
        at[name] = row
        for half in range(2):
            vectors.append((b_in[start:start + 64].rearrange("(c p) -> c p", p=64), row, 64 * half))
        row += 1
    put("b_qi", seg(C_QI, 512))
    put("b_pool", seg(C_POOL, 256))
    put("b_conv", seg(C_CONV, 512))
    put("b_gate", seg(C_GATE, 3 * D))
    vec = lambda name: layer(w[name], l).rearrange("(c p) -> c p", p=P)
    mat = lambda name: layer(w[name], l).rearrange("k (c p) -> (k c) p", p=P)
    put("pool_scale", vec("pool_scale"))
    put("conv_w", mat("conv_dw_w"))
    for name in ("conv_dw_b", "conv_ln_g", "conv_ln_b", "ln1_g", "ln1_b", "ln2_g", "ln2_b", "ffn_dw_b"):
        put(name, vec(name))
    put("ffn_w", mat("ffn_dw_w"))
    assert row <= columns.shape[1]
    with nc.sbuf_tensor("rows", [P, 3, P], F32) as rows:
        load_columns(nc, rows, columns, psum, ident, vectors)
    col = lambda name, i=0: cols(columns, at[name] + i)

    with ExitStack() as ctx:
        sb = lambda name, shape: ctx.enter_context(nc.sbuf_tensor(name, shape, F32))
        gates = sb("gates", [P, 3 * KD, L])
        queries = sb("queries", [P, 8, L])
        q, qi = queries[:, 0:4, :], queries[:, 4:8, :]
        keys = sb("keys", [P, 3, L])
        kd, ki = keys[:, 0:2, :], keys[:, 2, :]
        v = sb("v", [P, QB, P])
        wi = sb("w_idx", [P, QB, 8])
        pool_in = sb("pool_in", [P, 2, L])
        conv = sb("conv", [P, 2, L])

        with ExitStack() as inner:
            sbi = lambda name, shape: inner.enter_context(nc.sbuf_tensor(name, shape, F32))
            ring = Ring(nc, inner, "z", 2, KD * 256)
            conv_g = sbi("conv_g", [P, 2, L])
            padded = sbi("conv_padded", [P, 2, L + TAPS - 1])
            rope_t = sbi("rope_t", [P, 2, L])
            sums = sbi("sums", [P, 2, L])
            vrow = sbi("bias_rows", [1, P + 8])
            ones = sbi("ones", [1, P])

            with stage(nc, "bias_landed") as (block, sems):
                @block.sync
                def _(sp):
                    sp.dma_start(vrow[:, 0:P], b_in[C_V:C_V + P].rearrange("(o p) -> o p", o=1)).then_inc(sems[0], 16)
                    sp.dma_start(vrow[:, P:P + 8], b_in[C_WI:C_WI + 8].rearrange("(o p) -> o p", o=1)).then_inc(sems[0], 16)
                    sp.wait_ge(sems[0], 32)

                @block.vector
                def _(dve):
                    nc.vector.memset(ones[:, :], 1.0)
                    nc.vector.memset(padded[:, :, 0:TAPS - 1], 0.0)

            def shares(*parts_):
                out, at_ = [], 0
                for start, n, twice in parts_:
                    view = w_in[:, :, start:start + n]
                    if twice:
                        out += [(block_of(at_, KD, P, 64 * half, 64), view) for half in range(2)]
                    else:
                        out.append((block_of(at_, KD, n), view))
                    at_ += KD * (2 * n if twice else n)
                return out

            groups, what = [], []
            moving = lambda k: (parts[0][:, k, :], parts[1][:, k, :])
            loads = []

            def plain(start, kinds):
                loads.append(shares((start, 256, False)))
                for c, kind in enumerate(kinds):
                    groups.append((len(loads) - 1, dense(nc, c * P, KD, moving), "act"))
                    what.append(kind)

            def twice(at_, kind):
                groups.append((len(loads) - 1, dense(nc, at_, KD, moving, step=P), "act"))
                what.append((kind, 0))

            def by_token(at_, n, bias_at, kind):
                made = []
                for b in range(QB):
                    for k in range(KD + 1):
                        def issue(raw, hi, lo, region, k=k, b=b):
                            out = region[:, b * n:(b + 1) * n]
                            if k == KD:
                                return nc.tensor.matmul(out, ones[:, :], vrow[:, bias_at:bias_at + n], start=False, stop=True)
                            return nc.tensor.matmul(out, h[:, k, b * P:(b + 1) * P], raw[:, at_ + k * n:at_ + (k + 1) * n],
                                                    start=k == 0, stop=False)
                        made.append(issue)
                groups.append((len(loads) - 1, made, "act"))
                what.append((kind, 0))

            plain(C_Q, [("q", 0), ("q", 1)])
            plain(C_Q + 256, [("q", 2), ("q", 3)])
            loads.append(shares((C_K, 64, True), (C_K + 64, 64, True)))
            twice(0, "k0")
            twice(KD * P, "k1")
            loads.append(shares((C_KI, 64, True), (C_WI, 8, False)))
            twice(0, "ki")
            by_token(KD * P, 8, P, "wi")
            wi_tile = len(loads) - 1
            plain(C_QI, [("qi", 0), ("qi", 1)])
            plain(C_QI + 256, [("qi", 2), ("qi", 3)])
            loads.append(shares((C_V, 128, False)))
            by_token(0, P, 0, "v")
            v_tile = len(loads) - 1
            plain(C_CONV, [("conv_a", 0), ("conv_a", 1)])
            plain(C_CONV + 256, [("conv_g", 0), ("conv_g", 1)])
            plain(C_POOL, [("pool", 0), ("pool", 1)])
            late = sum(GATES_WHILE_PICKING) + sum(len(x) for x in GATES_AFTER_HEAD)
            early = 3 * KD - late
            for i in range(early // 2):
                plain(C_GATE + 256 * i, [("gate", 2 * i), ("gate", 2 * i + 1)])
            home = {"q": lambda i: q[:, i, :], "k0": lambda i: kd[:, 0, :], "k1": lambda i: kd[:, 1, :],
                    "ki": lambda i: ki, "qi": lambda i: qi[:, i, :]}
            bias_of = {"q": "b_q", "k0": "b_k0", "k1": "b_k1", "ki": "b_ki", "qi": "b_qi"}
            roped = [(g, home[kind](i)) for g, (kind, i) in enumerate(what) if kind in home]
            rope_at = {g: n for n, (g, _) in enumerate(roped)}
            done_at = {w_: g for g, w_ in enumerate(what)}

            def evacuate(g, region):
                kind, i = what[g]
                if kind in home:
                    return nc.scalar.activation(home[kind](i), region, ACT.Identity, bias=col(bias_of[kind], i))
                if kind == "v":
                    return nc.scalar.activation(v[:, :, :], region.rearrange("p (b n) -> p b n", b=QB), ACT.Identity)
                if kind == "wi":
                    return nc.scalar.activation(wi[:, :, :], region[:, 0:QB * 8].rearrange("p (b n) -> p b n", b=QB), ACT.Identity)
                if kind == "conv_a":
                    return nc.scalar.activation(conv[:, i, :], region, ACT.Identity, bias=col("b_conv", i))
                if kind == "conv_g":
                    return nc.scalar.activation(conv_g[:, i, :], region, ACT.Sigmoid, bias=col("b_conv", 2 + i))
                if kind == "pool":
                    return nc.scalar.activation(pool_in[:, i, :], region, ACT.Identity, bias=col("b_pool", i))
                return nc.scalar.activation(gates[:, i, :], region, ACT.Sigmoid, bias=col("b_gate", i))

            rotated = [psum[:, 6 * 512:7 * 512], psum[:, 7 * 512:8 * 512]]

            def also_pe(pe, g, s):
                turned, roped_out, _ = s.more
                if g - 1 in rope_at:
                    n = rope_at[g - 1]
                    pe.wait_ge(s.by_act, s.evacuated(g - 1, "act"))
                    if n >= 2:
                        pe.wait_ge(roped_out, n - 1)
                    nc.tensor.matmul(rotated[n % 2], rot64, roped[n][1], start=True, stop=True).then_inc(turned, 1)

            def also_dve(dve, s):
                turned, roped_out, step = s.more
                chain = Chain(dve, step)
                for n, (g, x) in enumerate(roped):
                    dve.wait_ge(turned, n + 1)
                    chain.then(nc.vector.tensor_tensor(rope_t[:, n % 2, :], rotated[n % 2], sin, ALU.mult))
                    chain.then(nc.vector.tensor_tensor(x, x, cos, ALU.mult))
                    nc.vector.tensor_tensor(x, x, rope_t[:, n % 2, :], ALU.add).then_inc(roped_out, 1)
                for i in range(2):
                    dve.wait_ge(s.by_act, s.evacuated(done_at[("conv_g", i)], "act"))
                    chain.then(nc.vector.tensor_tensor(padded[:, i, TAPS - 1:], conv[:, i, :], conv_g[:, i, :], ALU.mult))
                    chain.then(nc.vector.tensor_scalar(conv[:, i, :], padded[:, i, TAPS - 1:], col("conv_w", 2 * (TAPS - 1) + i),
                                                       col("conv_dw_b", i), ALU.mult, ALU.add))
                    for k in range(TAPS - 1):
                        chain.then(nc.vector.scalar_tensor_tensor(conv[:, i, :], padded[:, i, k:k + L], col("conv_w", 2 * k + i),
                                                                  conv[:, i, :], ALU.mult, ALU.add))
                for i in range(2):
                    dve.wait_ge(s.by_act, s.evacuated(done_at[("pool", i)], "act"))
                    a, b = sums[:, 0, :], sums[:, 1, :]
                    for half in range(2):
                        ps = slice(64 * half, 64 * half + 64)
                        src, shift, which = pool_in[ps, i, :], 1, 0
                        win = POOL_WINDOWS[2 * i + half]
                        while shift < win:
                            dst = sums[ps, which, :]
                            chain.then(nc.vector.tensor_tensor(dst[:, shift:], src[:, shift:], src[:, 0:L - shift], ALU.add))
                            chain.then(nc.vector.tensor_copy(dst[:, 0:shift], src[:, 0:shift]))
                            src, which, shift = dst, 1 - which, 2 * shift
                        cut = common["pool_cut"][ps, i * POOL_TAIL:(i + 1) * POOL_TAIL]
                        x = pool_in[ps, i, :]
                        other = sums[ps, which, 0:POOL_TAIL]
                        chain.then(nc.vector.tensor_tensor(other, src[:, 0:POOL_TAIL], cut, ALU.mult))
                        chain.then(nc.vector.scalar_tensor_tensor(x[:, POOL_TAIL:], src[:, POOL_TAIL:], 1.0 / win,
                                                                  x[:, POOL_TAIL:], ALU.mult, ALU.subtract))
                        chain.then(nc.vector.tensor_tensor(x[:, 0:POOL_TAIL], other, x[:, 0:POOL_TAIL], ALU.subtract))

            product_stage(nc, ring, loads, groups, psum, [(512 * b, 512) for b in range(6)], evacuate,
                          also_pe, also_dve, None, "turned roped step", raw_tiles=(v_tile,), both=(wi_tile,))


        o = sb("o", [P, 4, L])
        with ExitStack() as inner:
            ring = Ring(nc, inner, "gate", 1, KD * P)
            loads = [[(block_of(0, KD, P), w_in[:, :, C_GATE + P * i:C_GATE + P * (i + 1)])] for i in range(early, 3 * KD)]
            groups = [(i, dense(nc, 0, KD, moving_of(parts), step=P), "act") for i in range(late)]
            attention(nc, q, kd, qi, ki, v, wi, o, psum, common, ring, loads, groups,
                      lambda g, region: nc.scalar.activation(gates[:, early + g, :], region, ACT.Identity, bias=col("b_gate", early + g)))

        with ExitStack() as inner:
            sbi = lambda name, shape: inner.enter_context(nc.sbuf_tensor(name, shape, F32))
            ring = Ring(nc, inner, "merge", 2, KD * 256)
            pool_y = sbi("pool_y", [P, 2, L])
            sq = queries[:, :, :]
            stats = sbi("stats", [P, L])
            merged = queries
            y3 = keys
            pool_w = sbi("pool_w", [P, 2, 64])

            pw = layer(w["pool_w"], l)
            with stage(nc, "pool_w_landed mixed") as (block, sems):
                landed, mixed = sems

                @block.sync
                def _(sp):
                    for half in range(2):
                        sp.dma_start(pool_w[64 * half:64 * half + 64, :, :],
                                     pw.rearrange("(c h) i j -> h i c j", c=2)[half]).then_inc(landed, 16)

                @block.tensor
                def _(pe):
                    pe.wait_ge(landed, 32)
                    for c in range(2):
                        for half in range(2):
                            ps = slice(64 * half, 64 * half + 64)
                            last = nc.tensor.matmul(psum[ps, c * 512:(c + 1) * 512], pool_w[ps, c, :], pool_in[ps, c, :],
                                                    start=True, stop=True)
                    last.then_inc(mixed, 1)

                @block.scalar
                def _(act):
                    for i in range(early, 3 * KD):
                        nc.scalar.activation(gates[:, i, :], gates[:, i, :], ACT.Sigmoid)

                @block.vector
                def _(dve):
                    dve.wait_ge(mixed, 1)
                    for c in range(2):
                        nc.vector.tensor_scalar(pool_y[:, c, :], psum[:, c * 512:(c + 1) * 512], col("pool_scale", c), None, ALU.mult)

            layer_norm(nc, conv[:, :, :], sq[:, 0:2, :], stats[:, :], psum, common["mean_conv"],
                       columns[:, at["conv_ln_g"]:at["conv_ln_g"] + 2], columns[:, at["conv_ln_b"]:at["conv_ln_b"] + 2],
                       1e-5, silu=True)

            outs = [layer(w[n], l).rearrange("(k p) n -> p k n", p=P) for n in ("w_pool_out", "w_conv_out", "w_attn_out")]
            split_chunks(nc, [pool_y[:, 0, :], pool_y[:, 1, :], conv[:, 0, :], conv[:, 1, :]] + [o[:, i, :] for i in range(4)], parts)
            loads = [[(block_of(KD * 256 * at_ // 8, n, 256), outs[j][:, :, 256 * i:256 * i + 256])
                      for j, (at_, n) in enumerate(((0, 2), (2, 2), (4, 4)))] for i in range(4)]
            groups = []
            for m in range(KD):
                for at_, n in ((0, 2), (2, 2), (4, 4)):
                    groups.append((m // 2, dense(nc, at_ * 256 + (m % 2) * P, n,
                                                 lambda k, at_=at_: (parts[0][:, at_ + k, :], parts[1][:, at_ + k, :])), "dve"))

            def merge(dve, s):
                (step,) = s.more
                chain = Chain(dve, step)
                for m in range(KD):
                    for j in range(3):
                        g = 3 * m + j
                        dve.wait_ge(s.ready, g + 1)
                        nc.vector.tensor_tensor(y3[:, j, :], s.region(g), gates[:, j * KD + m, :], ALU.mult).then_inc(s.by_dve, 1)
                    dve.wait_ge(s.by_dve, 3 * m + 3)
                    chain.then(nc.vector.tensor_tensor(y3[:, 0, :], y3[:, 0, :], y3[:, 1, :], ALU.add))
                    chain.then(nc.vector.tensor_tensor(merged[:, m, :], y3[:, 0, :], y3[:, 2, :], ALU.add))

            product_stage(nc, ring, loads, groups, psum, [(512 * b, 512) for b in range(8)], None, None, merge, None, "step")
            split_chunks(nc, [merged[:, i, :] for i in range(KD)], parts)

            wo = layer(w["w_o"], l).rearrange("(k p) n -> p k n", p=P)
            loads = [[(block_of(0, KD, 256), wo[:, :, 256 * i:256 * i + 256])] for i in range(4)]
            groups = [(m // 2, dense(nc, (m % 2) * P, KD, moving_of(parts)), "dve") for m in range(KD)]
            product_stage(nc, ring, loads, groups, psum, [(512 * b, 512) for b in range(8)],
                          lambda g, region: nc.vector.scalar_tensor_tensor(h[:, g, :], h[:, g, :], ALPHA, region, ALU.mult, ALU.add))
            layer_norm(nc, h, gates[:, 0:KD, :], stats[:, :], psum, mean_d, columns[:, at["ln1_g"]:at["ln1_g"] + KD],
                       columns[:, at["ln1_b"]:at["ln1_b"] + KD], 1e-5, parts=parts)

    with ExitStack() as inner:
        hidden = [inner.enter_context(nc.sbuf_tensor(n, [P, KF, L], F32R)) for n in ("hidden_hi", "hidden_lo")]
        wu = layer(w["w_up"], l).rearrange("(k p) n -> p k n", p=P)
        loads = [[(block_of(0, KD, P), wu[:, :, P * i:P * i + P]),
                  (block_of(KD * P, KD, P), wu[:, :, D_FF + P * i:D_FF + P * i + P])] for i in range(KF)]
        groups = [(i, dense(nc, part * KD * P, KD, moving_of(parts), step=P), "act") for i in range(KF) for part in range(2)]
        with ExitStack() as up:
            ring = Ring(nc, up, "up", 2, KD * 256)
            u = up.enter_context(nc.sbuf_tensor("u", [P, 2, L + 2], F32))
            cv = up.enter_context(nc.sbuf_tensor("cv", [P, 4, L], F32))
            with stage(nc, "unused") as (block, sems):
                @block.vector
                def _(dve):
                    nc.vector.memset(u[:, :, 0:2], 0.0)
            ffn_up(nc, ring, loads, groups, psum, u, cv, hidden, col)
        wd = layer(w["w_down"], l).rearrange("(k p) n -> p k n", p=P)
        loads = [[(block_of(0, KF, P), wd[:, :, P * m:P * m + P])] for m in range(KD)]
        groups = [(m, dense(nc, 0, KF, moving_of(hidden), step=P), "dve") for m in range(KD)]
        ring = Ring(nc, inner, "down", 2, KF * P, lent=[x.rearrange("p k n -> p (k n)") for x in parts])
        product_stage(nc, ring, loads, groups, psum, [(512 * b, 512) for b in range(8)],
                      lambda g, region: nc.vector.scalar_tensor_tensor(h[:, g, :], h[:, g, :], ALPHA, region, ALU.mult, ALU.add))
    with ExitStack() as inner:
        sq = inner.enter_context(nc.sbuf_tensor("sq2", [P, KD, L], F32))[:, :, :]
        stats = inner.enter_context(nc.sbuf_tensor("stats2", [P, L], F32))
        layer_norm(nc, h, sq, stats[:, :], psum, mean_d, columns[:, at["ln2_g"]:at["ln2_g"] + KD],
                   columns[:, at["ln2_b"]:at["ln2_b"] + KD], 1e-5, parts=parts)


EPS2 = 1e-6
SPLIT = ((0, CTX), (CTX, T2))
LEVELS = (2, 4, 8, 16, 32)


def wide(psum, i):
    return psum[:, i * 1024 + 1024 - T2:(i + 1) * 1024]


def modulation(nc, ctx, psum, ident, columns, at, mod, silu_c, w):
    ring = Ring(nc, ctx, "ada", 4, KD * 512, split=0)
    tiles, per_tile = 6 * DEPTH, 512 // P
    made_rows = ctx.enter_context(nc.sbuf_tensor("mod_rows", [2, 2, 512], F32))
    loads, groups = [], []

    def row_product(k):
        return lambda raw, hi, lo, region: nc.tensor.matmul(region[0:2, :], silu_c[:, k, :], raw[:, 512 * k:512 * k + 512],
                                                            start=k == 0, stop=k == KD - 1)
    for i in range(tiles):
        aw = w["ada_w_2"][i // 6].rearrange("(k p) n -> p k n", p=P)
        at_ = 512 * (i % 6)
        loads.append([(block_of(0, KD, 512), aw[:, :, at_:at_ + 512])])
        groups.append((i, [row_product(k) for k in range(KD)], "act"))
    turned_at = lambda i, c: (4 + i % 2) * 512 + 2 * c

    def evacuate(g, region):
        return nc.scalar.activation(made_rows[:, g % 2, :], region[0:2, :], ACT.Identity)

    def turn(pe, i, s):
        turned, taken = s.more
        pe.wait_ge(s.by_act, i + 1)
        if i >= 2:
            pe.wait_ge(taken, i - 1)
        for c in range(per_tile):
            x = turned_at(i, c)
            last = nc.tensor.transpose(psum[:, x:x + 2], made_rows[:, i % 2, c * P:(c + 1) * P], ident[0:2, 0:2])
        last.then_inc(turned, 1)

    def also_pe(pe, g, s):
        if g:
            turn(pe, g - 1, s)
        if g == tiles - 1:
            turn(pe, g, s)

    def also_act(act, g, s):
        if g:
            act.wait_ge(s.more[0], g)

    def also_dve(dve, s):
        turned, taken = s.more
        for i in range(tiles):
            dve.wait_ge(turned, i + 1)
            x = turned_at(i, 0)
            bias = columns[:, at["ada_b"] + per_tile * i:at["ada_b"] + per_tile * (i + 1)].unsqueeze(2).to_broadcast([P, per_tile, 2])
            first = per_tile * (i % 6)
            nc.vector.tensor_tensor(mod[:, i // 6, first:first + per_tile, :],
                                    psum[:, x:x + 2 * per_tile].rearrange("p (c n) -> p c n", n=2), bias, ALU.add).then_inc(taken, 1)

    product_stage(nc, ring, loads, groups, psum, [(512 * b, 512) for b in range(4)], evacuate,
                  also_pe, also_dve, also_act, "turned taken", raw_tiles=range(tiles))


def rms_norm(nc, pieces, sq, stats, psum, mean_d):
    with stage(nc, "squared sum_ready safe root scaled rstd_ready") as (block, sems):
        squared, sum_ready, safe, root, scaled, rstd_ready = sems
        n = len(pieces)
        spans, done = [], 1024 - sum(x[0].shape[2] for x in pieces)
        for piece in pieces:
            spans.append((done, done + piece[0].shape[2]))
            done += piece[0].shape[2]
        lo, hi = spans[0][0], 1024

        @block.scalar
        def _(act):
            for (x, y, gain, bias, add_to), (a, b) in zip(pieces, spans):
                for c in range(KD):
                    nc.scalar.activation(sq[:, c, a - lo:b - lo], x[:, c, :], ACT.Square).then_inc(squared, 1)
            act.wait_ge(safe, 1)
            nc.scalar.activation(stats[:, 0:hi - lo], stats[:, 0:hi - lo], ACT.Sqrt).then_inc(root, 1)
            i = 0
            for (x, y, gain, bias, add_to), (a, b) in zip(pieces, spans):
                for c in range(KD):
                    i += 1
                    if add_to is None:
                        act.wait_ge(scaled, i)
                        nc.scalar.activation(y[:, c, :], y[:, c, :], ACT.Identity, bias=bias[:, c:c + 1],
                                             scale=gain[:, c:c + 1])

        @block.tensor
        def _(pe):
            for i, (a, b) in enumerate(spans):
                for c in range(KD):
                    pe.wait_ge(squared, i * KD + c + 1)
                    last = nc.tensor.matmul(psum[:, a:b], mean_d, sq[:, c, a - lo:b - lo], start=c == 0, stop=c == KD - 1)
            last.then_inc(sum_ready, 1)

        @block.vector
        def _(dve):
            dve.wait_ge(sum_ready, 1)
            nc.vector.tensor_scalar(stats[:, 0:hi - lo], psum[:, lo:hi], EPS2, None, ALU.add).then_inc(safe, 1)
            dve.wait_ge(root, 1)
            nc.vector.reciprocal(stats[:, 0:hi - lo], stats[:, 0:hi - lo]).then_inc(rstd_ready, 1)
            dve.wait_ge(rstd_ready, 1)
            i = 0
            for (x, y, gain, bias, add_to), (a, b) in zip(pieces, spans):
                for c in range(KD):
                    i += 1
                    nc.vector.tensor_tensor(y[:, c, :], x[:, c, :], stats[:, a - lo:b - lo], ALU.mult).then_inc(scaled, 1)
                    if add_to is not None:
                        dve.wait_ge(scaled, i)
                        nc.vector.scalar_tensor_tensor(add_to[:, c, :], y[:, c, :], gain[:, c:c + 1], add_to[:, c, :],
                                                       ALU.mult, ALU.add)


def serial(nc, steps):
    with stage(nc, "step_done") as (block, sems):
        (step_done,) = sems

        def run(engine, name):
            for i, (who, issue) in enumerate(steps):
                if who == name:
                    if i:
                        engine.wait_ge(step_done, i)
                    issue().then_inc(step_done, 1)

        @block.vector
        def _(dve):
            run(dve, "dve")

        @block.scalar
        def _(act):
            run(act, "act")

        @block.tensor
        def _(pe):
            run(pe, "pe")


def even_layer(nc, w, h, xc, common, psum, columns, at, mod, coef):
    ident = common["ident"]
    col = lambda name, i=0: cols(columns, at[name] + i)
    spill = lambda name, chunks, tokens=T2: nc.dram_tensor(name + "_spill", [P, chunks, tokens], F32, kind="Internal").ap()
    gates_dram, u_dram, o_dram, xc_dram = spill("gates", 8), spill("mixed", 20), spill("recurrence", RW_PAIRS), spill("context", KD, CTX)
    with ExitStack() as ctx:
        sb = lambda name, shape: ctx.enter_context(nc.sbuf_tensor("second_" + name, shape, F32))
        u = sb("mixed_in", [P, 20, T2])
        with ExitStack() as inner:
            sbi = lambda name, shape: inner.enter_context(nc.sbuf_tensor("second_" + name, shape, F32))
            gated = sbi("gated", [P, 10, T2])
            with ExitStack() as inner2:
                parts = [inner2.enter_context(nc.sbuf_tensor(n, [P, KD, T2], F32R)) for n in ("hn_hi", "hn_lo")]
                with nc.sbuf_tensor("stats_e", [P, T2], F32) as stats:
                    norm_in(nc, h, xc, u[:, 0:KD, :], gated[:, 0:KD, :], stats, psum, common, coef, 0)
                split_chunks(nc, [u[:, i, :] for i in range(KD)], parts)
                ring = Ring(nc, inner2, "even", 3, KD * P)
                raw = inner2.enter_context(nc.sbuf_tensor("raw", [P, 2, T2], F32))
                mus = inner2.enter_context(nc.sbuf_tensor("mus", [P, 7, 20], F32))
                mu = columns[:, at["mu"]:at["mu"] + 20]
                serial(nc, [("dve", lambda j=j: nc.vector.tensor_scalar(mus[:, j, :], mu, cols(common["lane"], j), None, ALU.mult))
                            for j in range(6)]
                       + [("dve", lambda: nc.vector.tensor_scalar(mus[:, 6, :], mu, -1.0, 1.0, ALU.mult, ALU.add))])
                ew = w["ev_w_in_2"][0].rearrange("(k p) n -> p k n", p=P)
                loads = [[(block_of(0, KD, P), ew[:, :, P * m:P * m + P])] for m in range(30)]
                groups = [(m, over_tokens(nc, 0, parts, SPLIT, step=P), "act") for m in range(30)]

                def evacuate(g, region):
                    if g < 20:
                        return nc.scalar.activation(raw[:, g % 2, :], region, ACT.Identity)
                    func = ACT.Identity if 26 <= g < 28 else ACT.Silu
                    return nc.scalar.activation(gated[:, g - 20, :], region, func)

                names = Products.names(ring) + "step shifted stored"
                with stage(nc, names) as (block, sems):
                    s = Products(nc, sems, ring, loads, groups, psum, [(1024 * r + 1024 - T2, T2) for r in range(4)])
                    step_, shifted, stored = s.more

                    @block.sync
                    def _(sp):
                        s.load(sp)

                    @block.gpsimd
                    def _(pool):
                        s.split_lo(pool)

                    @block.tensor
                    def _(pe):
                        for g in range(len(groups)):
                            s.multiply(pe, g)

                    @block.scalar
                    def _(act):
                        for g in range(len(groups)):
                            s.split_before(act, g)
                            act.wait_ge(s.ready, g + 1)
                            if 2 <= g < 22:
                                act.wait_ge(shifted, g - 1)
                                act.dma_start(u_dram[:, g - 2, :], u[:, g - 2, :]).then_inc(stored, 16)
                            evacuate(g, s.region(g)).then_inc(s.by_act, 1)
                        act.wait_ge(stored, 16 * 20)

                    @block.vector
                    def _(dve):
                        chain = Chain(dve, step_)
                        s.split_first(dve)
                        for g in range(20):
                            dve.wait_ge(s.by_act, g + 1)
                            x, y = raw[:, g % 2, :], u[:, g, :]
                            xg = x[:, CTX:].rearrange("p (r c) -> p r c", c=GRID_W)
                            yg = y[:, CTX:].rearrange("p (r c) -> p r c", c=GRID_W)
                            chain.then(nc.vector.tensor_scalar(y, x, mus[:, 6, g:g + 1], None, ALU.mult))
                            pairs = [(y[:, 1:CTX], x[:, 0:CTX - 1], 4), (y[:, 0:CTX - 1], x[:, 1:CTX], 5),
                                     (yg[:, :, 1:], xg[:, :, :-1], 0), (yg[:, :, :-1], xg[:, :, 1:], 1),
                                     (yg[:, 1:, :], xg[:, :-1, :], 2), (yg[:, :-1, :], xg[:, 1:, :], 3)]
                            for i, (dst, src, j) in enumerate(pairs):
                                made = nc.vector.scalar_tensor_tensor(dst, src, mus[:, j, g:g + 1], dst, ALU.mult, ALU.add)
                                if i < 5:
                                    chain.then(made)
                                else:
                                    made.then_inc(shifted, 1)
            fourier(nc, gated, psum, w)
            with stage(nc, "spilled") as (block, sems):
                @block.sync
                def _(sp):
                    sp.dma_start(gates_dram, gated[:, 0:8, :]).then_inc(sems[0], 16)
                    sp.dma_start(xc_dram, xc).then_inc(sems[0], 16)
                    sp.wait_ge(sems[0], 32)
    rwkv(nc, w, u_dram, o_dram, xc, common, psum, col, at, columns)
    even_finish(nc, w, o_dram, h, xc, xc_dram, gates_dram, psum, common, col, columns, at, coef)


def norm_in(nc, h, xc, hn, sq, stats, psum, common, coef, l):
    rms_norm(nc, [(xc, hn[:, :, 0:CTX], coef[:, l, 0, 1, :], coef[:, l, 1, 1, :], None),
                  (h, hn[:, :, CTX:T2], coef[:, l, 0, 0, :], coef[:, l, 1, 0, :], None)],
             sq, stats, psum, common["mean_d"])


def fourier(nc, gated, psum, w):
    with ExitStack() as ctx:
        sb = lambda name, shape: ctx.enter_context(nc.sbuf_tensor("second_" + name, shape, F32))
        ch = sb("dft_channels", [P, 2 * P])
        seq = sb("dft_seq", [P, 2, 4, L])
        cx = sb("dft_ctx", [P, 2, 2, CTX])
        z = sb("z", [P, 2, 6, 2 * P])
        with stage(nc, "tables_landed by_channel taken by_token") as (block, sems):
            tables_landed, by_channel, taken, by_token = sems

            @block.sync
            def _(sp):
                a, n = CONST_AT["dft_ch"]
                sp.dma_start(ch[:, :], w["consts"][:, a:a + n]).then_inc(tables_landed, 16)
                sp.dma_start(seq[:, :, :, :], w["dft_seq"].rearrange("s (c p) f -> p s c f", p=P)).then_inc(tables_landed, 16)
                sp.dma_start(cx[:, :, :, :], w["dft_ctx"].rearrange("s (c p) f -> p s c f", p=P)).then_inc(tables_landed, 16)

            @block.tensor
            def _(pe):
                pe.wait_ge(tables_landed, 48)
                for j in range(2):
                    for t in range(6):
                        i = 6 * j + t
                        if i >= 2:
                            pe.wait_ge(taken, i - 1)
                        nc.tensor.matmul(psum[:, (i % 2) * 512:(i % 2) * 512 + 2 * P], gated[:, 6 + j, t * P:(t + 1) * P], ch[:, :],
                                         start=True, stop=True).then_inc(by_channel, 1)
                pe.wait_ge(taken, 12)
                for j in range(2):
                    out = wide(psum, 1 + j)
                    for table, t0, nt, a, b in ((cx, 0, 2, 0, CTX), (seq, 2, 4, CTX, T2)):
                        for part in range(2):
                            for t in range(nt):
                                last = nc.tensor.matmul(out[:, a:b], z[:, j, t0 + t, part * P:(part + 1) * P], table[:, part, t, :],
                                                        start=part == 0 and t == 0, stop=part == 1 and t == nt - 1)
                    last.then_inc(by_token, 1)

            @block.scalar
            def _(act):
                for i in range(12):
                    act.wait_ge(by_channel, i + 1)
                    nc.scalar.activation(z[:, i // 6, i % 6, :], psum[:, (i % 2) * 512:(i % 2) * 512 + 2 * P], ACT.Identity).then_inc(taken, 1)

            @block.vector
            def _(dve):
                for j in range(2):
                    dve.wait_ge(by_token, j + 1)
                    nc.vector.tensor_tensor(gated[:, 6 + j, :], wide(psum, 1 + j), gated[:, 8 + j, :], ALU.mult)


class Recurrence:

    NAMES = "x_ready x_taken u_ready u_taken s_ready decayed state_ready o_added "

    def __init__(self, nc, sems, i, first, last, buf, psum):
        self.nc, self.i, self.d, self.first, self.steps = nc, i, i % 2, first, last - first
        (self.x_ready, self.x_taken, self.u_ready, self.u_taken, self.s_ready, self.decayed, self.state_ready,
         self.o_added) = sems
        self.buf = buf
        region = lambda b, n: psum[:, b * 512 + n * P:b * 512 + (n + 1) * P]
        self.x, self.u, self.s, self.y = region(6, 0), region(6, 1), region(6, 2), region(7, 0)
        self.order = chunk_order(self.d)
        self.fresh = 1 if first == 0 and self.steps else 0
        self.items = 3 * self.steps

    def at(self, item):
        k, part = divmod(item, 3)
        j = self.first + k
        return k, part, self.order[j], slot_of(self.i, j)

    def wait_state(self, engine, k):
        if k + self.fresh:
            engine.wait_ge(self.state_ready, k + self.fresh)

    def pe(self, pe, item):
        k, part, n, slot = self.at(item)
        b, mm = self.buf, self.nc.tensor.matmul
        v_tok, a_bd, r_bd = b.v_tok[:, self.i // 2 % 2, n, :], b.a_bd[:, self.i % 2, n, :], b.r_bd[:, self.i % 2, n, :]
        if part == 0:
            self.wait_state(pe, k)
            mm(self.x, b.nt[:, slot, :], v_tok, start=True, stop=False)
            mm(self.x, a_bd, b.st[:, :], start=False, stop=True).then_inc(self.x_ready, 1)
        elif part == 1:
            if k:
                pe.wait_ge(self.o_added, 2 * k)
            mm(self.y, b.st[:, :], r_bd, start=True, stop=False)
            mm(self.y, v_tok, b.rk[:, slot, :], start=False, stop=False)
            pe.wait_ge(self.x_taken, k + 1)
            mm(self.u, b.wt[:, slot, :], b.xs[:, :], start=True, stop=True).then_inc(self.u_ready, 1)
        else:
            pe.wait_ge(self.u_taken, k + 1)
            mm(self.y, b.us[:, :], b.rb[:, slot, :], start=False, stop=True)
            mm(self.s, b.k_tok[:, slot, :], v_tok, start=True, stop=False)
            mm(self.s, b.b_tok[:, slot, :], b.us[:, :], start=False, stop=True).then_inc(self.s_ready, 1)

    def act(self, act, item):
        k, part, n, slot = self.at(item)
        b = self.buf
        if part == 0:
            self.wait_state(act, k)
            self.nc.scalar.activation(b.sts[:, :], b.st[:, :], ACT.Identity, scale=b.decay[:, self.i % 2, n:n + 1]).then_inc(self.decayed, 1)
            act.wait_ge(self.x_ready, k + 1)
            self.nc.scalar.activation(b.xs[:, :], self.x, ACT.Identity).then_inc(self.x_taken, 1)

    def dve(self, dve, item):
        k, part, n, slot = self.at(item)
        b, V = self.buf, self.nc.vector
        if part == 0 and k == 0 and self.fresh:
            V.memset(b.st[:, :], 0.0).then_inc(self.state_ready, 1)
        elif part == 1:
            dve.wait_ge(self.u_ready, k + 1)
            V.tensor_copy(b.us[:, :], self.u).then_inc(self.u_taken, 1)
        elif part == 2:
            dve.wait_ge(self.s_ready, k + 1)
            dve.wait_ge(self.decayed, k + 1)
            V.scalar_tensor_tensor(b.st[:, :], self.s, b.decay[:, self.i % 2, n:n + 1], b.sts[:, :], ALU.mult, ALU.add)\
                .then_inc(self.state_ready, 1)
            for hf in range(2):
                o = b.o[64 * hf:64 * hf + 64, self.i // 2 % 2, n * CH:(n + 1) * CH]
                V.tensor_tensor(o, o, self.y[64 * hf:64 * hf + 64, 64 * hf:64 * hf + 64], ALU.add).then_inc(self.o_added, 1)

    def due(self, place, places):
        return range(self.items * place // places, self.items * (place + 1) // places)


class Operands:

    def __init__(self, sb):
        self.nt, self.wt, self.rb, self.rk = sb("nt", SLOTS, P), sb("wt", SLOTS, P), sb("rb", SLOTS, P), sb("rk", SLOTS, P)
        self.b_tok, self.k_tok = sb("b_tok", SLOTS, P), sb("k_tok", SLOTS, P)
        self.a_bd, self.r_bd, self.v_tok = sb("a_bd", 2, NCH, P), sb("r_bd", 2, NCH, P), sb("v_tok", 2, NCH, P)
        self.st, self.sts, self.xs, self.us = sb("st", P), sb("sts", P), sb("xs", P), sb("us", P)
        self.o, self.decay = sb("o", 2, T2), sb("decay", 2, NCH)


SLOTS = 20
EARLY = 4


def slot_of(i, j):
    return (NCH * i + j) % SLOTS


def chunk_order(d):
    n = CTX // CH
    return list(range(NCH)) if d == 0 else list(range(n - 1, -1, -1)) + list(range(NCH - 1, n - 1, -1))


def rwkv(nc, w, u_dram, o_dram, xc, common, psum, col, at, columns):
    passes = 2 * RW_PAIRS
    with ExitStack() as ctx:
        sb = lambda name, *shape: ctx.enter_context(nc.sbuf_tensor("second_" + name, [P, *shape], F32))
        m0, m1 = CONST_AT["upper"][0], CONST_AT["dft_ch"][0]
        masks = sb("masks", m1 - m0)
        mask = lambda name: masks[:, CONST_AT[name][0] - m0:sum(CONST_AT[name]) - m0]
        w2, lora = sb("w2", 2, RWKV_W), sb("lora", 2, T2)
        rkv = sb("rkv", 3, T2)
        reset, sg, cum, a, kk, e1, e2, e3, tmp = (sb(n, T2) for n in "reset sg cum a kk e1 e2 e3 tmp".split())
        k = sg
        buf = Operands(sb)
        b_bd, k_bd = sb("b_bd", NCH, P), sb("k_bd", NCH, P)
        room = xc.rearrange("p k t -> p (k t)")
        mt = room[:, 0:NCH * P].rearrange("p (n t) -> p n t", n=NCH)
        mm = room[:, NCH * P:(NCH + 4) * P].rearrange("p (n t) -> p n t", n=4)
        v_bd, y, wf = mt, b_bd, k_bd
        omka = sb("omka", RW_PAIRS)
        ident = common["ident"]
        V, S, PE, G = nc.vector, nc.scalar, nc.tensor, nc.gpsimd
        by_chunk = lambda x: x.rearrange("p (n t) -> p n t", t=CH)
        r, k0, v = rkv[:, 0, :], rkv[:, 1, :], rkv[:, 2, :]
        triple = lambda p: u_dram[:, 0:18, :].rearrange("p (s c) t -> p s c t", s=3)[:, :, p, :]

        with stage(nc, "landed tanh_ready reset_ones") as (block, sems):
            landed, tanh_ready, reset_ones = sems

            @block.sync
            def _(sp):
                sp.dma_start(lora[:, :, :], u_dram[:, 18:20, :]).then_inc(landed, 16)
                sp.dma_start(masks[:, :], w["consts"][:, m0:m1]).then_inc(landed, 16)
                sp.dma_start(w2[:, 0, :], w["ev_w2_2"][0].rearrange("d k n -> (d k) n")).then_inc(landed, 16)
                sp.dma_start(w2[:, 1, :], w["ev_a2_2"][0].rearrange("d k n -> (d k) n")).then_inc(landed, 16)
                sp.dma_start(rkv[:, :, :], triple(0)).then_inc(landed, 16)
                sp.wait_ge(landed, 16 * 5)

            @block.vector
            def _(dve):
                V.memset(reset[:, :], 1.0).then_inc(reset_ones, 1)
                for x in (b_bd, k_bd, v_bd):
                    V.memset(x[:, :, :], 0.0)
                V.tensor_scalar(omka[:, :], columns[:, at["k_a"]:at["k_a"] + RW_PAIRS], -1.0, 1.0, ALU.mult, ALU.add)
                dve.wait_ge(reset_ones, 1)
                V.memset(by_chunk(reset[:, :])[:, :, 0:1], 0.0)

            @block.gpsimd
            def _(pool):
                for x in (buf.a_bd, buf.r_bd):
                    G.memset(x[:, :, :, :], 0.0)

            @block.scalar
            def _(act):
                act.wait_ge(landed, 16 * 5)
                S.activation(lora[:, 0, :], lora[:, 0, :], ACT.Tanh)

        def project(region, lhsT, rhs):
            for lo_, hi_ in SPLIT:
                last = PE.matmul(region[:, lo_:hi_], lhsT, rhs[:, lo_:hi_], start=True, stop=True)
            return last

        def halves(bd, issue):
            for hf in range(2):
                ps = slice(64 * hf, 64 * hf + 64)
                last = issue(bd[ps, :, 64 * hf:64 * hf + 64], ps)
            return last

        class Terms:

            NAMES = ("w_projected a_projected sg_ready a_ready kk_ready squared norm_ready clamped root_ready sums_ready "
                     "exps_ready k_ready bonus_in bonus_ready step rkv_landed ")
            PHASES = 10

            def __init__(self, sems, i):
                (self.w_projected, self.a_projected, self.sg_ready, self.a_ready, self.kk_ready, self.squared,
                 self.norm_ready, self.clamped, self.root_ready, self.sums_ready, self.exps_ready, self.k_ready,
                 self.bonus_in, self.bonus_ready, self.step, self.rkv_landed) = sems
                self.p, self.d = divmod(i, 2)
                self.phases = self.PHASES if i < passes else 0
                self.region = wide(psum, 2)
                self.loads = self.d == 0 and 0 < self.p < RW_PAIRS

            def load(self, sp):
                if self.loads:
                    sp.dma_start(rkv[:, :, :], triple(self.p)).then_inc(self.rkv_landed, 16)

            def pe(self, pe, phase):
                p, d = self.p, self.d
                ds_ = slice(64 * d, 64 * d + 64)
                if phase == 0:
                    project(self.region, w2[ds_, 0, p * P:(p + 1) * P], lora[ds_, 0, :]).then_inc(self.w_projected, 1)
                if phase == 1:
                    pe.wait_ge(self.sg_ready, 1)
                    project(self.region, w2[ds_, 1, p * P:(p + 1) * P], lora[ds_, 1, :]).then_inc(self.a_projected, 1)
                if phase == 3 and d == 0:
                    pe.wait_ge(self.a_ready, 1)
                    pe.wait_ge(self.squared, 1)
                    project(self.region, common["head_sum"], tmp[:, :]).then_inc(self.norm_ready, 1)
                if phase == 5:
                    pe.wait_ge(*((self.clamped, 1) if d == 0 else (self.a_ready, 1)))
                    pe.wait_ge(self.bonus_in, 1)
                    project(self.region, common["head_sum"], cum[:, :]).then_inc(self.bonus_ready, 1)

            def act(self, act, phase):
                p, d = self.p, self.d
                if phase == 0:
                    act.wait_ge(self.w_projected, 1)
                    S.activation(sg[:, :], self.region, ACT.Sigmoid, bias=col("w0", 6 * d + p)).then_inc(self.sg_ready, 1)
                if phase == 1:
                    act.wait_ge(self.a_projected, 1)
                    S.activation(a[:, :], self.region, ACT.Sigmoid, bias=col("a0", 6 * d + p)).then_inc(self.a_ready, 1)
                if phase == 2 and d == 0:
                    act.wait_ge(self.kk_ready, 1)
                    S.activation(tmp[:, :], kk[:, :], ACT.Square).then_inc(self.squared, 1)
                if phase == 3:
                    act.wait_ge(self.sums_ready, 2)
                    S.activation(e3[:, :], e1[:, :], ACT.Exp, scale=DECAY).then_inc(self.exps_ready, 1)
                    act.wait_ge(self.exps_ready, 1)
                    S.activation(e1[:, :], e1[:, :], ACT.Exp, scale=-DECAY)
                    S.activation(e2[:, :], e2[:, :], ACT.Exp, scale=-DECAY)
                if phase == 5 and d == 0:
                    act.wait_ge(self.clamped, 1)
                    S.activation(tmp[:, :], tmp[:, :], ACT.Sqrt).then_inc(self.root_ready, 1)

            def dve(self, dve, phase, chain):
                p, d = self.p, self.d
                o = buf.o[:, p % 2, :]
                if phase == 1:
                    if self.loads:
                        dve.wait_ge(self.rkv_landed, 16)
                    if d == 0:
                        V.tensor_scalar(kk[:, :], k0, col("k_k", p), None, ALU.mult).then_inc(self.kk_ready, 1)
                    dve.wait_ge(self.sg_ready, 1)
                    chain.then(V.tensor_tensor_scan(cum[:, :], reset[:, :], sg[:, :], 0.0, ALU.mult, ALU.add))
                if phase == 2:
                    if d == 0:
                        V.tensor_copy(e1[:, :], cum[:, :]).then_inc(self.sums_ready, 1)
                        V.tensor_tensor(e2[:, :], cum[:, :], sg[:, :], ALU.subtract).then_inc(self.sums_ready, 1)
                    else:
                        total = by_chunk(cum[:, :])[:, :, CH - 1:CH].to_broadcast([P, NCH, CH])
                        V.tensor_tensor(by_chunk(e2[:, :]), total, by_chunk(cum[:, :]), ALU.subtract).then_inc(self.sums_ready, 1)
                        dve.wait_ge(self.sums_ready, 1)
                        V.tensor_tensor(e1[:, :], e2[:, :], sg[:, :], ALU.add).then_inc(self.sums_ready, 1)
                if phase == 3:
                    dve.wait_ge(self.sums_ready, 2)
                    dve.wait_ge(self.a_ready, 1)
                    chain.then(V.tensor_scalar(k[:, :], a[:, :], col("k_a", p), omka[:, p:p + 1], ALU.mult, ALU.add))
                    V.tensor_tensor(k[:, :], k[:, :], k0, ALU.mult).then_inc(self.k_ready, 1)
                    dve.wait_ge(self.k_ready, 1)
                    V.scalar_tensor_tensor(cum[:, :], r, col("r_k", p), k[:, :], ALU.mult, ALU.mult).then_inc(self.bonus_in, 1)
                if phase == 4 and d == 0:
                    dve.wait_ge(self.norm_ready, 1)
                    V.tensor_scalar(tmp[:, :], self.region, 1e-24, None, ALU.max).then_inc(self.clamped, 1)
                if phase == 6:
                    dve.wait_ge(self.bonus_ready, 1)
                    if d == 0:
                        V.tensor_tensor(o, self.region, v, ALU.mult)
                    else:
                        chain.then(V.tensor_tensor(tmp[:, :], self.region, v, ALU.mult))
                        V.tensor_tensor(o, o, tmp[:, :], ALU.add)
                if d == 0 and 6 <= phase < 9:
                    dve.wait_ge(self.root_ready, 1)
                    third = tmp[:, (phase - 6) * CTX:(phase - 5) * CTX]
                    chain.then(V.reciprocal(third, third))
                if phase == 9:
                    if d == 0:
                        chain.then(V.tensor_tensor(kk[:, :], kk[:, :], tmp[:, :], ALU.mult))
                    V.tensor_tensor(a[:, :], kk[:, :], a[:, :], ALU.mult)

            def due(self, place, places):
                return range(self.phases * place // places, self.phases * (place + 1) // places)

        def first_terms():
            with stage(nc, Terms.NAMES) as (block, sems):
                terms = Terms(sems, 0)

                @block.tensor
                def _(pe):
                    for phase in range(terms.phases):
                        terms.pe(pe, phase)

                @block.scalar
                def _(act):
                    for phase in range(terms.phases):
                        terms.act(act, phase)

                @block.vector
                def _(dve):
                    chain = Chain(dve, terms.step)
                    for phase in range(terms.phases):
                        terms.dve(dve, phase, chain)

        def blocks(i, rec_of):
            p, d = divmod(i, 2)
            a_bd, r_bd = buf.a_bd[:, d, :, :], buf.r_bd[:, d, :, :]
            with stage(nc, "stored " + Recurrence.NAMES) as (block, sems):
                stored, rec = sems[0], rec_of(sems[1:])
                PLACES = 4

                @block.tensor
                def _(pe):
                    for item in range(rec.items):
                        rec.pe(pe, item)

                @block.scalar
                def _(act):
                    for place in range(PLACES):
                        for item in rec.due(place, PLACES):
                            rec.act(act, item)
                        if place == 0 and d == 0:
                            halves(v_bd, lambda dst, ps: S.activation(dst, by_chunk(v[ps, :]), ACT.Identity))

                @block.vector
                def _(dve):
                    for place in range(PLACES):
                        for item in rec.due(place, PLACES):
                            rec.dve(dve, item)
                        if place == 0:
                            halves(a_bd, lambda dst, ps: V.scalar_tensor_tensor(dst, by_chunk(kk[ps, :]), -1.0, by_chunk(e2[ps, :]), ALU.mult, ALU.mult))
                        if place == 1:
                            halves(b_bd, lambda dst, ps: V.tensor_tensor(dst, by_chunk(a[ps, :]), by_chunk(e3[ps, :]), ALU.mult))
                        if place == 2:
                            whole = CH - 1 if d == 0 else 0
                            V.tensor_copy(buf.decay[:, d, :].unsqueeze(2), by_chunk(e1[:, :])[:, :, whole:whole + 1])

                @block.gpsimd
                def _(pool):
                    halves(r_bd, lambda dst, ps: G.tensor_tensor(dst, by_chunk(r[ps, :]), by_chunk(e1[ps, :]), ALU.mult))
                    halves(k_bd, lambda dst, ps: G.tensor_tensor(dst, by_chunk(k[ps, :]), by_chunk(e3[ps, :]), ALU.mult))

                if d == 1 and p:
                    @block.sync
                    def _(sp):
                        sp.dma_start(o_dram[:, p - 1, :], buf.o[:, (p - 1) % 2, :]).then_inc(stored, 16)
                        sp.wait_ge(stored, 16)

        def products(i, rec_of):
            p, d = divmod(i, 2)
            a_bd, r_bd, order = buf.a_bd[:, d, :, :], buf.r_bd[:, d, :, :], chunk_order(d)
            up, up_eq = ("upper", "upper_eq") if d == 0 else ("lower", "lower_eq")
            pre_t, pre_f = ("up", "lo") if d == 0 else ("lo", "up")
            over = lambda name: mask(name).unsqueeze(1).to_broadcast([P, 4, P])
            eye4 = ident.unsqueeze(1).to_broadcast([P, 4, P])
            bank = lambda b: psum[:, b * 512:(b + 1) * 512].rearrange("p (i n) -> p i n", n=P)
            kinds = ([("v_tok", v_bd, None)] if d == 0 else []) + \
                [("b_tok", b_bd, None), ("k_tok", k_bd, None), ("nt", k_bd, a_bd), ("rk", k_bd, r_bd), ("rb", b_bd, r_bd),
                 ("mt", b_bd, a_bd), ("m", a_bd, b_bd)]
            units = [(g, *kind) for g in range(3) for kind in kinds]
            by = ["act" if moving is None else "dve" for _, _, _, moving in units]
            taken_by = lambda n, who: by[:n + 1].count(who)
            slots = lambda g: slice(slot_of(i, 4 * g), slot_of(i, 4 * g) + 4)
            own = lambda g: slice(min(order[4 * g:4 * g + 4]), min(order[4 * g:4 * g + 4]) + 4)
            rounds = [(level, g) for level in range(len(LEVELS)) for g in range(3)]
            last_level = len(LEVELS) - 1
            PLACES = 6 + len(rounds) + 1
            BANKS = 4
            bank_y, bank_wt, bank_w = lambda n: bank(n % 2), bank(2), bank(3)
            half = (len(units) + 5) // 6
            names = ("unit_ready taken_act taken_dve wt_scaled wt_begun wf_begun masked y_ready y_taken ww_ready wt_ready "
                     "w_added wt_added ")
            with stage(nc, names + Terms.NAMES + Recurrence.NAMES) as (block, sems):
                (unit_ready, taken_act, taken_dve, wt_scaled, wt_begun, wf_begun, masked, y_ready, y_taken, ww_ready,
                 wt_ready, w_added, wt_added) = sems[:13]
                terms, rec = Terms(sems[13:29], i + 1), rec_of(sems[29:])

                @block.sync
                def _(sp):
                    terms.load(sp)

                @block.tensor
                def _(pe):
                    for n, (g, what, left, right) in enumerate(units):
                        if n >= BANKS:
                            pe.wait_ge(taken_act if by[n - BANKS] == "act" else taken_dve, taken_by(n - BANKS, by[n - BANKS]))
                        for c in range(4):
                            chunk = order[4 * g + c]
                            if right is None:
                                last = PE.transpose(bank(n % BANKS)[:, c, :], left[:, chunk if what != "v_tok" else 4 * g + c, :], ident)
                            else:
                                last = PE.matmul(bank(n % BANKS)[:, c, :], left[:, chunk, :], right[:, chunk, :], start=True, stop=True)
                        last.then_inc(unit_ready, 1)
                        if (n + 1) % half == 0 or n + 1 == len(units):
                            for phase in terms.due(n // half, PLACES):
                                terms.pe(pe, phase)
                            for item in rec.due(n // half, PLACES):
                                rec.pe(pe, item)
                    pe.wait_ge(taken_act, by.count("act"))
                    pe.wait_ge(taken_dve, by.count("dve"))
                    for n in range(len(rounds) + 1):
                        if n < len(rounds):
                            level, g = rounds[n]
                            pe.wait_ge(masked, n + 1)
                            if level == 0:
                                pe.wait_ge(wf_begun, g + 1)
                                pe.wait_ge(wt_begun, g + 1)
                            else:
                                pe.wait_ge(w_added, n - 2)
                                pe.wait_ge(wt_added, n - 2)
                            if n >= 2:
                                pe.wait_ge(y_taken, n - 1)
                            for c in range(4):
                                last = PE.matmul(bank_y(n)[:, c, :], mm[:, c, :], wf[:, own(g).start + c, :], start=True, stop=True)
                            last.then_inc(y_ready, 1)
                        if n:
                            level, g = rounds[n - 1]
                            s0 = slots(g).start
                            pe.wait_ge(y_taken, n)
                            if n > 1:
                                pe.wait_ge(wt_added, n - 1)
                            for c in range(4):
                                last = PE.matmul(bank_wt[:, c, :], y[:, own(g).start + c, :], buf.wt[:, s0 + c, :], start=True, stop=True)
                            last.then_inc(wt_ready, 1)
                            if level < last_level:
                                if n > 1:
                                    pe.wait_ge(w_added, n - 1)
                                for c in range(4):
                                    last = PE.matmul(bank_w[:, c, :], buf.wt[:, s0 + c, :], y[:, own(g).start + c, :], start=True, stop=True)
                                last.then_inc(ww_ready, 1)
                        for phase in terms.due(6 + n, PLACES):
                            terms.pe(pe, phase)
                        for item in rec.due(6 + n, PLACES):
                            rec.pe(pe, item)

                @block.scalar
                def _(act):
                    for n, (g, what, left, right) in enumerate(units):
                        if right is None:
                            act.wait_ge(unit_ready, n + 1)
                            if what == "v_tok":
                                dst = buf.v_tok[:, p % 2, 4 * g:4 * g + 4, :]
                            else:
                                dst = (buf.b_tok if what == "b_tok" else buf.k_tok)[:, slots(g), :]
                            S.activation(dst, bank(n % BANKS), ACT.Identity).then_inc(taken_act, 1)
                        if (n + 1) % half == 0 or n + 1 == len(units):
                            for phase in terms.due(n // half, PLACES):
                                terms.act(act, phase)
                            for item in rec.due(n // half, PLACES):
                                rec.act(act, item)
                    for n in range(len(rounds) + 1):
                        if n < len(rounds):
                            level, g = rounds[n]
                            act.wait_ge(y_ready, n + 1)
                            S.activation(y[:, own(g), :], bank_y(n), ACT.Identity).then_inc(y_taken, 1)
                        for phase in terms.due(6 + n, PLACES):
                            terms.act(act, phase)
                        for item in rec.due(6 + n, PLACES):
                            rec.act(act, item)

                @block.vector
                def _(dve):
                    chain = Chain(dve, terms.step)
                    for n, (g, what, left, right) in enumerate(units):
                        if right is not None:
                            dve.wait_ge(unit_ready, n + 1)
                            if what == "mt":
                                made = V.tensor_tensor(mt[:, own(g), :], bank(n % BANKS), over(up), ALU.mult)
                            elif what == "m":
                                made = V.tensor_tensor(wf[:, own(g), :], bank(n % BANKS), over(pre_f + "1"), ALU.mult)
                            elif what == "nt":
                                made = V.tensor_tensor(buf.nt[:, slots(g), :], bank(n % BANKS), over(up), ALU.mult)
                            else:
                                made = V.tensor_tensor((buf.rk if what == "rk" else buf.rb)[:, slots(g), :], bank(n % BANKS), over(up_eq), ALU.mult)
                            made.then_inc(taken_dve, 1)
                            if what == "m":
                                dve.wait_ge(taken_dve, taken_by(n, "dve"))
                                V.tensor_tensor(wf[:, own(g), :], wf[:, own(g), :], eye4, ALU.add).then_inc(wf_begun, 1)
                        if (n + 1) % half == 0 or n + 1 == len(units):
                            for phase in terms.due(n // half, PLACES):
                                terms.dve(dve, phase, chain)
                            for item in rec.due(n // half, PLACES):
                                rec.dve(dve, item)
                    for n in range(len(rounds) + 1):
                        if n:
                            level, g = rounds[n - 1]
                            dve.wait_ge(wt_ready, n)
                            if level < last_level:
                                dve.wait_ge(ww_ready, n)
                            V.tensor_tensor(buf.wt[:, slots(g), :], buf.wt[:, slots(g), :], bank_wt, ALU.add).then_inc(wt_added, 1)
                            if level < last_level:
                                V.tensor_tensor(wf[:, own(g), :], wf[:, own(g), :], bank_w, ALU.add).then_inc(w_added, 1)
                        for phase in terms.due(6 + n, PLACES):
                            terms.dve(dve, phase, chain)
                        for item in rec.due(6 + n, PLACES):
                            rec.dve(dve, item)

                @block.gpsimd
                def _(pool):
                    def off_diagonal(n):
                        level, g = rounds[n]
                        if n:
                            pool.wait_ge(y_ready, n)
                        G.tensor_tensor(mm[:, :, :], mt[:, own(g), :], over(f"{pre_t}{LEVELS[level]}"), ALU.mult).then_inc(masked, 1)

                    for g in range(3):
                        pool.wait_ge(taken_dve, taken_by(len(kinds) * (g + 1) - 2, "dve"))
                        G.tensor_tensor(buf.wt[:, slots(g), :], mt[:, own(g), :], over(pre_t + "1"), ALU.mult).then_inc(wt_scaled, 1)
                        pool.wait_ge(wt_scaled, g + 1)
                        G.tensor_tensor(buf.wt[:, slots(g), :], buf.wt[:, slots(g), :], eye4, ALU.add).then_inc(wt_begun, 1)
                        if g == 1:
                            off_diagonal(0)
                    for n in range(1, len(rounds)):
                        off_diagonal(n)

        def steps_of(i, first, last):
            if i < 0:
                first = last = 0
            return lambda sems: Recurrence(nc, sems, i, first, last, buf, psum)

        first_terms()
        for i in range(passes):
            blocks(i, steps_of(i - 1, 0, EARLY))
            products(i, steps_of(i - 1, EARLY, NCH))
        with stage(nc, "stored " + Recurrence.NAMES) as (block, sems):
            rec = steps_of(passes - 1, 0, NCH)(sems[1:])

            @block.tensor
            def _(pe):
                for item in range(rec.items):
                    rec.pe(pe, item)

            @block.scalar
            def _(act):
                for item in range(rec.items):
                    rec.act(act, item)

            @block.vector
            def _(dve):
                for item in range(rec.items):
                    rec.dve(dve, item)

            @block.sync
            def _(sp):
                sp.wait_ge(rec.o_added, 2 * NCH)
                sp.dma_start(o_dram[:, RW_PAIRS - 1, :], buf.o[:, (RW_PAIRS - 1) % 2, :]).then_inc(sems[0], 16)
                sp.wait_ge(sems[0], 16)


def even_finish(nc, w, o_dram, h, xc, xc_dram, gates_dram, psum, common, col, columns, at, coef):
    with ExitStack() as ctx:
        sb = lambda name, shape: ctx.enter_context(nc.sbuf_tensor("second_" + name, shape, F32))
        gated = sb("gated2", [P, 8, T2])
        u = sb("recurrence", [P, RW_PAIRS, T2])
        sq = sb("sq3", [P, 8, T2])
        stats = sb("stats3", [P, T2])
        rows = sb("head_rows", [RW_HEADS, RW_PAIRS * P])
        dev = sb("deviations", [RW_HEADS, T2])
        names = "o_landed gates_landed rows_landed mean_ready centered squared var_ready safe root inverted spread taken step"
        with stage(nc, names) as (block, sems):
            (o_landed, gates_landed, rows_landed, mean_ready, centered, squared, var_ready, safe, root, inverted,
             spread, taken, step) = sems
            var = wide(psum, 2)[0:RW_HEADS, :]

            @block.sync
            def _(sp):
                for c in range(RW_PAIRS):
                    sp.dma_start(u[:, c, :], o_dram[:, c, :]).then_inc(o_landed, 16)
                sp.dma_start(rows[:, :], w["head_rows"][:, 0:RW_PAIRS * P]).then_inc(rows_landed, 16)
                sp.dma_start(gated[:, :, :], gates_dram).then_inc(gates_landed, 16)
                sp.dma_start(xc, xc_dram).then_inc(gates_landed, 16)

            @block.tensor
            def _(pe):
                pe.wait_ge(o_landed, 16 * RW_PAIRS)
                for c in range(RW_PAIRS):
                    if c >= 2:
                        pe.wait_ge(centered, c - 1)
                    for a, b in SPLIT:
                        last = nc.tensor.matmul(wide(psum, c % 2)[:, a:b], common["head_mean"], u[:, c, a:b], start=True, stop=True)
                    last.then_inc(mean_ready, 1)
                for c in range(RW_PAIRS):
                    pe.wait_ge(squared, c + 1)
                    pick = common["pick_pair"][:, RW_HEADS - 2 - 2 * c:2 * RW_HEADS - 2 - 2 * c]
                    for a, b in SPLIT:
                        last = nc.tensor.matmul(var[:, a:b], pick, sq[:, c, a:b], start=c == 0, stop=c == RW_PAIRS - 1)
                last.then_inc(var_ready, 1)
                pe.wait_ge(rows_landed, 16)
                pe.wait_ge(inverted, 1)
                for c in range(RW_PAIRS):
                    if c >= 2:
                        pe.wait_ge(taken, c - 1)
                    for a, b in SPLIT:
                        last = nc.tensor.matmul(wide(psum, c % 2)[:, a:b], rows[:, c * P:(c + 1) * P], dev[:, a:b], start=True, stop=True)
                    last.then_inc(spread, 1)

            @block.scalar
            def _(act):
                for c in range(RW_PAIRS):
                    act.wait_ge(centered, c + 1)
                    nc.scalar.activation(sq[:, c, :], u[:, c, :], ACT.Square).then_inc(squared, 1)
                act.wait_ge(safe, 1)
                nc.scalar.activation(dev[:, :], dev[:, :], ACT.Sqrt).then_inc(root, 1)

            @block.vector
            def _(dve):
                chain = Chain(dve, step)
                for c in range(RW_PAIRS):
                    dve.wait_ge(mean_ready, c + 1)
                    nc.vector.tensor_tensor(u[:, c, :], u[:, c, :], wide(psum, c % 2), ALU.subtract).then_inc(centered, 1)
                dve.wait_ge(var_ready, 1)
                nc.vector.tensor_scalar(dev[:, :], var, 64e-5, None, ALU.add).then_inc(safe, 1)
                dve.wait_ge(root, 1)
                nc.vector.reciprocal(dev[:, :], dev[:, :]).then_inc(inverted, 1)
                dve.wait_ge(gates_landed, 32)
                for c in range(RW_PAIRS):
                    dve.wait_ge(spread, c + 1)
                    nc.vector.tensor_tensor(u[:, c, :], u[:, c, :], wide(psum, c % 2), ALU.mult).then_inc(taken, 1)
                    dve.wait_ge(taken, c + 1)
                    chain.then(nc.vector.tensor_scalar(u[:, c, :], u[:, c, :], col("lnx_g", c), col("lnx_b", c), ALU.mult, ALU.add))
                    nc.vector.tensor_tensor(gated[:, c, :], u[:, c, :], gated[:, c, :], ALU.mult)
        wo = w["ev_w_out_2"][0].rearrange("(k p) n -> p k n", p=P)
        out_product(nc, wo, gated, gated, psum, SPLIT, P)
        out = gated
        rms_norm(nc, [(out[:, :, 0:CTX], out[:, :, 0:CTX], coef[:, 0, 2, 1, :], None, xc),
                      (out[:, :, CTX:T2], out[:, :, CTX:T2], coef[:, 0, 2, 0, :], None, h)],
                 sq[:, :, :], stats[:, :], psum, common["mean_d"])


def over_tokens(nc, offset, parts, split, step=256):
    made = []
    for a, b in split:
        made += dense(nc, offset, KD, lambda k, a=a, b=b: (parts[0][:, k, a:b], parts[1][:, k, a:b]), step=step, columns=(a, b))
    return made


def out_product(nc, wo, y, out, psum, split, width):
    n, per = split[-1][1], width // P
    loads = [[(block_of(0, KD, width), wo[:, :, width * i:width * (i + 1)])] for i in range(D // width)]
    with ExitStack() as ctx:
        parts = [ctx.enter_context(nc.sbuf_tensor(f"y{n}_{part}", [P, KD, n], F32R)) for part in ("hi", "lo")]
        split_chunks(nc, [y[:, i, :] for i in range(KD)], parts)
        groups = [(m // per, over_tokens(nc, (m % per) * P, parts, split, step=width), "act") for m in range(KD)]
        ring = Ring(nc, ctx, f"out{n}", 2, KD * width)
        product_stage(nc, ring, loads, groups, psum, [(1024 * r + 1024 - n, n) for r in range(4)],
                      lambda g, region: nc.scalar.activation(out[:, g, :], region, ACT.Identity))


def odd_layer(nc, w, h, xc, common, psum, coef, lg):
    with ExitStack() as ctx:
        sb = lambda name, shape: ctx.enter_context(nc.sbuf_tensor("second_" + name, shape, F32))
        q = sb("q2", [P, RET_HEADS, L])
        k = sb("k2", [P, RET_HEADS, T2])
        v = sb("v2", [P, 6, D])
        g_ = sb("g2", [P, RET_HEADS, L])
        with ExitStack() as inner:
            sbi = lambda name, shape: inner.enter_context(nc.sbuf_tensor("second_" + name, shape, F32))
            parts = [inner.enter_context(nc.sbuf_tensor(n, [P, KD, T2], F32R)) for n in ("hn1_hi", "hn1_lo")]
            with ExitStack() as inner2:
                stats = inner2.enter_context(nc.sbuf_tensor("stats4", [P, T2], F32))
                hn = inner2.enter_context(nc.sbuf_tensor("hn1", [P, KD, T2], F32))
                norm_in(nc, h, xc, hn[:, :, :], k[:, :, :], stats[:, :], psum, common, coef, 1)
                split_chunks(nc, [hn[:, i, :] for i in range(KD)], parts)
            room = xc.rearrange("p k t -> p (k t)").rearrange("p (a b t) -> p a b t", a=2, b=2)
            axial, rope_t = room[:, 0, :, :], room[:, 1, :, :]
            ring = Ring(nc, inner, "odd", 1, KD * 256)
            with stage(nc, "axial_landed") as (block, sems):
                @block.sync
                def _(sp):
                    a = CONST_AT["axial_cos"][0]
                    sp.dma_start(axial, w["consts"][:, a:a + 2 * L].rearrange("p (s t) -> p s t", s=2)).then_inc(sems[0], 16)
                    sp.wait_ge(sems[0], 16)
            ow = w["od_w_in_2"][0].rearrange("(k p) n -> p k n", p=P)
            loads = [[(block_of(0, KD, 256), ow[:, :, 256 * i:256 * i + 256])] for i in range(16)]
            groups, what = [], []

            def by_token(t):
                def product(kc, i, which, part):
                    return lambda raw, hi, lo, region: nc.tensor.matmul(
                        region[:, 512:768], parts[part][:, kc, t * P:(t + 1) * P],
                        (hi, lo)[which][:, kc * 256:(kc + 1) * 256], start=kc == 0 and i == 0, stop=kc == KD - 1 and i == 2)
                return [product(kc, i, which, part) for kc in range(KD)
                        for i, (which, part) in enumerate(((0, 0), (0, 1), (1, 0)))]

            for i in range(16):
                kind = "qkvg"[i // 4]
                if kind == "v":
                    for t in range(6):
                        groups.append((i, by_token(t), "act"))
                        what.append(("v", t, i - 8))
                    continue
                for m in range(2):
                    groups.append((i, over_tokens(nc, m * P, parts, SPLIT if kind == "k" else SPLIT[1:]), "act"))
                    what.append((kind, 2 * (i % 4) + m, 0))

            def evacuate(g, region):
                kind, i, j = what[g]
                if kind == "v":
                    return nc.scalar.activation(v[:, i, 256 * j:256 * j + 256], region[:, 512:768], ACT.Identity)
                if kind == "q":
                    return nc.scalar.activation(q[:, i, :], region[:, CTX:], ACT.Identity)
                if kind == "k":
                    return nc.scalar.activation(k[:, i, :], region, ACT.Identity, scale=float(P) ** -0.5)
                return nc.scalar.activation(g_[:, i, :], region[:, CTX:], ACT.Silu)

            roped = [(g, q[:, i, :] if kind == "q" else k[:, i, CTX:]) for g, (kind, i, _) in enumerate(what) if kind in "qk"]
            rope_at = {g: n for n, (g, _) in enumerate(roped)}
            rotated = [psum[:, 6 * 512:7 * 512], psum[:, 7 * 512:8 * 512]]

            def also_pe(pe, g, s):
                turned, roped_out, _ = s.more
                if g - 1 in rope_at:
                    n = rope_at[g - 1]
                    pe.wait_ge(s.by_act, s.evacuated(g - 1, "act"))
                    if n >= 2:
                        pe.wait_ge(roped_out, n - 1)
                    nc.tensor.matmul(rotated[n % 2], common["rot128"], roped[n][1], start=True, stop=True).then_inc(turned, 1)

            def also_dve(dve, s):
                turned, roped_out, step = s.more
                chain = Chain(dve, step)
                for n, (g, x) in enumerate(roped):
                    dve.wait_ge(turned, n + 1)
                    chain.then(nc.vector.tensor_tensor(rope_t[:, n % 2, :], rotated[n % 2], axial[:, 1, :], ALU.mult))
                    chain.then(nc.vector.tensor_tensor(x, x, axial[:, 0, :], ALU.mult))
                    nc.vector.tensor_tensor(x, x, rope_t[:, n % 2, :], ALU.add).then_inc(roped_out, 1)

            product_stage(nc, ring, loads, groups, psum, [(1024 * r + 1024 - T2, T2) for r in range(3)], evacuate,
                          also_pe, also_dve, None, "turned roped step")

        with ExitStack() as inner:
            sbi = lambda name, shape: inner.enter_context(nc.sbuf_tensor("second_" + name, shape, F32))
            dist = sbi("dist", [P, 24 * P])
            near = sbi("near", [P, 2, 7 * P])
            far = sbi("far", [P, 2, 5 * P])
            far_b = sbi("far_b", [P, 5 * P])
            weighed = sbi("weighed", [P, 2, 6, L])
            y = g_
            sq = sbi("sq4", [P, RET_HEADS, L])
            rows = sbi("head_rows2", [RET_HEADS, RET_HEADS * P])
            dev = sbi("deviations2", [RET_HEADS, L])
            names = ("dist_landed exponent near_ready far_ready far_b_ready decay_ready scores_ready weighted_ready "
                     "o_ready squared mean_ready safe root inverted spread taken step y_ready rows_landed")
            with stage(nc, names) as (block, sems):
                (dist_landed, exponent, near_ready, far_ready, far_b_ready, decay_ready, scores_ready, weighted_ready,
                 o_ready, squared, mean_ready, safe, root, inverted, spread, taken, step, y_ready, rows_landed) = sems
                fwd, bwd = dist[:, 0:7 * P], dist[:, 7 * P:14 * P]
                cf, cb = dist[:, 14 * P:19 * P], dist[:, 19 * P:24 * P]
                scores = lambda n: psum[:, (n % 4) * 512:(n % 4) * 512 + L]
                result = lambda hd: psum[:, (4 + hd % 2) * 512:(5 + hd % 2) * 512]
                mean = psum[0:RET_HEADS, 6 * 512:7 * 512]

                @block.sync
                def _(sp):
                    sp.dma_start(dist[:, :], w["retention"]).then_inc(dist_landed, 16)
                    sp.dma_start(rows[:, :], w["head_rows"][0:RET_HEADS, RW_PAIRS * P:(RW_PAIRS + RET_HEADS) * P]).then_inc(rows_landed, 16)

                @block.tensor
                def _(pe):
                    def score(hd, c):
                        n = hd * 6 + c
                        if n >= 4:
                            pe.wait_ge(weighted_ready, n - 3)
                        nc.tensor.matmul(scores(n), k[:, hd, c * P:(c + 1) * P], q[:, hd, :], start=True, stop=True).then_inc(scores_ready, 1)

                    def mean_square(hd):
                        pe.wait_ge(squared, hd + 1)
                        pick = common["pick_head"][:, RET_HEADS - 1 - hd:2 * RET_HEADS - 1 - hd]
                        return nc.tensor.matmul(mean, pick, sq[:, hd, :], start=hd == 0, stop=hd == RET_HEADS - 1)

                    for c in range(6):
                        score(0, c)
                    for hd in range(RET_HEADS):
                        for c in range(6):
                            if hd + 1 < RET_HEADS:
                                score(hd + 1, c)
                            if c == 0 and hd >= 2:
                                pe.wait_ge(y_ready, hd - 1)
                            if c == 3 and hd:
                                mean_square(hd - 1)
                            pe.wait_ge(weighted_ready, hd * 6 + c + 1)
                            last = nc.tensor.matmul(result(hd), v[:, c, hd * P:(hd + 1) * P], weighed[:, hd % 2, c, :], start=c == 0, stop=c == 5)
                        last.then_inc(o_ready, 1)
                    mean_square(RET_HEADS - 1).then_inc(mean_ready, 1)
                    pe.wait_ge(rows_landed, 16)
                    pe.wait_ge(inverted, 1)
                    for hd in range(RET_HEADS):
                        if hd >= 4:
                            pe.wait_ge(taken, hd - 3)
                        nc.tensor.matmul(scores(hd), rows[:, hd * P:(hd + 1) * P], dev[:, :], start=True, stop=True).then_inc(spread, 1)

                @block.scalar
                def _(act):
                    act.wait_ge(dist_landed, 16)

                    def decays(hd):
                        if hd >= RET_HEADS:
                            return
                        act.wait_ge(exponent, hd + 1)
                        nc.scalar.activation(near[:, hd % 2, :], near[:, hd % 2, :], ACT.Exp).then_inc(near_ready, 1)
                        if hd >= 2:
                            act.wait_ge(weighted_ready, 6 * (hd - 1))
                        if hd >= 1:
                            act.wait_ge(decay_ready, hd)
                        nc.scalar.activation(far[:, hd % 2, :], cf, ACT.Exp, scale=lg[:, hd:hd + 1]).then_inc(far_ready, 1)
                        nc.scalar.activation(far_b[:, :], cb, ACT.Exp, scale=lg[:, 8 + hd:9 + hd]).then_inc(far_b_ready, 1)

                    decays(0)
                    decays(1)
                    for hd in range(RET_HEADS):
                        decays(hd + 2)
                        act.wait_ge(o_ready, hd + 1)
                        nc.scalar.activation(sq[:, hd, :], result(hd), ACT.Square).then_inc(squared, 1)
                    act.wait_ge(safe, 1)
                    nc.scalar.activation(dev[:, :], dev[:, :], ACT.Sqrt).then_inc(root, 1)

                @block.vector
                def _(dve):
                    chain = Chain(dve, step)
                    dve.wait_ge(dist_landed, 16)

                    def exponents(hd):
                        if hd >= RET_HEADS:
                            return
                        if hd >= 2:
                            dve.wait_ge(weighted_ready, 6 * (hd - 1))
                        chain.then(nc.vector.tensor_scalar(near[:, hd % 2, :], fwd, lg[:, hd:hd + 1], None, ALU.mult))
                        nc.vector.scalar_tensor_tensor(near[:, hd % 2, :], bwd, lg[:, 8 + hd:9 + hd], near[:, hd % 2, :], ALU.mult, ALU.add)\
                            .then_inc(exponent, 1)

                    def far_sum(hd):
                        if hd >= RET_HEADS:
                            return
                        dve.wait_ge(far_b_ready, hd + 1)
                        nc.vector.tensor_tensor(far[:, hd % 2, :], far[:, hd % 2, :], far_b[:, :], ALU.add).then_inc(decay_ready, 1)

                    def weigh(hd):
                        dve.wait_ge(decay_ready, hd + 1)
                        if hd >= 2:
                            dve.wait_ge(o_ready, hd - 1)
                        for c in range(6):
                            n = hd * 6 + c
                            dve.wait_ge(scores_ready, n + 1)
                            if c < 2:
                                factor = far[:, hd % 2, P * (1 - c):P * (1 - c) + L]
                            else:
                                factor = near[:, hd % 2, P * (5 - c):P * (5 - c) + L]
                            nc.vector.tensor_tensor(weighed[:, hd % 2, c, :], scores(n), factor, ALU.mult).then_inc(weighted_ready, 1)

                    def gate(hd):
                        dve.wait_ge(squared, hd + 1)
                        nc.vector.tensor_tensor(y[:, hd, :], result(hd), g_[:, hd, :], ALU.mult).then_inc(y_ready, 1)

                    exponents(0)
                    exponents(1)
                    far_sum(0)
                    weigh(0)
                    far_sum(1)
                    for hd in range(RET_HEADS):
                        exponents(hd + 2)
                        if hd + 1 < RET_HEADS:
                            weigh(hd + 1)
                        if hd:
                            gate(hd - 1)
                        far_sum(hd + 2)
                    gate(RET_HEADS - 1)
                    dve.wait_ge(mean_ready, 1)
                    nc.vector.tensor_scalar(dev[:, :], mean, EPS2, None, ALU.add).then_inc(safe, 1)
                    dve.wait_ge(root, 1)
                    nc.vector.reciprocal(dev[:, :], dev[:, :]).then_inc(inverted, 1)
                    dve.wait_ge(y_ready, RET_HEADS)
                    for hd in range(RET_HEADS):
                        dve.wait_ge(spread, hd + 1)
                        nc.vector.tensor_tensor(y[:, hd, :], y[:, hd, :], scores(hd), ALU.mult).then_inc(taken, 1)
        out_product(nc, w["od_w_out_2"][0].rearrange("(k p) n -> p k n", p=P), g_, g_, psum, ((0, L),), 256)
        with nc.sbuf_tensor("stats_o", [P, L], F32) as stats:
            rms_norm(nc, [(g_[:, :, :], g_[:, :, :], coef[:, 1, 2, 0, :], None, h)], q[:, :, :], stats[:, :], psum, common["mean_d"])


def second_block(nc, w, out, h, common, psum, columns):
    with ExitStack() as ctx:
        sb = lambda name, shape: ctx.enter_context(nc.sbuf_tensor("second_" + name, shape, F32))
        xc = sb("xc", [P, KD, CTX])[:, :, :]
        coef = sb("coef", [P, DEPTH, 3, 2, KD])
        mod = sb("mod", [P, DEPTH, 24, 2])
        silu_c = sb("silu_c", [P, KD, 2])
        lg = sb("log_gamma", [P, 16])
        lt = sb("log_tmp", [P, 2, 16])
        vectors, at = [], {}
        row = 0
        for name, src in (("c", w["c_2"][0]), ("c_ctx", w["c_ctx_2"]), ("mu", w["ev_mu_2"][0]), ("k_k", w["ev_k_k_2"][0]),
                          ("k_a", w["ev_k_a_2"][0]), ("r_k", w["ev_r_k_2"][0].rearrange("h d -> (h d)")),
                          ("lnx_g", w["ev_lnx_g_2"][0]), ("lnx_b", w["ev_lnx_b_2"][0]),
                          ("w0", w["ev_w0_2"][0].rearrange("a d -> (a d)")), ("a0", w["ev_a0_2"][0].rearrange("a d -> (a d)")),
                          ("ada_b", w["ada_b_2"].rearrange("l d -> (l d)")), ("pre", w["norm_pre_2"].rearrange("l d -> (l d)")),
                          ("post", w["norm_post_2"].rearrange("l d -> (l d)"))):
            view = src.rearrange("(c p) -> c p", p=P)
            at[name] = row
            vectors.append((view, row, 0))
            row += view.shape[0]
        with nc.sbuf_tensor("rows_second", [P, 2, P], F32) as rows:
            load_columns(nc, rows, columns, psum, common["ident"], vectors)
        with ExitStack() as inner:
            x_tokens = inner.enter_context(nc.sbuf_tensor("ctx_tokens", [P, 2, D], F32))
            transpose_in(nc, x_tokens, xc, psum, common["ident"], w["ctx_2"].rearrange("o t d -> (o t) d"))
        serial(nc, [("act", lambda i=i, n=n: nc.scalar.activation(silu_c[:, :, i], columns[:, at[n]:at[n] + KD], ACT.Silu))
                    for i, n in enumerate(("c", "c_ctx"))])
        with stage(nc, "logits_landed") as (block, sems):
            @block.sync
            def _(sp):
                sp.dma_start(lg[:, :], w["od_decay_logit_2"].rearrange("o a h -> o (a h)").partition_broadcast(P)).then_inc(sems[0], 16)
                sp.wait_ge(sems[0], 16)
        V, S = nc.vector, nc.scalar
        serial(nc, [("dve", lambda: V.scalar_tensor_tensor(lt[:, 0, :], lg[:, :], -1.0, lg[:, :], ALU.mult, ALU.min)),
                    ("act", lambda: S.activation(lt[:, 0, :], lt[:, 0, :], ACT.Exp)),
                    ("dve", lambda: V.tensor_scalar(lt[:, 0, :], lt[:, 0, :], 1.0, None, ALU.add)),
                    ("act", lambda: S.activation(lt[:, 0, :], lt[:, 0, :], ACT.Ln)),
                    ("dve", lambda: V.tensor_scalar(lt[:, 1, :], lg[:, :], 0.0, None, ALU.min)),
                    ("dve", lambda: V.tensor_tensor(lg[:, :], lt[:, 1, :], lt[:, 0, :], ALU.subtract))])
        with ExitStack() as inner:
            modulation(nc, inner, psum, common["ident"], columns, at, mod, silu_c, w)
        steps = []
        for l in range(DEPTH):
            pre = columns[:, at["pre"] + KD * l:at["pre"] + KD * (l + 1)]
            post = columns[:, at["post"] + KD * l:at["post"] + KD * (l + 1)]
            for who in range(2):
                part = lambda i, l=l, who=who: mod[:, l, KD * i:KD * (i + 1), who]
                steps.append(("dve", lambda l=l, who=who, pre=pre, part=part: V.scalar_tensor_tensor(
                    coef[:, l, 0, who, :], part(1), 1.0, pre, ALU.add, ALU.mult)))
                steps.append(("dve", lambda l=l, who=who, part=part: V.tensor_copy(coef[:, l, 1, who, :], part(0))))
                steps.append(("dve", lambda l=l, who=who, post=post, part=part: V.tensor_tensor(
                    coef[:, l, 2, who, :], part(2), post, ALU.mult)))
        serial(nc, steps)
        even_layer(nc, w, h, xc, common, psum, columns, at, mod, coef)
        odd_layer(nc, w, h, xc, common, psum, coef, lg)
        write_out(nc, h, psum, common["ident"], out)


def write_out(nc, h, psum, ident, out):
    with ExitStack() as ctx:
        y = ctx.enter_context(nc.sbuf_tensor("y_tokens", [P, QB, D], F32))
        with stage(nc, "turned taken stored") as (block, sems):
            turned, taken, stored = sems

            @block.tensor
            def _(pe):
                for b in range(QB):
                    if b >= 4:
                        pe.wait_ge(taken, b - 3)
                    for c in range(KD):
                        last = nc.tensor.transpose(psum[:, b * 1024 + c * P:b * 1024 + (c + 1) * P], h[:, c, b * P:(b + 1) * P], ident)
                    last.then_inc(turned, 1)

            @block.vector
            def _(dve):
                for b in range(QB):
                    dve.wait_ge(turned, b + 1)
                    nc.vector.tensor_copy(y[:, b, :], psum[:, b * 1024:(b + 1) * 1024]).then_inc(taken, 1)

            @block.sync
            def _(sp):
                for b in range(QB):
                    sp.wait_ge(taken, b + 1)
                    sp.dma_start(out[0, b * P:(b + 1) * P, :], y[:, b, :]).then_inc(stored, 16)
                sp.wait_ge(stored, 16 * QB)


COMMON = ("ident", "mean_d", "mean_conv", "rot64", "rot128", "head_sum", "head_mean", "mean_head128",
          "future", "masked", "pool_cut", "inv_freq", "lane", "pick_pair", "pick_head")


def program(nc, w, out):
    with ExitStack() as ctx:
        sb = lambda name, shape, dt=F32: ctx.enter_context(nc.sbuf_tensor(name, shape, dt))
        psum = ctx.enter_context(nc.psum_tensor("psum", [P, 8 * 512], F32))
        n_common = CONST_AT["upper"][0]
        table = sb("table", [P, n_common])
        h = sb("h", [P, KD, L])
        columns = sb("columns", [P, 3 * P])
        common = {n: table[:, CONST_AT[n][0]:sum(CONST_AT[n])] for n in COMMON}
        with stage(nc, "table_landed") as (block, sems):
            @block.sync
            def _(sp):
                sp.dma_start(table[:, :], w["consts"][:, 0:n_common]).then_inc(sems[0], 16)
                sp.wait_ge(sems[0], 16)
        with ExitStack() as inner:
            parts = [inner.enter_context(nc.sbuf_tensor(n, [P, KD, L], F32R))[:, :, :] for n in ("moving_hi", "moving_lo")]
            sbi = lambda name, shape, dt=F32: inner.enter_context(nc.sbuf_tensor(name, shape, dt))
            cos, sin = sbi("cos", [P, L]), sbi("sin", [P, L])
            with ExitStack() as start:
                sbs = lambda name, shape, dt=F32: start.enter_context(nc.sbuf_tensor(name, shape, dt))
                x_tokens = sbs("x_tokens", [P, QB, D])
                transpose_in(nc, x_tokens, h[:, :, :], psum, common["ident"], w["x"].rearrange("o t d -> (o t) d"))
                rope_tables(nc, sbs("pos", [P, L], I32), cos[:, :], sin[:, :], sbs("tmp", [P, 2, L]), w["positions"], common["inv_freq"])
                vec = lambda n: w[n].rearrange("(c p) -> c p", p=P)
                load_columns(nc, sbs("rows_in", [P, 1, P]), columns, psum, common["ident"],
                             [(vec("ln_in_g"), 0, 0), (vec("ln_in_b"), KD, 0)])
                layer_norm(nc, h[:, :, :], sbs("sq0", [P, KD, L])[:, :, :], sbs("stats0", [P, L])[:, :], psum, common["mean_d"],
                           columns[:, 0:KD], columns[:, KD:2 * KD], 1e-5, parts=parts)
            clear_last(nc)
            with nc.Fori(0, DEPTH) as l:
                first_block_layer(nc, l, w, h[:, :, :], parts, common, psum, cos[:, :], sin[:, :], columns)
                clear_last(nc)
        second_block(nc, w, out, h[:, :, :], common, psum, columns)
        clear_last(nc)


def kernel(**inputs):
    import concourse.bacc as bacc
    from concourse.bass_utils import run_bass_kernel_spmd

    nc = bacc.Bacc("TRN2", target_bir_lowering=False, num_devices=1)
    arrays = {name: np.ascontiguousarray(a) for name, a in inputs.items()}
    dft_ctx, dft_seq = dft_tables()
    arrays.update(consts=CONSTS, dft_ctx=dft_ctx, dft_seq=dft_seq, retention=retention_tables(), head_rows=head_rows())
    w = {name: nc.dram_tensor(f"in_{name}", a.shape, mybir.dt.from_np(a.dtype), kind="ExternalInput").ap()
         for name, a in arrays.items()}
    out = nc.dram_tensor("out", (1, L, D), F32, kind="ExternalOutput").ap()
    program(nc, w, out)
    r = run_bass_kernel_spmd(nc, [{f"in_{name}": a for name, a in arrays.items()}], core_ids=[0])
    return np.asarray(r.results[0]["out"])
```
